# Optimizing a Trainium2 kernel written in Bass

```python
import math
import jax, jax.numpy as jnp
from jax import lax
import numpy as np

D_MODEL = 2048
BATCH = 1
SEQ = 128
DEPTH = 2
DEC_BATCH = 1
DEC_SEQ = 128
PAST_LEN = 128

GRID_W = 64
N_MIXERS = 2
N_HEADS = 16
HEAD_DIM = D_MODEL // N_HEADS
NA_ROWS_MAX = 8
NA_COLS = 16
RPB_R = 2 * NA_ROWS_MAX - 1
RPB_C = 2 * NA_COLS - 1
S5_CH = 16
S5_GROUPS = D_MODEL // S5_CH
S5_P = 64
Q_BLOCK = 128
EPS = 1e-6
DT_MIN = 0.001
DT_MAX = 0.1

kernel_name = "hybrid_na_s5_prefix_denoise_step"

def _rmsnorm(x, g):
    xf = x.astype(jnp.float32)
    y = xf * lax.rsqrt(jnp.mean(xf * xf, axis=-1, keepdims=True) + EPS)
    return (y * g.astype(jnp.float32)).astype(x.dtype)

def _pre(x, cond, g, w_ada, b_ada):
    shift, scale, gate = jnp.split(jax.nn.silu(cond) @ w_ada + b_ada, 3, axis=-1)
    h = _rmsnorm(x, g) * (1 + scale) + shift
    return h, gate

def _na_proj(h, w_in):
    b, l, _ = h.shape
    q, k, v, z = jnp.split(h @ w_in, 4, axis=-1)
    shp = (b, l, N_HEADS, HEAD_DIM)
    return q.reshape(shp), k.reshape(shp), v.reshape(shp), z

def _ctx_attention(q, k, v):
    b, l, h, d = q.shape
    nblk = l // Q_BLOCK
    qb = jnp.moveaxis(q.reshape(b, nblk, Q_BLOCK, h, d), 1, 0)
    scale = HEAD_DIM ** -0.5

    def blk(qi):
        s = jnp.einsum("bqhd,bkhd->bhqk", qi, k).astype(jnp.float32) * scale
        p = jax.nn.softmax(s, axis=-1).astype(v.dtype)
        return jnp.einsum("bhqk,bkhd->bqhd", p, v)

    o = lax.map(blk, qb)
    return jnp.moveaxis(o, 0, 1).reshape(b, l, h, d)

def _latent_na(q, k, v, k_ctx, v_ctx, rpb):
    b, n, h, d = q.shape
    rows = n // GRID_W
    kr = min(NA_ROWS_MAX, rows)
    qg = q.reshape(b, rows, GRID_W, h, d)
    kg = k.reshape(b, rows, GRID_W, h, d)
    vg = v.reshape(b, rows, GRID_W, h, d)
    col = jnp.arange(GRID_W)
    c0 = jnp.clip(col - NA_COLS // 2, 0, GRID_W - NA_COLS)
    col_ok = (col[None, :] >= c0[:, None]) & (col[None, :] < c0[:, None] + NA_COLS)
    dc_idx = jnp.clip(col[None, :] - col[:, None] + NA_COLS - 1, 0, RPB_C - 1)
    scale = HEAD_DIM ** -0.5
    neg = jnp.float32(-1e30)

    def row_block(r):
        r0 = jnp.clip(r - kr // 2, 0, rows - kr)
        qr = lax.dynamic_index_in_dim(qg, r, axis=1, keepdims=False)
        kw = lax.dynamic_slice_in_dim(kg, r0, kr, axis=1)
        vw = lax.dynamic_slice_in_dim(vg, r0, kr, axis=1)
        dr_idx = r0 + jnp.arange(kr) - r + NA_ROWS_MAX - 1
        bias = rpb[:, dr_idx[:, None, None], dc_idx[None, :, :]]
        bias = jnp.transpose(bias, (0, 2, 1, 3)).astype(jnp.float32)
        s_loc = jnp.einsum("bqhd,bikhd->bhqik", qr, kw).astype(jnp.float32) * scale + bias[None]
        s_loc = jnp.where(col_ok[None, None, :, None, :], s_loc, neg)
        s_ctx = jnp.einsum("bqhd,bjhd->bhqj", qr, k_ctx).astype(jnp.float32) * scale
        s = jnp.concatenate([s_loc.reshape(b, h, GRID_W, kr * GRID_W), s_ctx], axis=-1)
        p = jax.nn.softmax(s, axis=-1).astype(v.dtype)
        p_loc = p[..., : kr * GRID_W].reshape(b, h, GRID_W, kr, GRID_W)
        p_ctx = p[..., kr * GRID_W:]
        return (jnp.einsum("bhqik,bikhd->bqhd", p_loc, vw)
                + jnp.einsum("bhqj,bjhd->bqhd", p_ctx, v_ctx))

    o = lax.map(row_block, jnp.arange(rows))
    return jnp.moveaxis(o, 0, 1).reshape(b, n, h, d)

def _na_out(x, o, z, gate, w_out):
    b, l = x.shape[:2]
    out = (o.reshape(b, l, D_MODEL) * jax.nn.silu(z)) @ w_out
    return x + gate * out

def _na_layer_ctx(x, c_ctx, p):
    g, w_ada, b_ada, w_in, rpb, w_out = p
    h, gate = _pre(x, c_ctx, g, w_ada, b_ada)
    q, k, v, z = _na_proj(h, w_in)
    o = _ctx_attention(q, k, v)
    return _na_out(x, o, z, gate, w_out), k, v

def _na_layer_lat(x, cond, k_ctx, v_ctx, p):
    g, w_ada, b_ada, w_in, rpb, w_out = p
    h, gate = _pre(x, cond, g, w_ada, b_ada)
    q, k, v, z = _na_proj(h, w_in)
    o = _latent_na(q, k, v, k_ctx, v_ctx, rpb)
    return _na_out(x, o, z, gate, w_out)

def _s5_discretise(a_re, a_im, log_dt, b_re, b_im):
    a_re = a_re.astype(jnp.float32)
    a_im = a_im.astype(jnp.float32)
    b_re = b_re.astype(jnp.float32)
    b_im = b_im.astype(jnp.float32)
    dt = jnp.exp(log_dt.astype(jnp.float32))[:, None]
    mag = jnp.exp(a_re * dt)
    ab_re = mag * jnp.cos(a_im * dt)
    ab_im = mag * jnp.sin(a_im * dt)
    den = a_re * a_re + a_im * a_im
    nr = ab_re - 1.0
    f_re = (nr * a_re + ab_im * a_im) / den
    f_im = (ab_im * a_re - nr * a_im) / den
    bb_re = f_re[..., None] * b_re - f_im[..., None] * b_im
    bb_im = f_re[..., None] * b_im + f_im[..., None] * b_re
    return ab_re, ab_im, bb_re, bb_im

def _complex_combine(e1, e2):
    a1r, a1i, b1r, b1i = e1
    a2r, a2i, b2r, b2i = e2
    return (a2r * a1r - a2i * a1i, a2r * a1i + a2i * a1r,
            a2r * b1r - a2i * b1i + b2r, a2r * b1i + a2i * b1r + b2i)

def _s5_scan(ug, a_re, a_im, log_dt, b_re, b_im, h0):
    ab_re, ab_im, bb_re, bb_im = _s5_discretise(a_re, a_im, log_dt, b_re, b_im)
    bu_re = jnp.einsum("blgc,gpc->blgp", ug, bb_re)
    bu_im = jnp.einsum("blgc,gpc->blgp", ug, bb_im)
    if h0 is not None:
        h0r, h0i = h0
        bu_re = bu_re.at[:, 0].add(ab_re * h0r - ab_im * h0i)
        bu_im = bu_im.at[:, 0].add(ab_re * h0i + ab_im * h0r)
    ar = jnp.broadcast_to(ab_re, bu_re.shape)
    ai = jnp.broadcast_to(ab_im, bu_re.shape)
    _, _, hr, hi = lax.associative_scan(_complex_combine, (ar, ai, bu_re, bu_im), axis=1)
    return hr, hi

def _s5_readout(hr, hi, c_re, c_im):
    return (jnp.einsum("blgp,gcp->blgc", hr, c_re.astype(jnp.float32))
            - jnp.einsum("blgp,gcp->blgc", hi, c_im.astype(jnp.float32)))

def _s5_layer(x, cond, p, init, return_state):
    (g, w_ada, b_ada, w_in, a_re, a_im, log_dt, b_re, b_im, c_re, c_im,
     d_skip, w_glu, b_glu, w_out) = p
    bsz, l, _ = x.shape
    h, gate = _pre(x, cond, g, w_ada, b_ada)
    u, z = jnp.split(h @ w_in, 2, axis=-1)
    uf = u.astype(jnp.float32)
    ug = uf.reshape(bsz, l, S5_GROUPS, S5_CH)
    if init is None:
        h0f, h0b = None, None
    else:
        st = init.astype(jnp.float32)
        h0f, h0b = (st[:, 0, 0], st[:, 0, 1]), (st[:, 1, 0], st[:, 1, 1])
    hfr, hfi = _s5_scan(ug, a_re[0], a_im[0], log_dt[0], b_re[0], b_im[0], h0f)
    hbr, hbi = _s5_scan(ug[:, ::-1], a_re[1], a_im[1], log_dt[1], b_re[1], b_im[1], h0b)
    y = _s5_readout(hfr, hfi, c_re[0], c_im[0]) + _s5_readout(hbr, hbi, c_re[1], c_im[1])[:, ::-1]
    y = y.reshape(bsz, l, D_MODEL) + d_skip.astype(jnp.float32) * uf
    y = jax.nn.gelu(y).astype(x.dtype)
    y = y * jax.nn.sigmoid(y @ w_glu + b_glu)
    out = (y * jax.nn.silu(z)) @ w_out
    x_new = x + gate * out
    if return_state:
        final = jnp.stack([jnp.stack([hfr[:, -1], hfi[:, -1]], axis=1),
                           jnp.stack([hbr[:, -1], hbi[:, -1]], axis=1)], axis=1)
        return x_new, final
    return x_new

def setup_inputs(seed: int = 0) -> dict:
    key = jax.random.key(seed)
    ks = jax.random.split(key, 32)
    f32 = jnp.float32
    d = D_MODEL
    sd = d ** -0.5

    def nrm(k, shape, s=1.0):
        return jax.random.normal(k, shape, f32) * s

    n_idx = jnp.arange(S5_P, dtype=f32)
    return {
        "x_prompt": nrm(ks[0], (BATCH, SEQ, d)),
        "x_sample": nrm(ks[1], (DEC_BATCH, DEC_SEQ, d)),
        "cache_l0_k": nrm(ks[2], (DEC_BATCH, PAST_LEN, N_HEADS, HEAD_DIM)),
        "cache_l0_v": nrm(ks[3], (DEC_BATCH, PAST_LEN, N_HEADS, HEAD_DIM)),
        "state_l1_s5": nrm(ks[4], (DEC_BATCH, 2, 2, S5_GROUPS, S5_P), 0.5),
        "c": nrm(ks[5], (DEC_BATCH, d)),
        "c_ctx": nrm(ks[6], (d,)),
        "l0_norm_g": 1.0 + nrm(ks[7], (d,), 0.1),
        "l0_w_ada": nrm(ks[8], (d, 3 * d), 0.5 * sd),
        "l0_b_ada": nrm(ks[9], (3 * d,), 0.01),
        "l0_w_in": nrm(ks[10], (d, 4 * d), sd),
        "l0_rpb": nrm(ks[11], (N_HEADS, RPB_R, RPB_C), 0.1),
        "l0_w_out": nrm(ks[12], (d, d), sd),
        "l1_norm_g": 1.0 + nrm(ks[13], (d,), 0.1),
        "l1_w_ada": nrm(ks[14], (d, 3 * d), 0.5 * sd),
        "l1_b_ada": nrm(ks[15], (3 * d,), 0.01),
        "l1_w_in": nrm(ks[16], (d, 2 * d), sd),
        "l1_a_re": -0.5 + nrm(ks[17], (2, S5_GROUPS, S5_P), 0.01),
        "l1_a_im": jnp.pi * n_idx + nrm(ks[18], (2, S5_GROUPS, S5_P), 0.01),
        "l1_log_dt": jax.random.uniform(ks[19], (2, S5_GROUPS), f32,
                                        minval=math.log(DT_MIN), maxval=math.log(DT_MAX)),
        "l1_b_re": nrm(ks[20], (2, S5_GROUPS, S5_P, S5_CH), (2.0 * S5_CH) ** -0.5),
        "l1_b_im": nrm(ks[21], (2, S5_GROUPS, S5_P, S5_CH), (2.0 * S5_CH) ** -0.5),
        "l1_c_re": nrm(ks[22], (2, S5_GROUPS, S5_CH, S5_P), (2.0 * S5_P) ** -0.5),
        "l1_c_im": nrm(ks[23], (2, S5_GROUPS, S5_CH, S5_P), (2.0 * S5_P) ** -0.5),
        "l1_d": nrm(ks[24], (d,)),
        "l1_w_glu": nrm(ks[25], (d, d), sd),
        "l1_b_glu": nrm(ks[26], (d,), 0.01),
        "l1_w_out": nrm(ks[27], (d, d), sd),
        "final_norm_g": 1.0 + nrm(ks[28], (d,), 0.1),
    }

def reference(x_prompt, x_sample, cache_l0_k, cache_l0_v, state_l1_s5, c, c_ctx,
              l0_norm_g, l0_w_ada, l0_b_ada, l0_w_in, l0_rpb, l0_w_out,
              l1_norm_g, l1_w_ada, l1_b_ada, l1_w_in, l1_a_re, l1_a_im, l1_log_dt,
              l1_b_re, l1_b_im, l1_c_re, l1_c_im, l1_d, l1_w_glu, l1_b_glu, l1_w_out,
              final_norm_g):
    params = [
        (l0_norm_g, l0_w_ada, l0_b_ada, l0_w_in, l0_rpb, l0_w_out),
        (l1_norm_g, l1_w_ada, l1_b_ada, l1_w_in, l1_a_re, l1_a_im, l1_log_dt,
         l1_b_re, l1_b_im, l1_c_re, l1_c_im, l1_d, l1_w_glu, l1_b_glu, l1_w_out),
    ]
    caches = [(cache_l0_k, cache_l0_v), (state_l1_s5,)]
    cond = c[:, None, :]
    yp, ys = x_prompt, x_sample
    new_state = []
    for i in range(DEPTH):
        if i % N_MIXERS == 0:
            yp, k_new, v_new = _na_layer_ctx(yp, c_ctx, params[i])
            ys = _na_layer_lat(ys, cond, caches[i][0], caches[i][1], params[i])
            new_state += [k_new, v_new]
        else:
            yp, st_new = _s5_layer(yp, c_ctx, params[i], None, True)
            ys = _s5_layer(ys, cond, params[i], caches[i][0], False)
            new_state.append(st_new)
    y_prompt = _rmsnorm(yp, final_norm_g)
    y_sample = _rmsnorm(ys, final_norm_g)
    new_k_l0, new_v_l0, new_state_l1 = new_state
    return (y_prompt, y_sample, new_k_l0, new_v_l0, new_state_l1)


_drawn_inputs = setup_inputs


def setup_inputs(seed=0):
    import zlib

    import numpy as np

    out = dict(_drawn_inputs(seed))
    spreads = {}
    factors = {'cache_l0_k': 2.937,
     'l0_b_ada': 4.257,
     'l0_rpb': 64.0,
     'l1_b_ada': 3.047,
     'l1_a_re': 20.615,
     'l1_b_glu': 64.0,
     'l1_c_re': 3.219,
     'l1_c_im': 3.234}
    for name, (base, spread) in spreads.items():
        noise = np.random.default_rng([zlib.crc32(name.encode()), seed]).standard_normal(out[name].shape)
        drawn = base * np.exp(spread * noise) if base else spread * noise
        out[name] = __import__('jax').numpy.asarray(drawn.astype(out[name].dtype))
    for name, factor in factors.items():
        out[name] = (out[name] * factor).astype(out[name].dtype)
    return out
```

```python
import math
from contextlib import ExitStack

import concourse.bass as bass
from concourse import mybir
import numpy as np

F32 = mybir.dt.float32
F32R = mybir.dt.float32r
ALU = mybir.AluOpType
ACT = mybir.ActivationFunctionType
AX = mybir.AxisListType.X

P = 128
D = 2048
KT = D // P
NS = 2
BN = 512
CK = 4
NCK = KT // CK
NH = 16
HB = BN // P
EPS = 1e-6
QSCALE = float(P) ** -0.5
GRID_W, NA_COLS, NA_ROWS = 64, 16, 8
NEG = -1e30
S5G, S5P, S5C = 128, 64, 16
CH = 4
NCH = P // CH
M2 = NS * NCH
NW = 4
NR = 16
GW = 2 * NR
NDL = 2 * CH - 1

B_IN0, B_OUT0, B_IN1, B_GLU, B_OUT1, B_END = 0, 16, 20, 28, 32, 36
A_EARLY = 8


S5_U0 = (B_GLU - 1, 3)
UB = 2 * NCK
NU = B_END * UB
TG = KT // 2
STAGES = (B_IN0, B_OUT0, B_IN1, B_GLU, B_OUT1)


EARLY = (("ada", 0), ("ada", 1), ("ada", 2), ("ada", 3), ("b", 0), ("ada", 4), ("band", 0), ("ada", 5), ("b", 1),
         ("ada", 6), ("ada", 7), ("band", 1), ("b", 2), ("band", 2), ("b", 3), ("band", 3))
ROUND = 1.5 * 2.0 ** 23
TWO_PI_HI = 6.28125
TWO_PI_LO = 2 * math.pi - TWO_PI_HI


def ada_beside(b):
    if 0 <= b < 12:
        return 8 + b
    if B_OUT0 <= b < B_OUT0 + 4:
        return 20 + b - B_OUT0
    return None


def is_gate(a):
    return a % 12 >= 8


def fins(b):
    return sum(1 + is_gate(ada_beside(x)) for x in range(b) if ada_beside(x) is not None)


def ada_order(b):
    return sum(ada_beside(x) is not None for x in range(b))



def build(nc, d):
    with ExitStack() as ctx:
        K = 1024

        def at(name, shape, off, dt=F32):
            return nc.alloc_sbuf_tensor_at(name, shape, dt, offset=16512 + off)

        def sem(name):
            return ctx.enter_context(nc.semaphore(name))

        raw = at("raw", [P, 4, CK * BN], 0)
        whi = at("whi", [P, 4, 2, BN], 32 * K, F32R)
        wlo = at("wlo", [P, 4, 2, BN], 48 * K, F32R)
        araw = at("araw", [P, 2, CK * BN], 64 * K)
        xhi = at("xhi", [P, KT, NS, P], 80 * K, F32R)
        xlo = at("xlo", [P, KT, NS, P], 96 * K, F32R)
        X = at("X", [P, NS, D], 112 * K)
        gate = at("gate", [P, NS, D], 128 * K)
        WA = at("WA", [P, NS, D], 144 * K)
        m = 160 * K
        ident = at("ident", [P, P], m)
        perm = at("perm", [P, P], m + 512)
        selbc = at("selbc", [P, NS, P], m + K)
        coef = at("coef", [P, NW, 2, 2, 2 * GW], m + 2 * K)
        sel2 = at("sel2", [P, NS], m + 6 * K)
        bT = at("bT", [P, 24, 4], m + 6 * K + 64)
        gT = at("gT", [P, 2, KT], m + 6 * K + 512)
        shT = at("shT", [P, 2, KT, NS], m + 6 * K + 768)
        gsT = at("gsT", [P, 2, KT, NS], m + 7 * K + 256)
        condT = at("condT", [P, KT, NS], m + 7 * K + 512)
        stat = at("stat", [P, 32], m + 7 * K + 640)
        modt = at("modt", [P, 64], m + 7 * K + 768)
        cT32 = at("cT32", [P, KT, 32], m + 8 * K)
        adasb = at("adasb", [P, 2, BN], m + 10 * K)
        bgate = at("bgate", [P, BN], m + 14 * K)
        ar = 176 * K
        qkvz = at("qkvz", [P, 4, NS, BN], 112 * K)
        qT = at("qT", [P, NS, BN], ar)
        kT = at("kT", [P, NS, BN], ar + 4 * K)
        pr = at("pr", [P, 3, BN], ar + 8 * K)
        pT = at("pT", [P, 3, BN], ar + 14 * K)
        bias_b = at("bias_b", [P, BN], ar + 20 * K)
        kc_b = at("kc_b", [P, BN], ar + 22 * K)
        vc_b = at("vc_b", [P, BN], ar + 24 * K)
        asm = at("asm", [P, 16, HB], ar + 26 * K)
        tmo = at("tmo", [P, 2, BN], ar + 27 * K)
        cre = at("cre", [P, S5G, S5C], 32 * K)
        cim = at("cim", [P, S5G, S5C], 40 * K)
        bre = at("bre", [P, S5G, S5C], 48 * K)
        bim = at("bim", [P, S5G, S5C], 56 * K)
        bt = at("bt", [P, 2, NR, 2, CH * S5C], 48 * K)
        bb = at("bb", [P, 2, S5G, S5C], 64 * K)
        m1 = at("m1", [P, GW * CH * S5C], 80 * K)
        m2 = at("m2", [P, GW * CH * S5C], 88 * K)
        ce = at("ce", [P, 2, GW, CH + 2, S5C], 96 * K)
        bbf = at("bbf", [P, 2, NR, 2, S5C], 120 * K)
        bbb = at("bbb", [P, 2, NR, 2, S5C], 124 * K)
        bs = at("bs", [P, NR, 2, P], ar)
        bands = at("bands", [P, 4, 2, NDL, S5C], ar + 16 * K)
        pb = at("pb", [P, 2, CH, S5G], ar + 20 * K)
        py = at("py", [P, 2, CH, S5G], ar + 24 * K)
        dm = at("dm", [P, NR, 2, S5C], ar + 28 * K)
        tmp = at("tmp", [P, 18, S5G], ar)
        apw = at("apw", [P, 2, CH + 1, S5G], ar + 9 * K)
        btab = at("btab", [P, 2, NR, 2, P], 0)
        ctab = at("ctab", [P, 2, GW, CH * S5C], 32 * K)
        hy = at("hy", [P, 2, 2 * GW, NCH], 48 * K)
        kd = at("kd", [P, NR, P], 64 * K)
        ub = at("ub", [P, 2, NS, BN], 72 * K)
        ys = at("ys", [P, CH, NR * S5C], 72 * K)
        sb = at("sb", [P, 2, NCH + 1, 2, 2 * GW], 79 * K)
        utf = at("utf", [P, 2, NR, P], ar)
        utr = at("utr", [P, NR, P], m + 8 * K)
        u2p = at("u2p", [P, 8, 2 * CH * S5C], ar + 16 * K)
        u2 = at("u2", [P, CH, 2, P], ar + 20 * K)
        ss = at("ss", [P, 2, 2 * P], ar + 24 * K)
        h0 = at("h0", [P, NW, 2, 2 * GW], ar + 26 * K)
        fs = at("fs", [P, 2, S5G], ar + 28 * K)
        t12 = at("t12", [P, 2, 2, 2 * GW], ar + 29 * K)
        fso = at("fso", [P, 2, P], ar + 30 * K)
        Y = at("Y", [P, NS, D], 64 * K)
        bglu = at("bglu", [P, D], ar)
        gfin = at("gfin", [P, D], ar + 8 * K)
        tg = at("tg", [P, 4, BN], ar + 16 * K)

        ps = ctx.enter_context(nc.psum_tensor("ps", [P, 8, BN], F32))

        band_d = nc.dram_tensor("band_scratch", (NW, 4, 4, 2, S5C, NDL * S5C), F32).ap()
        bt_d = nc.dram_tensor("btab_scratch", (NW, P, NR * 2 * P), F32).ap()
        ct_d = nc.dram_tensor("ctab_scratch", (NW, P, 2, GW, CH * S5C), F32).ap()
        u_d = nc.dram_tensor("u_scratch", (NS * P, D), F32).ap()
        y_d = nc.dram_tensor("y_scratch", (NS * P, D), F32).ap()

        s_const, s_pole, s_par, s_x = sem("const_in"), sem("poles_in"), sem("params_in"), sem("x_in")
        s_raw = [sem(f"raw_in{i}") for i in range(4)]
        s_araw = [sem(f"araw_in{i}") for i in range(2)]
        s_hi, s_lo, s_wused = sem("w_hi"), sem("w_lo"), sem("w_used")
        s_ada0, s_ada1 = sem("ada_early_used"), sem("ada_used")
        s_cz, s_cond, s_adasb = sem("cond_zero"), sem("cond_ready"), sem("ada_sb")
        s_adaE, s_adaEout = sem("ada_early_fin"), sem("ada_early_out")
        s_adafin, s_adaout, s_bg = sem("ada_fin"), sem("ada_out"), sem("bgate_in")
        s_evA, s_evV = sem("acc_evacuated_act"), sem("acc_evacuated_dve")
        s_tp, s_taff, s_xhi, s_xlo = sem("t_pe"), sem("t_affine"), sem("x_hi"), sem("x_lo")
        s_dve, s_act, s_pool = sem("dve_order"), sem("act_order"), sem("pool_order")
        s_ang, s_exp, s_pow, s_pbpy = sem("s5_angles"), sem("s5_exp"), sem("s5_powers"), sem("pb_py")
        s_btm, s_btT, s_bs, s_bsout = sem("b_table"), sem("b_tr"), sem("b_staged"), sem("b_stored")
        s_ctm, s_ends, s_bbm, s_ctout = sem("c_table"), sem("c_ends"), sem("bb_ready"), sem("c_stored")
        s_band, s_bandsb, s_bandd, s_bandout = sem("band_pe"), sem("band_sb"), sem("band_d"), sem("band_stored")
        s_attin, s_kvout = sem("att_in"), sem("kv_out")
        s_qT, s_qTsb, s_kT, s_kTsb = sem("qT_pe"), sem("qT_sb"), sem("kT_pe"), sem("kT_sb")
        s_sc, s_sub, s_prob, s_rs = sem("scores"), sem("scores_shifted"), sem("probs"), sem("row_sums")
        s_pT, s_pTsb, s_pv, s_og = sem("pT_pe"), sem("pT_sb"), sem("pv"), sem("gated_o")
        s_x2in, s_stat, s_rstd, s_xn = sem("x_again"), sem("square_sums"), sem("rstd"), sem("x_normed")
        s_ubout = [sem(f"u_stored{i}") for i in range(2)]
        s_u2, s_u2p, s_zero = sem("u2_in"), sem("u2_ordered"), sem("zeros")
        s_uT, s_uTsb = sem("uT_pe"), sem("uT_sb")
        s_bt = [sem(f"btab_in{i}") for i in range(2)]
        s_hyf, s_factors = sem("hy_forward"), sem("scan_factors")
        s_ct, s_kd, s_h0 = sem("ctab_in"), sem("kd_in"), sem("h0_in")
        s_S, s_Ssb, s_ST, s_STsb = sem("S_pe"), sem("S_sb"), sem("ST_pe"), sem("ST_sb")
        s_scan, s_hy, s_y, s_ysb = sem("scan"), sem("hy"), sem("y_pe"), sem("y_sb")
        s_yout, s_fs, s_fsT, s_fso, s_yin = sem("y_stored"), sem("fin_state"), sem("fin_T"), sem("fin_sb"), sem("y_in")
        s_mag = sem("s5_mag")
        s_vec, s_gsig, s_g = sem("vectors_in"), sem("glu_sig"), sem("gated_y")
        s_x2, s_fin, s_out = sem("x2"), sem("final"), sem("outputs")
        block = ctx.enter_context(nc.Block())

        def wait_evacuated(eng, b):
            if b < B_OUT0:
                eng.wait_ge(s_evA, NS * (b + 1))
            elif b < B_IN1:
                eng.wait_ge(s_evV, NS * (b - B_OUT0 + 1))
            elif b < B_GLU:
                eng.wait_ge(s_evA, NS * (B_OUT0 + b - B_IN1 + 1))
            else:
                eng.wait_ge(s_evV, NS * (B_IN1 - B_OUT0 + b - B_GLU + 1))

        def chain(eng, s):
            n = [0]

            def mark(ins):
                n[0] += 1
                ins.then_inc(s, 1)
                eng.wait_ge(s, n[0])
            return mark

        @block.sync
        def _(sp):
            for name, dst in (("condT", condT), ("ident", ident), ("perm", perm), ("selbc", selbc),
                              ("sel2", sel2), ("bT", bT), ("gT", gT)):
                sp.dma_start(dst[:], d[name]).then_inc(s_const, 16)
            for e in range(A_EARLY * NCK):
                if e >= 4:
                    sp.wait_ge(s_ada0, e - 3)
                sp.dma_start(raw[:, e % 4], d["wada"][e // NCK, :, e % NCK]).then_inc(s_raw[e % 4], 16)
            def load_tables():
                def b_table(w):
                    sp.dma_start(btab[:, w % 2].rearrange("p r i c -> p (r i c)"), bt_d[w]).then_inc(s_bt[w % 2], 16)

                def y_tables(w):
                    sp.dma_start(ctab[:], ct_d[w]).then_inc(s_ct, 16)
                    for e in range(2):
                        for s in range(CH):
                            p0 = e * CH * S5C + s * S5C
                            k0 = (CH - 1 - s) * S5C
                            sp.dma_start(kd[p0:p0 + S5C, :, e * 64:e * 64 + 64],
                                         band_d[w, :, :, e].rearrange("q j c k -> c (q j) k")[:, :, k0:k0 + 64]).then_inc(s_kd, 16)

                sp.wait_ge(s_bsout, 16 * NW)
                sp.wait_ge(s_ctout, 32 * NW)
                sp.wait_ge(s_bandout, 128 * NW)
                sp.wait_ge(s_zero, 1)
                for w in range(2):
                    sp.wait_ge(s_lo, UB * B_GLU - 4 + 4 * w)
                    b_table(w)
                sp.wait_ge(s_wused, UB * B_GLU)
                y_tables(0)
                for w in range(1, NW):
                    if w + 1 < NW:
                        sp.wait_ge(s_S, NR * w)
                        b_table(w + 1)
                    sp.wait_ge(s_y, 4 * w)
                    y_tables(w)

            for g in range(B_END * NCK):
                b, c = g // NCK, g % NCK
                if g == B_GLU * NCK:
                    load_tables()
                    sp.wait_ge(s_S, NR * NW)
                if g < 4:
                    sp.wait_ge(s_ada0, A_EARLY * NCK - 3 + g)
                else:
                    sp.wait_ge(s_hi, 2 * (g - 3))
                    sp.wait_ge(s_lo, 2 * (g - 3))
                sp.dma_start(raw[:, g % 4], d["w"][b, :, c]).then_inc(s_raw[g % 4], 16)
                b, c = (g - 3) // NCK, (g - 3) % NCK
                if ada_beside(b) is not None:
                    n = NCK * ada_order(b) + c
                    if n == 0:
                        sp.wait_ge(s_ends, NW)
                        sp.wait_ge(s_btm, NW)
                    if n >= 2:
                        sp.wait_ge(s_ada1, n - 1)
                    sp.dma_start(araw[:, n % 2], d["wada"][ada_beside(b), :, c]).then_inc(s_araw[n % 2], 16)

        @block.gpsimd
        def _(pool):
            seq = chain(pool, s_pool)
            for name, dst in (("ldt", tmp[:, 0]), ("are", tmp[:, 1]), ("aim", tmp[:, 2])):
                pool.dma_start(dst, d[name]).then_inc(s_pole, 16)
            for st in range(NS):
                pool.dma_start(WA[:, st], d["x"][st]).then_inc(s_x, 16)
            for name, dst in (("bre", bre), ("bim", bim), ("cre", cre), ("cim", cim), ("dm", dm)):
                pool.dma_start(dst[:], d[name]).then_inc(s_par, 16)
            seq(nc.gpsimd.memset(bbf[:], 0.0))
            seq(nc.gpsimd.memset(bbb[:], 0.0))
            pool.wait_ge(s_pow, 1)
            for w in range(NW):
                for e in range(2):
                    g0 = w * GW + e * NR
                    for src, dst, ri, sign in ((0, 0, 0, 1.0), (0, 1, 1, 1.0), (1, 0, 1, -1.0), (1, 1, 0, 1.0)):
                        o = coef[:, w, src, dst].rearrange("p (r e s) -> p r e s", e=2, s=NS)[:, :, e]
                        power = apw[:, ri, CH, g0:g0 + NR].unsqueeze(2).to_broadcast([P, NR, NS])
                        last = nc.gpsimd.tensor_scalar(o, power, sign, None, ALU.mult)
                        if (w, e, src, dst) != (NW - 1, 1, 1, 1):
                            seq(last)
            last.then_inc(s_factors, 1)
            pool.wait_ge(s_factors, 1)
            pool.wait_ge(s_par, 16 * 5)
            pool.wait_ge(s_bbm, 1)
            for w in range(NW):
                if w >= 1:
                    pool.wait_ge(s_band, 4 * w)
                    pool.wait_ge(s_ctout, 32 * w)
                for ri in range(2):
                    for e in range(2):
                        g0 = w * GW + e * NR
                        seq(nc.gpsimd.tensor_copy(bbf[0:64, ri, :, e], bb[0:64, ri, g0:g0 + NR]))
                        seq(nc.gpsimd.tensor_copy(bbb[64:128, ri, :, e], bb[64:128, ri, g0:g0 + NR]))
                gs = slice(w * GW, (w + 1) * GW)
                for j in (0, CH + 1):
                    seq(nc.gpsimd.tensor_copy(ce[:, 0, :, j], cre[:, gs]))
                    last = nc.gpsimd.tensor_scalar(ce[:, 1, :, j], cim[:, gs], -1.0, None, ALU.mult)
                    if j == 0:
                        seq(last)
                last.then_inc(s_ends, 1)
                pool.wait_ge(s_ends, w + 1)
            pool.wait_ge(s_bandout, 16 * 8 * NW)
            pool.wait_ge(s_bsout, 16 * NW)
            for hb in range(NH // HB):
                if hb >= 1:
                    pool.wait_ge(s_pv, hb)
                for name, dst in (("bias", bias_b), ("kcT", kc_b), ("vc", vc_b)):
                    pool.dma_start(dst[:], d[name][hb]).then_inc(s_attin, 16)
                if hb == 0:
                    pool.dma_start(bgate[:], d["bgate"][0].partition_broadcast(P)).then_inc(s_bg, 16)
                for i, name in ((1, "new_k"), (2, "new_v")):
                    pool.wait_ge(s_evA, NS * (4 * hb + i + 1))
                    pool.dma_start(d[name][:, hb * BN:(hb + 1) * BN], qkvz[:, i, 0]).then_inc(s_kvout, 16)
                    if hb == 0:
                        pool.wait_ge(s_adaout, 2 * i)
                        pool.dma_start(bgate[:], d["bgate"][i].partition_broadcast(P)).then_inc(s_bg, 16)
                if hb == 0:
                    pool.wait_ge(s_adaout, 6)
                    pool.dma_start(bgate[:], d["bgate"][3].partition_broadcast(P)).then_inc(s_bg, 16)
            pool.wait_ge(s_adaout, 8)
            pool.dma_start(bgate[:], d["bgate"][4].partition_broadcast(P)).then_inc(s_bg, 16)
            pool.wait_ge(s_og, 8)
            pool.wait_ge(s_kvout, 16 * 8)
            for st in range(NS):
                pool.dma_start(X[:, st], d["x"][st]).then_inc(s_x2in, 16)
            pool.dma_start(h0[:], d["h0"]).then_inc(s_h0, 16)
            for i in range(1, 4):
                pool.wait_ge(s_adaout, 16 + 2 * i)
                pool.dma_start(bgate[:], d["bgate"][4 + i].partition_broadcast(P)).then_inc(s_bg, 16)
            pool.wait_ge(s_x2, 1)
            pool.wait_ge(s_adaout, fins(B_END))
            seq(nc.gpsimd.memset(kd[:], 0.0))
            seq(nc.gpsimd.memset(utf[:], 0.0))
            nc.gpsimd.memset(utr[:], 0.0).then_inc(s_zero, 1)
            for w in range(NW):
                wait_evacuated(pool, B_IN1 + w)
                for st in range(NS):
                    pool.dma_start(u_d[st * P:(st + 1) * P, w * BN:(w + 1) * BN], ub[:, w % 2, st]).then_inc(s_ubout[w % 2], 16)

            def load_u(w):
                for gh in range(2):
                    for e in range(2):
                        c0 = w * BN + e * 256 + gh * P
                        pool.dma_start(u2[gh * M2:(gh + 1) * M2, :, e],
                                       u_d[:, c0:c0 + P].rearrange("(m t) c -> m t c", t=CH)).then_inc(s_u2, 16)
                pool.wait_ge(s_u2, 64 * (w + 1))
                if w >= 1:
                    pool.wait_ge(s_uT, 4 * w)
                for e in range(2):
                    for t in range(CH):
                        o = u2p[:].rearrange("p v (e t c) -> p v e t c", e=2, t=CH)[:, :, e, t]
                        last = nc.gpsimd.tensor_copy(o, u2[:, t, e].rearrange("p (v c) -> p v c", c=S5C))
                        if (e, t) != (1, CH - 1):
                            seq(last)
                last.then_inc(s_u2p, 1)
                pool.wait_ge(s_u2p, w + 1)

            for i in range(2):
                pool.wait_ge(s_ubout[i], 16 * NW)
            load_u(0)
            load_u(1)
            for w in range(NW):
                if w + 2 < NW:
                    load_u(w + 2)
                pool.wait_ge(s_scan, w + 1)
                if w >= 1:
                    pool.wait_ge(s_y, 4 * w)
                src = sb[:, w % 2].rearrange("p k i x -> p i x k")
                for ri in range(2):
                    nc.gpsimd.tensor_copy(hy[0:S5P, ri], src[0:S5P, ri, :, 0:NCH]).then_inc(s_hyf, 1)
                    pool.wait_ge(s_hyf, 2 * w + ri + 1)
                pool.wait_ge(s_ysb, 4 * (w + 1))
                for e in range(2):
                    c0 = w * BN + e * 256
                    pool.dma_start(y_d[:, c0:c0 + 256].rearrange("(m t) c -> m t c", t=CH),
                                   ys[e * M2:(e + 1) * M2]).then_inc(s_yout, 16)
            pool.wait_ge(s_yout, 32 * NW)
            for st in range(NS):
                pool.dma_start(Y[:, st], y_d[st * P:(st + 1) * P]).then_inc(s_yin, 16)
            pool.wait_ge(s_y, 4 * NW)
            pool.dma_start(bglu[:], d["b_glu"].partition_broadcast(P)).then_inc(s_vec, 16)
            pool.dma_start(gfin[:], d["g_fin"].partition_broadcast(P)).then_inc(s_vec, 16)
            pool.wait_ge(s_fso, 1)
            for ri in range(2):
                pool.dma_start(d["new_state"][:, ri].rearrange("d g p -> g d p"),
                               fso[:, ri].rearrange("g (d p) -> g d p", d=2)).then_inc(s_out, 16)
            for st in range(NS):
                pool.wait_ge(s_fin, st + 1)
                pool.dma_start(d["y"][st], X[:, st]).then_inc(s_out, 16)
            pool.wait_ge(s_out, 64)
            pool.wait_ge(s_kvout, 128)

        @block.tensor
        def _(pe):
            mm = nc.tensor.matmul
            tr = nc.tensor.transpose

            def ada_chunk(bank, rhs, c):
                for j in range(CK):
                    last = mm(ps[32 * j:32 * j + 32, bank], cT32[:, c * CK + j], rhs[:, j * BN:(j + 1) * BN],
                              start=c == 0, stop=c == NCK - 1)
                return last

            def ada_columns(a, out):
                for i in range(4):
                    last = mm(out[:, 2 * i:2 * i + 2], adasb[:, a % 2, i * P:(i + 1) * P], sel2[:],
                              start=True, stop=True)
                return last

            pe.wait_ge(s_const, 16 * 7)
            pe.wait_ge(s_cond, 1)

            def ada_early(a):
                if a >= 2:
                    pe.wait_ge(s_adasb, a - 1)
                for c in range(NCK):
                    pe.wait_ge(s_raw[c], 16 * (a + 1))
                    last = ada_chunk(4 if a % 2 == 0 else 1, raw[:, c], c)
                    last.then_inc(s_ada0, 1)

            def b_tables(w):
                pe.wait_ge(s_btm, w + 1)
                for i in range(NR // 2):
                    n = w * 8 + i
                    if n >= 2:
                        pe.wait_ge(s_bs, n - 1)
                    for r in range(2):
                        for ri in range(2):
                            c0 = (2 * r + ri) * P
                            last = tr(ps[:, 5 + n % 2, c0:c0 + P],
                                      bt[:, ri, 2 * i + r].rearrange("p e c -> p (e c)"), ident[:])
                    last.then_inc(s_btT, 1)

            def band_products(w):
                pe.wait_ge(s_ctm, w + 1)
                pe.wait_ge(s_ends, w + 1)
                for q in range(4):
                    n = w * 4 + q
                    if n >= 2:
                        pe.wait_ge(s_bandd, n - 1)
                    for half in range(2):
                        for ri in range(2):
                            for j in range(4):
                                r = 4 * q + j
                                lhs = (bbf, bbb)[half][:, ri, r].rearrange("p e c -> p (e c)")
                                j0 = (0, 2)[half]
                                rhs = ce[:, ri].rearrange("p (e r) j c -> p e r (j c)", e=2)[
                                    :, :, r, j0 * S5C:(j0 + CH) * S5C]
                                last = mm(ps[32 * j:32 * j + 32, (7, 3)[n % 2], half * P:(half + 1) * P], lhs, rhs,
                                          start=ri == 0, stop=ri == 1)
                    last.then_inc(s_band, 1)

            for step, n in EARLY:
                if step == "ada":
                    ada_early(n)
                    pe.wait_ge(s_adasb, n + 1)
                    last = ada_columns(n, ps[:, 0, 8 * n:8 * n + 8])
                    if n == A_EARLY - 1:
                        last.then_inc(s_adaE, 1)
                elif step == "b":
                    b_tables(n)
                else:
                    band_products(n)
            pe.wait_ge(s_bandd, 16)
            pe.wait_ge(s_bs, 32)
            pe.wait_ge(s_adaEout, 1)

            def transposes(i, src):
                for g in range(TG):
                    n = TG * i + g
                    if g >= 3:
                        pe.wait_ge(s_xlo, n - 2)
                    for k in range(2):
                        for st in range(NS):
                            last = tr(ps[:, 5 + n % 3, (2 * k + st) * P:(2 * k + st + 1) * P],
                                      src[:, st, (2 * g + k) * P:(2 * g + k + 1) * P], ident[:])
                    last.then_inc(s_tp, 1)

            def unit(b, u):
                k0 = UB * b + u
                if b in STAGES:
                    pe.wait_ge(s_xlo, TG * STAGES.index(b) + u + 1)
                if u == 0 and b >= 2:
                    wait_evacuated(pe, b - 2)
                pe.wait_ge(s_lo, k0 + 1)
                s = k0 % 4
                for k in range(2):
                    kt = 2 * u + k
                    for st in range(NS):
                        acc = ps[:, 2 * (b % 2) + st]
                        mm(acc, xhi[:, kt, st], whi[:, s, k], start=kt == 0, stop=False)
                        mm(acc, xhi[:, kt, st], wlo[:, s, k], start=False, stop=False)
                        last = mm(acc, xlo[:, kt, st], whi[:, s, k], start=False, stop=kt == KT - 1)
                last.then_inc(s_wused, 1)

            def q_or_k(src, dst_bank, s):
                for st in range(NS):
                    for h in range(HB):
                        last = tr(ps[:, dst_bank + st, h * P:(h + 1) * P], src[:, st, h * P:(h + 1) * P], ident[:])
                last.then_inc(s, 1)

            def attention(hb, b, u):
                j = b % 4
                if (j, u) == (1, 3):
                    wait_evacuated(pe, 4 * hb)
                    if hb >= 1:
                        pe.wait_ge(s_og, 2 * hb)
                    q_or_k(qkvz[:, 0], 5, s_qT)
                if (j, u) == (2, 3):
                    wait_evacuated(pe, 4 * hb + 1)
                    pe.wait_ge(s_qTsb, 2 * (hb + 1))
                    q_or_k(qkvz[:, 1], 5, s_kT)
                if (j, u) == (2, 7):
                    pe.wait_ge(s_kTsb, 2 * (hb + 1))
                    pe.wait_ge(s_attin, 48 * (hb + 1))
                    pe.wait_ge(s_adaout, fins(b))
                    for h in range(HB):
                        c = slice(h * P, (h + 1) * P)
                        mm(ps[:, 5, c], qT[:, 0, c], kT[:, 0, c], start=True, stop=True)
                        mm(ps[:, 6, c], qT[:, 1, c], kT[:, 1, c], start=True, stop=True)
                        last = mm(ps[:, 7, c], qT[:, 1, c], kc_b[:, c], start=True, stop=True)
                    last.then_inc(s_sc, 1)
                if (j, u) == (3, 6):
                    pe.wait_ge(s_prob, 3 * (hb + 1))
                    pe.wait_ge(s_adaout, fins(b))
                    for i in range(3):
                        for h in range(HB):
                            c = slice(h * P, (h + 1) * P)
                            last = tr(ps[:, 5 + i, c], pr[:, i, c], ident[:])
                    last.then_inc(s_pT, 1)
                if (j, u) == (3, 7):
                    wait_evacuated(pe, 4 * hb + 2)
                    pe.wait_ge(s_pTsb, 3 * (hb + 1))
                    for h in range(HB):
                        c = slice(h * P, (h + 1) * P)
                        mm(ps[:, 5, c], pT[:, 0, c], qkvz[:, 2, 0, c], start=True, stop=True)
                        mm(ps[:, 6, c], pT[:, 1, c], qkvz[:, 2, 1, c], start=True, stop=False)
                        last = mm(ps[:, 6, c], pT[:, 2, c], vc_b[:, c], start=False, stop=True)
                    last.then_inc(s_pv, 1)

            def modulation(b, u):
                a0 = ada_beside(b - 1)
                a1 = ada_beside(b)
                if a0 is not None and u == 2:
                    pe.wait_ge(s_adasb, A_EARLY + ada_order(b))
                    if fins(b - 1) > 0:
                        pe.wait_ge(s_adaout, fins(b - 1))
                    if b % 4 == 3 and b < B_OUT0:
                        pe.wait_ge(s_sub, 3 * (b // 4 + 1))
                    elif 4 <= b < B_OUT0:
                        pe.wait_ge(s_pTsb, 3 * (b // 4))
                    elif b in STAGES:
                        pe.wait_ge(s_xlo, TG * (STAGES.index(b) + 1))
                    if is_gate(a0):
                        last = mm(ps[:, 7], selbc[:, 0], adasb[:, a0 % 2], start=True, stop=True)
                    else:
                        last = ada_columns(a0, ps[:, 7])
                    last.then_inc(s_adafin, 1)
                if a0 is not None and u == 4 and is_gate(a0):
                    pe.wait_ge(s_adaout, fins(b - 1) + 1)
                    mm(ps[:, 7], selbc[:, 1], adasb[:, a0 % 2], start=True, stop=True).then_inc(s_adafin, 1)
                if a1 is not None and u % 2 == 1:
                    c = u // 2
                    if c == 0:
                        pe.wait_ge(s_adasb, A_EARLY + ada_order(b))
                    n = NCK * ada_order(b) + c
                    pe.wait_ge(s_araw[n % 2], 16 * (n // 2 + 1))
                    ada_chunk(4, araw[:, n % 2], c).then_inc(s_ada1, 1)

            def s5_transposed(w):
                pe.wait_ge(s_u2p, w + 1)
                for i in range(4):
                    n = 4 * w + i
                    if n >= 2:
                        pe.wait_ge(s_uTsb, 2 * (n - 1))
                    for v in range(4):
                        src = u2p[:, 4 * (i // 2) + v]
                        out = ps[:, 5 + n % 2, v * P:(v + 1) * P]
                        if i % 2 == 0:
                            last = tr(out, src, ident[:])
                        else:
                            last = mm(out, src, perm[:], start=True, stop=True)
                    last.then_inc(s_uT, 1)

            def s5_sums(w):
                pe.wait_ge(s_uTsb, 8 * (w + 1))
                pe.wait_ge(s_bt[w % 2], 16 * (w // 2 + 1))

                def sums(r):
                    n = NR * w + r
                    if n >= 2:
                        pe.wait_ge(s_Ssb, n - 1)
                    for dr, src in ((0, utf[:, w % 2, r]), (1, utr[:, r])):
                        out = ps[:, (4, 7)[n % 2], 0:2 * P].rearrange("p (i c) -> p i c", i=2)[
                            :, :, dr * S5P:(dr + 1) * S5P]
                        last = mm(out, src, btab[:, w % 2, r, :, dr * S5P:(dr + 1) * S5P], start=True, stop=True)
                    last.then_inc(s_S, 1)

                sums(0)
                sums(1)
                for g in range(NR // 2):
                    n = NR // 2 * w + g
                    if g + 1 < NR // 2:
                        sums(2 * g + 2)
                        sums(2 * g + 3)
                    pe.wait_ge(s_Ssb, 2 * n + 2)
                    if n >= 2:
                        pe.wait_ge(s_STsb, n - 1)
                    for k in range(2):
                        for ri in range(2):
                            c0 = (2 * ri + k) * P
                            last = tr(ps[:, n % 2, c0:c0 + P], ss[:, k, ri * P:(ri + 1) * P], ident[:])
                    last.then_inc(s_ST, 1)

            def s5_outputs(w):
                pe.wait_ge(s_hy, 2 * (w + 1))
                pe.wait_ge(s_hyf, 2 * (w + 1))
                pe.wait_ge(s_ct, 16 * (w + 1))
                pe.wait_ge(s_kd, 16 * 8 * (w + 1))
                for q in range(4):
                    n = 4 * w + q
                    if n >= 2:
                        pe.wait_ge(s_ysb, n - 1)
                    for k in range(4):
                        r = 4 * q + k
                        out = ps[:, 2 + n % 2, k * P:(k + 1) * P]
                        mm(out, utf[:, w % 2, r], kd[:, r], start=True, stop=False)
                        for ri in range(2):
                            last = mm(out.rearrange("p (e k) -> p e k", e=2),
                                      hy[:, ri, 4 * r:4 * r + 4].rearrange("p x j -> p (x j)"),
                                      ctab[:, ri].rearrange("p (e r) k -> p e r k", e=2)[:, :, r],
                                      start=False, stop=ri == 1)
                    last.then_inc(s_y, 1)

            for b in range(B_END):
                if b == B_IN0:
                    pe.wait_ge(s_xn, 2)
                    transposes(0, WA)
                if b == B_OUT0:
                    pe.wait_ge(s_og, 8)
                    transposes(1, WA)
                if b == B_IN1:
                    pe.wait_ge(s_xn, 4)
                    transposes(2, WA)
                if b == B_GLU:
                    wait_evacuated(pe, B_GLU - 1)
                    s5_sums(0)
                    s5_transposed(1)
                    s5_sums(1)
                    for w in range(NW):
                        s5_outputs(w)
                        if w + 2 < NW:
                            s5_transposed(w + 2)
                            s5_sums(w + 2)
                    pe.wait_ge(s_scan, NW)
                    pe.wait_ge(s_Ssb, NR * NW)
                    for ri in range(2):
                        last = tr(ps[:, 4, ri * P:(ri + 1) * P], fs[:, ri], ident[:])
                    last.then_inc(s_fsT, 1)
                    pe.wait_ge(s_STsb, 8 * NW)
                    pe.wait_ge(s_ysb, 4 * NW)
                    pe.wait_ge(s_yin, 32)
                    transposes(3, Y)
                if b == B_OUT1:
                    pe.wait_ge(s_g, 8)
                    transposes(4, WA)
                for u in range(UB):
                    unit(b, u)
                    if b < B_OUT0:
                        attention(b // 4, b, u)
                    modulation(b, u)
                    if (b, u) == S5_U0:
                        s5_transposed(0)

        @block.scalar
        def _(act):
            seq = chain(act, s_act)
            af = nc.scalar.activation
            act.wait_ge(s_const, 16 * 7)
            act.wait_ge(s_cz, 1)
            af(cT32[:, :, 0:NS], condT[:], ACT.Silu).then_inc(s_cond, 1)

            def square_sums(i, src, junk):
                for st in range(NS):
                    af(junk[:, st], src[:, st], ACT.Square, accum_out=stat[:, 8 * i + st:8 * i + st + 1]).then_inc(s_stat, 1)

            def scale_rows(i, src, dst):
                act.wait_ge(s_rstd, 2 * i + 1)
                af(stat[:, 8 * i + 4:8 * i + 6], stat[:, 8 * i + 2:8 * i + 4], ACT.Sqrt).then_inc(s_stat, 1)
                act.wait_ge(s_rstd, 2 * i + 2)
                for st in range(NS):
                    af(dst[:, st], src[:, st], ACT.Copy, scale=stat[:, 8 * i + 6 + st:8 * i + 7 + st]).then_inc(s_xn, 1)

            act.wait_ge(s_pole, 16 * 3)
            af(tmp[:, 3], tmp[:, 0], ACT.Exp).then_inc(s_exp, 1)
            act.wait_ge(s_ang, 1)
            af(tmp[:, 5], tmp[:, 4], ACT.Exp)
            af(tmp[:, 9], tmp[:, 8], ACT.Sin)
            af(tmp[:, 10], tmp[:, 8], ACT.Sin, scale=0.5).then_inc(s_mag, 1)
            act.wait_ge(s_pow, 1)
            fwd, bwd = slice(0, S5P), slice(S5P, P)
            af(pb[fwd], apw[fwd][:, :, ::-1][:, :, 1:CH + 1], ACT.Copy)
            af(pb[bwd], apw[bwd][:, :, 0:CH], ACT.Copy)
            af(py[fwd], apw[fwd][:, :, 1:CH + 1], ACT.Copy)
            af(py[bwd], apw[bwd][:, :, ::-1][:, :, 0:CH], ACT.Copy).then_inc(s_pbpy, 1)

            def adasb_early(a):
                act.wait_ge(s_ada0, NCK * (a + 1))
                af(adasb[:, a % 2], ps[:, 4 if a % 2 == 0 else 1], ACT.Copy).then_inc(s_adasb, 1)

            def b_staged(w):
                if w == 0:
                    act.wait_ge(s_factors, 1)
                    act.wait_ge(s_bbm, 1)
                else:
                    act.wait_ge(s_bsout, 16 * w)
                for i in range(NR // 2):
                    act.wait_ge(s_btT, NR // 2 * w + i + 1)
                    af(bs[:, 2 * i:2 * i + 2].rearrange("p r i c -> p (r i c)"), ps[:, 5 + i % 2], ACT.Copy).then_inc(s_bs, 1)
                act.wait_ge(s_bs, NR // 2 * (w + 1))
                act.dma_start(bt_d[w], bs[:].rearrange("p r i c -> p (r i c)")).then_inc(s_bsout, 16)
                if w >= 1:
                    store_bands(w - 1)

            def store_bands(w):
                act.wait_ge(s_bandd, 4 * (w + 1))
                for j in range(4):
                    for e in range(2):
                        p0 = 32 * j + 16 * e
                        act.dma_start(band_d[w, :, j, e].rearrange("q c k -> c q k"),
                                      bands[p0:p0 + 16, :, e].rearrange("p q k c -> p q (k c)")).then_inc(s_bandout, 16)

            def bands_staged(w):
                act.wait_ge(s_ctm, w + 1)
                for ri in range(2):
                    act.dma_start(ct_d[w, :, ri], ce[:, ri, :, 1:CH + 1].rearrange("p g j c -> p g (j c)")).then_inc(s_ctout, 16)
                if w >= 1:
                    act.wait_ge(s_bandout, 16 * 8 * w)
                for q in range(4):
                    n = 4 * w + q
                    act.wait_ge(s_band, n + 1)
                    bank = ps[:, (7, 3)[n % 2]]
                    af(bands[:, q, :, CH - 1:NDL], bank[:, 0:P].rearrange("p (e k c) -> p e k c", e=2, c=S5C), ACT.Copy)
                    af(bands[:, q, :, 0:CH - 1], bank[:, P:2 * P].rearrange("p (e k c) -> p e k c", e=2, c=S5C)[
                        :, :, 0:CH - 1], ACT.Copy).then_inc(s_bandsb, 1)

            for step, n in EARLY:
                if step == "ada":
                    adasb_early(n)
                    if n == 2:
                        act.wait_ge(s_x, 32)
                        square_sums(0, WA, gate)
                elif step == "b":
                    b_staged(n)
                else:
                    bands_staged(n)
                    if n == 0:
                        act.wait_ge(s_stat, 2)
                        scale_rows(0, WA, WA)
            store_bands(NW - 1)

            def split(k):
                g = k // 2
                if k == 0:
                    act.wait_ge(s_btT, NW * NR // 2)
                    act.wait_ge(s_ends, NW)
                    act.wait_ge(s_ctm, NW)
                act.wait_ge(s_raw[g % 4], 16 * (A_EARLY * NCK // 4 + g // 4 + 1))
                if k >= 4:
                    act.wait_ge(s_wused, k - 3)
                src = raw[:, g % 4, (k % 2) * 2 * BN:(k % 2 + 1) * 2 * BN]
                af(whi[:, k % 4].rearrange("p k c -> p (k c)"), src, ACT.Copy).then_inc(s_hi, 1)

            def stage(i):
                if i == 0:
                    act.wait_ge(s_ctm, NW)
                for g in range(TG):
                    n = TG * i + g
                    act.wait_ge(s_tp, n + 1)
                    if i in (0, 2):
                        act.wait_ge(s_taff, TG * (i // 2) + g + 1)
                    af(xhi[:, 2 * g:2 * g + 2].rearrange("p k s c -> p (k s c)"), ps[:, 5 + n % 3], ACT.Copy).then_inc(s_xhi, 1)

            def evacuate_in0(b):
                hb, j = b // 4, b % 4
                if b == 0:
                    act.wait_ge(s_ctout, 32 * NW)
                    act.wait_ge(s_ends, NW)
                if hb >= 1:
                    if j == 0:
                        act.wait_ge(s_qT, hb)
                    elif j == 1:
                        act.wait_ge(s_kT, hb)
                        act.wait_ge(s_kvout, 32 * hb)
                    elif j == 2:
                        act.wait_ge(s_pv, hb)
                        act.wait_ge(s_kvout, 32 * hb)
                    else:
                        act.wait_ge(s_og, 2 * hb)
                for st in range(NS):
                    af(qkvz[:, j, st], ps[:, 2 * (b % 2) + st], ACT.Silu if j == 3 else ACT.Copy).then_inc(s_evA, 1)

            def attention(hb, j, u):
                if (j, u) == (1, 3):
                    if hb == 0:
                        act.wait_ge(s_bsout, 16 * NW)
                        act.wait_ge(s_bandout, 128 * NW)
                    act.wait_ge(s_qT, hb + 1)
                    if hb >= 1:
                        act.wait_ge(s_sc, hb)
                    for st in range(NS):
                        af(qT[:, st], ps[:, 5 + st], ACT.Copy, scale=QSCALE).then_inc(s_qTsb, 1)
                if (j, u) == (2, 3):
                    act.wait_ge(s_kT, hb + 1)
                    for st in range(NS):
                        af(kT[:, st], ps[:, 5 + st], ACT.Copy).then_inc(s_kTsb, 1)
                if (j, u) == (3, 1):
                    for i in range(3):
                        act.wait_ge(s_sub, 3 * hb + i + 1)
                        af(pr[:, i], pr[:, i], ACT.Exp).then_inc(s_prob, 1)
                if (j, u) == (3, 6):
                    act.wait_ge(s_pT, hb + 1)
                    if hb >= 1:
                        act.wait_ge(s_pv, hb)
                    for i in range(3):
                        af(pT[:, i], ps[:, 5 + i], ACT.Copy).then_inc(s_pTsb, 1)

            def s5_transposed(w):
                act.wait_ge(s_zero, 1)
                for i in range(4):
                    act.wait_ge(s_uT, 4 * w + i + 1)
                    if i == 0 and w >= 2:
                        act.wait_ge(s_y, 4 * (w - 1))
                    if i == 1 and w >= 1:
                        act.wait_ge(s_S, NR * w)
                    for e in range(2):
                        h = slice(e * M2, (e + 1) * M2)
                        dst = utf[h, w % 2] if i % 2 == 0 else utr[h]
                        dst = dst.rearrange("p (g v) m -> p v g m", g=2)[:, 4 * (i // 2):4 * (i // 2) + 4, :, h]
                        af(dst, ps[h, 5 + i % 2].rearrange("p (v g m) -> p v g m", v=4, g=2), ACT.Copy).then_inc(s_uTsb, 1)

            def s5_sums(w):
                def sums(r):
                    n = NR * w + r
                    act.wait_ge(s_S, n + 1)
                    if n >= 2:
                        act.wait_ge(s_ST, n // 2)
                    af(ss[:, r % 2], ps[:, (4, 7)[n % 2], 0:2 * P], ACT.Copy).then_inc(s_Ssb, 1)

                sums(0)
                sums(1)
                if w >= 2:
                    act.wait_ge(s_hy, 2 * (w - 1))
                    act.wait_ge(s_hyf, 2 * (w - 1))
                for g in range(NR // 2):
                    n = NR // 2 * w + g
                    act.wait_ge(s_ST, n + 1)
                    dst = sb[:, w % 2, 1:NCH + 1, :, 8 * g:8 * g + 8].rearrange("p k i x -> p i x k")
                    af(dst, ps[:, n % 2].rearrange("p (i x k) -> p i x k", i=2, k=NCH), ACT.Copy).then_inc(s_STsb, 1)
                    if g + 1 < NR // 2:
                        sums(2 * g + 2)
                        sums(2 * g + 3)

            def s5_outputs(w):
                act.wait_ge(s_scan, w + 1)
                act.wait_ge(s_wused, UB * B_GLU)
                src = sb[:, w % 2].rearrange("p k i x -> p i x k")
                for ri in range(2):
                    af(hy[S5P:P, ri], src[S5P:P, ri, :, 0:NCH][:, :, ::-1], ACT.Copy).then_inc(s_hy, 1)
                if w >= 1:
                    act.wait_ge(s_yout, 32 * w)
                for q in range(4):
                    n = 4 * w + q
                    act.wait_ge(s_y, n + 1)
                    for e in range(2):
                        h = slice(e * M2, (e + 1) * M2)
                        src_y = ps[h, 2 + n % 2].rearrange("p (r e t c) -> p e t r c", r=4, e=2, t=CH)[:, e]
                        dst = ys[h, :, 64 * q:64 * q + 64].rearrange("p t (r c) -> p t r c", r=4)
                        last = af(dst, src_y, ACT.Gelu_apprx_tanh)
                    last.then_inc(s_ysb, 1)

            for k in range(-4, NU):
                if k + 4 < NU and not 0 <= k + 4 - UB * B_GLU < 4:
                    split(k + 4)
                b, u = k // UB, k % UB
                if k >= 0 and u == 0 and ada_beside(b - 1) is not None:
                    a = ada_beside(b - 1)
                    act.wait_ge(s_ada1, NCK * ada_order(b))
                    if ada_order(b) > 2:
                        act.wait_ge(s_adafin, fins(b - 1))
                    af(adasb[:, a % 2], ps[:, 4], ACT.Copy).then_inc(s_adasb, 1)
                if 0 <= b < B_OUT0:
                    attention(b // 4, b % 4, u)
                if (b, u) == S5_U0:
                    s5_transposed(0)
                if u == UB - 1:
                    if 0 <= b < B_GLU and not B_OUT0 <= b < B_IN1:
                        act.wait_ge(s_wused, UB * (b + 1))
                    if 0 <= b < B_OUT0:
                        evacuate_in0(b)
                    if B_IN1 <= b < B_IN1 + NW:
                        w = b - B_IN1
                        if w >= 2:
                            act.wait_ge(s_ubout[w % 2], 32 * (w // 2))
                        for st in range(NS):
                            af(ub[:, w % 2, st], ps[:, 2 * (b % 2) + st], ACT.Copy).then_inc(s_evA, 1)
                    if B_IN1 + NW <= b < B_GLU:
                        c0 = (b - B_IN1 - NW) * BN
                        for st in range(NS):
                            af(WA[:, st, c0:c0 + BN], ps[:, 2 * (b % 2) + st], ACT.Silu).then_inc(s_evA, 1)
                    if b == B_IN1 - 1:
                        act.wait_ge(s_x2, 1)
                        square_sums(1, X, WA)
                        act.wait_ge(s_stat, 5)
                        scale_rows(1, X, WA)
                    if b == B_GLU - 1:
                        s5_sums(0)
                        s5_transposed(1)
                        s5_sums(1)
                        for w in range(NW):
                            s5_outputs(w)
                            if w + 2 < NW:
                                s5_transposed(w + 2)
                                s5_sums(w + 2)
                        act.wait_ge(s_fsT, 1)
                        af(fso[:].rearrange("p i c -> p (i c)"), ps[:, 4, 0:2 * P], ACT.Copy).then_inc(s_fso, 1)
                        for j in range(4):
                            split(UB * B_GLU + j)
                    if B_GLU <= b < B_OUT1:
                        for st in range(NS):
                            n = NS * (b - B_GLU) + st
                            act.wait_ge(s_evV, NS * (B_IN1 - B_OUT0) + n + 1)
                            if n >= 2:
                                act.wait_ge(s_g, n - 1)
                            af(tg[:, 2 + st], tg[:, st], ACT.Sigmoid).then_inc(s_gsig, 1)
                    if b + 1 in STAGES:
                        stage(STAGES.index(b + 1))
            act.wait_ge(s_x2, 2)
            square_sums(2, X, WA)
            act.wait_ge(s_stat, 8)
            scale_rows(2, X, WA)

        @block.vector
        def _(dve):
            seq = chain(dve, s_dve)
            tt = nc.vector.tensor_tensor
            ts = nc.vector.tensor_scalar
            nc.vector.memset(cT32[:], 0.0).then_inc(s_cz, 1)
            nc.vector.memset(apw[:, 0, 0], 1.0)
            seq(nc.vector.memset(apw[:, 1, 0], 0.0))
            ldt, are, aim, dt, xr, mag, th, kk, rr, sn, sh_, t0, t1, t2, f_re, f_im, den = [tmp[:, i] for i in range(17)]

            dve.wait_ge(s_exp, 1)
            tt(xr, are, dt, ALU.mult)
            seq(tt(th, aim, dt, ALU.mult))
            seq(ts(kk, th, 1.0 / (2 * math.pi), ROUND, ALU.mult, ALU.add))
            seq(ts(kk, kk, -ROUND, None, ALU.add))
            seq(nc.vector.scalar_tensor_tensor(rr, kk, -TWO_PI_HI, th, ALU.mult, ALU.add))
            seq(nc.vector.scalar_tensor_tensor(rr, kk, -TWO_PI_LO, rr, ALU.mult, ALU.add))
            ts(rr, rr, 3.1415925, -3.1415925, ALU.min, ALU.max).then_inc(s_ang, 1)

            def mean_squares(i, first):
                dve.wait_ge(s_stat, first)
                ts(stat[:, 8 * i + 2:8 * i + 4], stat[:, 8 * i:8 * i + 2], 1.0 / D, EPS, ALU.mult, ALU.add).then_inc(s_rstd, 1)
                dve.wait_ge(s_stat, first + 1)
                nc.vector.reciprocal(stat[:, 8 * i + 6:8 * i + 8], stat[:, 8 * i + 4:8 * i + 6]).then_inc(s_rstd, 1)

            dve.wait_ge(s_mag, 1)
            seq(tt(t0, sh_, sh_, ALU.mult))
            seq(ts(t0, t0, -2.0, 1.0, ALU.mult, ALU.add))
            tt(apw[:, 0, 1], mag, t0, ALU.mult)
            seq(tt(apw[:, 1, 1], mag, sn, ALU.mult))
            for i, j in ((1, 1), (2, 1), (2, 2)):
                tt(t0, apw[:, 0, i], apw[:, 0, j], ALU.mult)
                tt(t1, apw[:, 1, i], apw[:, 1, j], ALU.mult)
                tt(t2, apw[:, 0, i], apw[:, 1, j], ALU.mult)
                seq(tt(den, apw[:, 1, i], apw[:, 0, j], ALU.mult))
                tt(apw[:, 0, i + j], t0, t1, ALU.subtract)
                last = tt(apw[:, 1, i + j], t2, den, ALU.add)
                if i + j < CH:
                    seq(last)
            last.then_inc(s_pow, 1)
            dve.wait_ge(s_pow, 1)
            tt(t0, are, are, ALU.mult)
            seq(tt(t1, aim, aim, ALU.mult))
            seq(tt(den, t0, t1, ALU.add))
            seq(nc.vector.reciprocal(den, den))
            seq(ts(t2, apw[:, 0, 1], -1.0, None, ALU.add))
            tt(f_re, t2, are, ALU.mult)
            seq(tt(t0, apw[:, 1, 1], aim, ALU.mult))
            seq(tt(f_re, f_re, t0, ALU.add))
            seq(tt(f_re, f_re, den, ALU.mult))
            tt(f_im, apw[:, 1, 1], are, ALU.mult)
            seq(tt(t0, t2, aim, ALU.mult))
            seq(tt(f_im, f_im, t0, ALU.subtract))
            seq(tt(f_im, f_im, den, ALU.mult))
            dve.wait_ge(s_par, 16 * 5)
            m1g = m1[:].rearrange("p (g c) -> p g c", c=S5C)
            m2g = m2[:].rearrange("p (g c) -> p g c", c=S5C)

            def times(out, f, v):
                return tt(out, f.unsqueeze(2).to_broadcast([P, S5G, S5C]), v, ALU.mult)

            times(m1g, f_re, bre[:])
            seq(times(m2g, f_im, bim[:]))
            seq(tt(bb[:, 0], m1g, m2g, ALU.subtract))
            times(m1g, f_re, bim[:])
            seq(times(m2g, f_im, bre[:]))
            tt(bb[:, 1], m1g, m2g, ALU.add).then_inc(s_bbm, 1)
            dve.wait_ge(s_bbm, 1)
            dve.wait_ge(s_pbpy, 1)

            def table(out, pw, v_re, v_im, w, im_sign, done):
                gs = slice(w * GW, (w + 1) * GW)

                def prod(dst, a, v):
                    return tt(dst[:].rearrange("p (g t c) -> p g t c", t=CH, c=S5C),
                              a[:, :, gs].rearrange("p t g -> p g t").unsqueeze(3).to_broadcast([P, GW, CH, S5C]),
                              v[:, gs].unsqueeze(2).to_broadcast([P, GW, CH, S5C]), ALU.mult)

                def shaped(x):
                    return x[:].rearrange("p (e r t c) -> p e r (t c)", e=2, t=CH, c=S5C)
                prod(m1, pw[:, 0], v_re)
                seq(prod(m2, pw[:, 1], v_im))
                seq(tt(out[0], shaped(m1), shaped(m2), ALU.subtract))
                prod(m1, pw[:, 0], v_im)
                seq(prod(m2, pw[:, 1], v_re))
                if im_sign > 0:
                    last = tt(out[1], shaped(m1), shaped(m2), ALU.add)
                else:
                    last = nc.vector.scalar_tensor_tensor(out[1], shaped(m1), -1.0, shaped(m2), ALU.mult, ALU.subtract)
                last.then_inc(done, 1)
                dve.wait_ge(done, w + 1)

            def add_diagonals(w):
                for q in range(4):
                    n = 4 * w + q
                    dve.wait_ge(s_bandsb, n + 1)
                    diag = bands[:, q, :, CH - 1]
                    back = ps[:, (7, 3)[n % 2], P:2 * P].rearrange("p (e k c) -> p e k c", e=2, c=S5C)[:, :, CH - 1]
                    seq(tt(diag, diag, back, ALU.add))
                    tt(diag, diag, dm[:, n], ALU.add).then_inc(s_bandd, 1)

            for w in range(NW):
                if w >= 1:
                    dve.wait_ge(s_btT, NR // 2 * w)
                table([bt[:, ri].rearrange("p r e k -> p e r k") for ri in range(2)], pb, bb[:, 0], bb[:, 1], w, 1, s_btm)
                if w >= 1:
                    add_diagonals(w - 1)
                    if w == 1:
                        mean_squares(0, 2)
                    dve.wait_ge(s_ctout, 32 * w)
                    dve.wait_ge(s_band, 4 * w)
                table([ce[:, ri, :, 1:CH + 1].rearrange("p (e r) j c -> p e r (j c)", e=2) for ri in range(2)],
                      py, cre, cim, w, -1, s_ctm)
            add_diagonals(NW - 1)

            def shift_or_scale(src, lay, a0, kt0, nk, done):
                nb = (nk + 3) // 4
                for isc in range(2):
                    a = a0 + 4 * isc
                    if src[isc] is None:
                        continue
                    val = src[isc]
                    bias = bT[:, a:a + nb].rearrange("p a i -> p (a i)").unsqueeze(2).to_broadcast([P, nk, NS])
                    if isc == 0:
                        last = tt(shT[:, lay, kt0:kt0 + nk], val, bias, ALU.add)
                    else:
                        t = modt[:, 0:nk * NS].rearrange("p (k s) -> p k s", s=NS)
                        seq(tt(t, val, bias, ALU.add))
                        gain = gT[:, lay, kt0:kt0 + nk].unsqueeze(2).to_broadcast([P, nk, NS])
                        last = nc.vector.scalar_tensor_tensor(gsT[:, lay, kt0:kt0 + nk], t, 1.0, gain, ALU.add, ALU.mult)
                last.then_inc(done, 1)

            dve.wait_ge(s_adaE, 1)
            cols = [ps[:, 0, 32 * i:32 * i + 32].rearrange("p (k s) -> p k s", s=NS) for i in range(2)]
            shift_or_scale(cols, 0, 0, 0, KT, s_adaEout)
            dve.wait_ge(s_adaEout, 1)

            def split(k):
                g = k // 2
                if k == 0:
                    dve.wait_ge(s_btT, NW * NR // 2)
                dve.wait_ge(s_hi, k + 1)
                if k >= 4:
                    dve.wait_ge(s_wused, k - 3)
                src = raw[:, g % 4, (k % 2) * 2 * BN:(k % 2 + 1) * 2 * BN]
                tt(wlo[:, k % 4].rearrange("p k c -> p (k c)"), src,
                   whi[:, k % 4].rearrange("p k c -> p (k c)").bitcast(F32), ALU.subtract).then_inc(s_lo, 1)

            def stage(i):
                if i == 0:
                    dve.wait_ge(s_band, 4 * NW)
                    dve.wait_ge(s_ctout, 32 * NW)
                lay = i // 2

                def affine(g):
                    n = TG * i + g
                    dve.wait_ge(s_tp, n + 1)
                    for k in range(2):
                        for st in range(NS):
                            kt = 2 * g + k
                            x = ps[:, 5 + n % 3, (2 * k + st) * P:(2 * k + st + 1) * P]
                            last = ts(x, x, gsT[:, lay, kt, st:st + 1], shT[:, lay, kt, st:st + 1], ALU.mult, ALU.add)
                    last.then_inc(s_taff, 1)

                def low(g):
                    n = TG * i + g
                    dve.wait_ge(s_xhi, n + 1)
                    tt(xlo[:, 2 * g:2 * g + 2].rearrange("p k s c -> p (k s c)"), ps[:, 5 + n % 3],
                       xhi[:, 2 * g:2 * g + 2].rearrange("p k s c -> p (k s c)").bitcast(F32), ALU.subtract).then_inc(s_xlo, 1)

                if i in (0, 2):
                    affine(0)
                    for g in range(TG):
                        if g + 1 < TG:
                            affine(g + 1)
                        low(g)
                else:
                    for g in range(TG):
                        low(g)

            def by_head(x):
                return x.rearrange("p (h c) -> p h c", h=HB)

            def over_keys(x):
                return x.unsqueeze(2).to_broadcast([P, HB, P])

            def attention(hb, j, u):
                if (j, u) == (3, 0):
                    dve.wait_ge(s_sc, hb + 1)
                    if hb >= 1:
                        dve.wait_ge(s_pT, hb)
                    tr_ = nc.vector.tensor_reduce
                    tr_(asm[:, 0], by_head(ps[:, 5]), AX, ALU.max)
                    seq(tr_(asm[:, 2], by_head(ps[:, 7]), AX, ALU.max))
                    tt(by_head(pr[:, 0]), by_head(ps[:, 5]), over_keys(asm[:, 0]), ALU.subtract).then_inc(s_sub, 1)
                    seq(tt(pr[:, 1], ps[:, 6], bias_b[:], ALU.add))
                    seq(tr_(asm[:, 1], by_head(pr[:, 1]), AX, ALU.max))
                    seq(tt(asm[:, 3], asm[:, 1], asm[:, 2], ALU.max))
                    tt(by_head(pr[:, 1]), by_head(pr[:, 1]), over_keys(asm[:, 3]), ALU.subtract).then_inc(s_sub, 1)
                    tt(by_head(pr[:, 2]), by_head(ps[:, 7]), over_keys(asm[:, 3]), ALU.subtract).then_inc(s_sub, 1)
                if (j, u) == (3, 2):
                    dve.wait_ge(s_prob, 3 * (hb + 1))
                    for i in range(3):
                        last = nc.vector.tensor_reduce(asm[:, 4 + i], by_head(pr[:, i]), AX, ALU.add)
                    seq(last)
                    seq(tt(asm[:, 5], asm[:, 5], asm[:, 6], ALU.add))
                    seq(nc.vector.reciprocal(asm[:, 8:10], asm[:, 4:6]))
                if (j, u) == (3, 7):
                    dve.wait_ge(s_pv, hb + 1)
                    wait_evacuated(dve, 4 * hb + 3)
                    if hb >= 1:
                        dve.wait_ge(s_og, 2 * hb)
                    for st in range(NS):
                        seq(tt(by_head(tmo[:, st]), by_head(ps[:, 5 + st]), over_keys(asm[:, 8 + st]), ALU.mult))
                        tt(WA[:, st, hb * BN:(hb + 1) * BN], tmo[:, st], qkvz[:, 3, st], ALU.mult).then_inc(s_og, 1)

            def modulation(b, u):
                a0 = ada_beside(b - 1)
                if a0 is None or not (u == 3 or u == 5 and is_gate(a0)):
                    return
                part = (u - 3) // 2
                dve.wait_ge(s_adafin, fins(b - 1) + part + 1)
                i = a0 % 4
                if is_gate(a0):
                    dve.wait_ge(s_bg, 16 * (4 * (a0 // 12) + i + 1))
                    if a0 >= 12:
                        wait_evacuated(dve, b - 1)
                    tt(gate[:, part, i * BN:(i + 1) * BN], ps[:, 7], bgate[:], ALU.add).then_inc(s_adaout, 1)
                else:
                    val = ps[:, 7, 0:4 * NS].rearrange("p (k s) -> p k s", s=NS)
                    scale = a0 % 12 >= 4
                    shift_or_scale((None, val) if scale else (val, None), a0 // 12, a0 - 4 * scale, 4 * i, 4, s_adaout)

            def residual(b, lay, buf):
                c0 = b % 4 * BN
                dve.wait_ge(s_wused, UB * (b + 1))
                for st in range(NS):
                    tt(buf[:, st], ps[:, 2 * (b % 2) + st], gate[:, st, c0:c0 + BN], ALU.mult).then_inc(s_evV, 1)
                wait_evacuated(dve, b)
                for st in range(NS):
                    last = tt(X[:, st, c0:c0 + BN], X[:, st, c0:c0 + BN], buf[:, st], ALU.add)
                if b % 4 == 3:
                    last.then_inc(s_x2, 1)
                else:
                    seq(last)

            def scan(w):
                dve.wait_ge(s_h0, 16)
                dve.wait_ge(s_wused, UB * B_GLU)
                if w >= 2:
                    dve.wait_ge(s_hy, 2 * (w - 1))
                    dve.wait_ge(s_hyf, 2 * (w - 1))
                seq(nc.vector.tensor_copy(sb[:, w % 2, 0], h0[:, w]))
                dve.wait_ge(s_STsb, 8 * (w + 1))
                for k in range(NCH):
                    now, nxt = sb[:, w % 2, k], sb[:, w % 2, k + 1]
                    seq(tt(t12[:], coef[:, w], now.unsqueeze(2).to_broadcast([P, 2, 2, 2 * GW]), ALU.mult))
                    seq(tt(nxt, nxt, t12[:, 0], ALU.add))
                    seq(tt(nxt, nxt, t12[:, 1], ALU.add))
                fin = sb[:, w % 2, NCH].rearrange("p i (r e s) -> p i e r s", e=2, s=NS)
                for e in range(2):
                    g0 = w * GW + e * NR
                    last = nc.vector.tensor_copy(fs[:, :, g0:g0 + NR], fin[:, :, e, :, 0])
                last.then_inc(s_scan, 1)

            for k in range(-4, NU):
                if k + 4 < NU and not 0 <= k + 4 - UB * B_GLU < 4:
                    split(k + 4)
                b, u = k // UB, k % UB
                if k >= 0:
                    modulation(b, u)
                if k == UB * B_GLU:
                    wait_evacuated(dve, B_GLU - 1)
                    dve.wait_ge(s_yin, 32)
                    for st in range(NS):
                        last = tt(WA[:, st], WA[:, st], Y[:, st], ALU.mult)
                    seq(last)
                if 0 <= b < B_OUT0:
                    attention(b // 4, b % 4, u)
                if u == UB - 1:
                    if B_OUT0 <= b < B_IN1:
                        if b == B_OUT0:
                            dve.wait_ge(s_x2in, 32)
                        residual(b, 0, pr)
                    if b == B_IN1 - 1:
                        mean_squares(1, 5)
                    if b == B_GLU - 1:
                        for w in range(NW):
                            scan(w)
                        for j in range(4):
                            split(UB * B_GLU + j)
                    if B_GLU <= b < B_OUT1:
                        c0 = (b - B_GLU) * BN
                        dve.wait_ge(s_wused, UB * (b + 1))
                        dve.wait_ge(s_vec, 32)
                        for st in range(NS):
                            n = NS * (b - B_GLU) + st
                            if n >= 2:
                                dve.wait_ge(s_gsig, n - 1)
                            tt(tg[:, st], ps[:, 2 * (b % 2) + st], bglu[:, c0:c0 + BN], ALU.add).then_inc(s_evV, 1)
                        for st in range(NS):
                            n = NS * (b - B_GLU) + st
                            dve.wait_ge(s_gsig, n + 1)
                            g_ = WA[:, st, c0:c0 + BN]
                            tt(g_, g_, tg[:, 2 + st], ALU.mult).then_inc(s_g, 1)
                    if b >= B_OUT1:
                        residual(b, 1, tg)
                    if b + 1 in STAGES:
                        stage(STAGES.index(b + 1))
            mean_squares(2, 8)
            for st in range(NS):
                dve.wait_ge(s_xn, 5 + st)
                tt(X[:, st], WA[:, st], gfin[:], ALU.mult).then_inc(s_fin, 1)


_OUTS = {"y": (NS, P, D), "new_k": (P, D), "new_v": (P, D), "new_state": (2, 2, S5G, S5P)}


def _blocks(w):
    n = w.shape[1] // BN
    v = w.reshape(NCK, CK, P, n, BN).transpose(3, 2, 0, 1, 4)
    return v.reshape(n, P, NCK, CK * BN)


def _lay_out(i):
    f = np.float32
    w_in0 = _blocks(i["l0_w_in"]).reshape(4, 4, P, NCK, CK * BN).transpose(1, 0, 2, 3, 4).reshape(16, P, NCK, CK * BN)
    out = {
        "x": np.stack([i["x_prompt"][0], i["x_sample"][0]]),
        "w": np.concatenate([w_in0, _blocks(i["l0_w_out"]), _blocks(i["l1_w_in"]), _blocks(i["l1_w_glu"]),
                             _blocks(i["l1_w_out"])]),
        "wada": np.concatenate([_blocks(i["l0_w_ada"]), _blocks(i["l1_w_ada"])]),
        "condT": np.stack([i["c_ctx"], i["c"][0]]).reshape(NS, KT, P).transpose(2, 1, 0),
        "gT": np.stack([i["l0_norm_g"], i["l1_norm_g"]]).reshape(2, KT, P).transpose(2, 0, 1),
        "bT": np.stack([i["l0_b_ada"], i["l1_b_ada"]]).reshape(24, 4, P).transpose(2, 0, 1),
        "bgate": np.concatenate([i["l0_b_ada"][2 * D:], i["l1_b_ada"][2 * D:]]).reshape(8, BN),
        "b_glu": i["l1_b_glu"],
        "g_fin": i["final_norm_g"],
        "ident": np.eye(P, dtype=f),
        "kcT": i["cache_l0_k"][0].reshape(P, 4, HB, P).transpose(1, 3, 2, 0).reshape(4, P, BN),
        "vc": i["cache_l0_v"][0].reshape(P, 4, BN).transpose(1, 0, 2),
        "are": i["l1_a_re"].transpose(0, 2, 1).reshape(P, S5G),
        "aim": i["l1_a_im"].transpose(0, 2, 1).reshape(P, S5G),
        "ldt": np.repeat(i["l1_log_dt"][:, None], S5P, axis=1).reshape(P, S5G),
        "bre": i["l1_b_re"].transpose(0, 2, 1, 3).reshape(P, S5G, S5C),
        "bim": i["l1_b_im"].transpose(0, 2, 1, 3).reshape(P, S5G, S5C),
        "cre": i["l1_c_re"].transpose(0, 3, 1, 2).reshape(P, S5G, S5C),
        "cim": i["l1_c_im"].transpose(0, 3, 1, 2).reshape(P, S5G, S5C),
    }
    rows = np.arange(P)
    perm = np.zeros((P, P), f)
    perm[rows, rows // NCH * NCH + NCH - 1 - rows % NCH] = 1.0
    out["perm"] = perm
    sel2 = np.zeros((P, NS), f)
    sel2[rows[rows % 32 < NS], rows[rows % 32 < NS] % 32] = 1.0
    out["sel2"] = sel2
    out["selbc"] = np.repeat(sel2[:, :, None], P, axis=2)
    q, k = rows[:, None], rows[None, :]
    dr = k // GRID_W - q // GRID_W + NA_ROWS - 1
    dc = np.clip(k % GRID_W - q % GRID_W + NA_COLS - 1, 0, 2 * NA_COLS - 2)
    c0 = np.clip(q % GRID_W - NA_COLS // 2, 0, GRID_W - NA_COLS)
    ok = (k % GRID_W >= c0) & (k % GRID_W < c0 + NA_COLS)
    bias = np.where(ok[None], i["l0_rpb"][:, dr, dc], f(NEG))
    out["bias"] = bias.reshape(4, HB, P, P).transpose(0, 2, 1, 3).reshape(4, P, BN)
    skip = i["l1_d"].reshape(NW, 2, 4, 4, S5C)
    dm = np.zeros((4, 2, S5C, NW, 4, 2, S5C), f)
    for e in range(2):
        for c in range(S5C):
            dm[:, e, c, :, :, e, c] = skip[:, e, :, :, c].transpose(2, 0, 1)
    out["dm"] = dm.reshape(P, NR, 2, S5C)
    st = i["state_l1_s5"][0].reshape(2, 2, NW, 2, NR, S5P)
    h0 = np.zeros((2, S5P, NW, 2, NR, 2, NS), f)
    h0[..., 1] = st.transpose(0, 5, 2, 1, 4, 3)
    out["h0"] = h0.reshape(P, NW, 2, 2 * GW)
    return {name: np.ascontiguousarray(a) for name, a in out.items()}


def kernel(**inputs):
    import concourse.bacc as bacc
    from concourse.bass_utils import run_bass_kernel_spmd

    arrays = _lay_out({name: np.asarray(a) for name, a in inputs.items()})
    nc = bacc.Bacc("TRN2", target_bir_lowering=False, num_devices=1)
    d = {name: nc.dram_tensor("in_" + name, a.shape, mybir.dt.from_np(a.dtype), kind="ExternalInput").ap()
         for name, a in arrays.items()}
    for name, shape in _OUTS.items():
        d[name] = nc.dram_tensor("out_" + name, shape, F32, kind="ExternalOutput").ap()
    build(nc, d)
    r = run_bass_kernel_spmd(nc, [{"in_" + name: a for name, a in arrays.items()}], core_ids=[0]).results[0]
    y = r["out_y"]
    return (y[0:1], y[1:2], r["out_new_k"].reshape(1, P, NH, P), r["out_new_v"].reshape(1, P, NH, P),
            r["out_new_state"].reshape(1, 2, 2, S5G, S5P))
```

```python
import math
from contextlib import ExitStack

import concourse.bass as bass
from concourse import mybir
import numpy as np

F32 = mybir.dt.float32
F32R = mybir.dt.float32r
ALU = mybir.AluOpType
ACT = mybir.ActivationFunctionType
AX = mybir.AxisListType.X

P = 128
D = 2048
KT = D // P
NS = 2
BN = 512
CK = 4
NCK = KT // CK
NH = 16
HB = BN // P
EPS = 1e-6
QSCALE = float(P) ** -0.5
GRID_W, NA_COLS, NA_ROWS = 64, 16, 8
NEG = -1e30
S5G, S5P, S5C = 128, 64, 16
CH = 4
NCH = P // CH
M2 = NS * NCH
NW = 4
NR = 16
GW = 2 * NR
NDL = 2 * CH - 1

B_IN0, B_OUT0, B_IN1, B_GLU, B_OUT1, B_END = 0, 16, 20, 28, 32, 36
A_EARLY = 8


UB = 2 * NCK
NU = B_END * UB
TG = KT // 2
STAGES = (B_IN0, B_OUT0, B_IN1, B_GLU, B_OUT1)


EARLY = (("ada", 0), ("ada", 1), ("ada", 2), ("ada", 3), ("b", 0), ("ada", 4), ("band", 0), ("ada", 5), ("b", 1),
         ("ada", 6), ("ada", 7), ("band", 1), ("b", 2), ("band", 2), ("b", 3), ("band", 3))
ROUND = 1.5 * 2.0 ** 23
TWO_PI_HI = 6.28125
TWO_PI_LO = 2 * math.pi - TWO_PI_HI


def ada_beside(b):
    if 0 <= b < 12:
        return 8 + b
    if B_OUT0 <= b < B_OUT0 + 4:
        return 20 + b - B_OUT0
    return None


S5_BESIDE = (("u", 0, UB * 22 + 1, 2), ("S", 0, UB * 22 + 3, 9), ("u", 1, UB * 23 + 4, 2), ("S", 1, UB * 23 + 6, 9),
             ("u", 2, UB * 25 + 2, 2))
SCAN_FROM = (UB * 23 + 4, UB * 24 + 7)
SCAN_LAG = 16


def s5_beside(k):
    return next(((step, w, k - first) for step, w, first, n in S5_BESIDE if first <= k < first + n), (None, 0, 0))


def is_gate(a):
    return a % 12 >= 8


def fins(b):
    return sum(1 + is_gate(ada_beside(x)) for x in range(b) if ada_beside(x) is not None)


def ada_order(b):
    return sum(ada_beside(x) is not None for x in range(b))



def build(nc, d):
    with ExitStack() as ctx:
        K = 1024

        def at(name, shape, off, dt=F32):
            return nc.alloc_sbuf_tensor_at(name, shape, dt, offset=16512 + off)

        def sem(name):
            return ctx.enter_context(nc.semaphore(name))

        raw = at("raw", [P, 4, CK * BN], 0)
        whi = at("whi", [P, 4, 2, BN], 32 * K, F32R)
        wlo = at("wlo", [P, 4, 2, BN], 48 * K, F32R)
        araw = at("araw", [P, 2, CK * BN], 64 * K)
        xhi = at("xhi", [P, KT, NS, P], 80 * K, F32R)
        xlo = at("xlo", [P, KT, NS, P], 96 * K, F32R)
        X = at("X", [P, NS, D], 112 * K)
        gate = at("gate", [P, NS, D], 128 * K)
        WA = at("WA", [P, NS, D], 144 * K)
        m = 160 * K
        ident = at("ident", [P, P], m)
        perm = at("perm", [P, P], m + 512)
        selbc = at("selbc", [P, NS, P], m + K)
        coef = at("coef", [P, NW, 2, 2, 2 * GW], m + 2 * K)
        sel2 = at("sel2", [P, NS], m + 6 * K)
        bT = at("bT", [P, 24, 4], m + 6 * K + 64)
        gT = at("gT", [P, 2, KT], m + 6 * K + 512)
        shT = at("shT", [P, 2, KT, NS], m + 6 * K + 768)
        gsT = at("gsT", [P, 2, KT, NS], m + 7 * K + 256)
        condT = at("condT", [P, KT, NS], m + 7 * K + 512)
        stat = at("stat", [P, 32], m + 7 * K + 640)
        modt = at("modt", [P, 64], m + 7 * K + 768)
        cT32 = at("cT32", [P, KT, 32], m + 8 * K)
        adasb = at("adasb", [P, 2, BN], m + 10 * K)
        bgate = at("bgate", [P, BN], m + 14 * K)
        ar = 176 * K
        qkvz = at("qkvz", [P, 4, NS, BN], 112 * K)
        qT = at("qT", [P, NS, BN], ar)
        kT = at("kT", [P, NS, BN], ar + 4 * K)
        pr = at("pr", [P, 3, BN], ar + 8 * K)
        pT = at("pT", [P, 3, BN], ar + 14 * K)
        bias_b = at("bias_b", [P, BN], ar + 20 * K)
        kc_b = at("kc_b", [P, BN], ar + 22 * K)
        vc_b = at("vc_b", [P, BN], ar + 24 * K)
        asm = at("asm", [P, 16, HB], ar + 26 * K)
        tmo = at("tmo", [P, 2, BN], ar + 27 * K)
        cre = at("cre", [P, S5G, S5C], 32 * K)
        cim = at("cim", [P, S5G, S5C], 40 * K)
        bre = at("bre", [P, S5G, S5C], 48 * K)
        bim = at("bim", [P, S5G, S5C], 56 * K)
        bt = at("bt", [P, 2, NR, 2, CH * S5C], 48 * K)
        bb = at("bb", [P, 2, S5G, S5C], 64 * K)
        m1 = at("m1", [P, GW * CH * S5C], 80 * K)
        m2 = at("m2", [P, GW * CH * S5C], 88 * K)
        ce = at("ce", [P, 2, GW, CH + 2, S5C], 96 * K)
        bbf = at("bbf", [P, 2, NR, 2, S5C], 120 * K)
        bbb = at("bbb", [P, 2, NR, 2, S5C], 124 * K)
        bs = at("bs", [P, NR, 2, P], ar)
        bands = at("bands", [P, 4, 2, NDL, S5C], ar + 16 * K)
        pb = at("pb", [P, 2, CH, S5G], ar + 20 * K)
        py = at("py", [P, 2, CH, S5G], ar + 24 * K)
        dm = at("dm", [P, NR, 2, S5C], ar + 28 * K)
        tmp = at("tmp", [P, 18, S5G], ar)
        apw = at("apw", [P, 2, CH + 1, S5G], ar + 9 * K)
        btab = at("btab", [P, 2, NR, 2, P], 0)
        bth = at("bth", [P, 2, NR // 2, 2, P], 64 * K)
        ctab = at("ctab", [P, 2, GW, CH * S5C], 32 * K)
        kd = at("kd", [P, NR, P], 48 * K)
        hy = at("hy", [P, 2, 2, 2 * GW, NCH], 80 * K)
        sb = at("sb", [P, 2, NCH, 2, 2 * GW], 112 * K)
        ub = at("ub", [P, 2, NS, BN], 152 * K)
        utf01 = at("utf01", [P, 2, NR, P], ar)
        utf23 = at("utf23", [P, 2, NR, P], 64 * K)
        utr = at("utr", [P, NR, P], m + 8 * K)
        ys = at("ys", [P, 2, CH, NR * S5C], m + 8 * K)
        u2p = at("u2p", [P, 8, 2 * CH * S5C], ar + 16 * K)
        u2 = at("u2", [P, CH, 2, P], ar + 20 * K)
        ss = at("ss", [P, 2, 2 * P], ar + 24 * K)
        h0 = at("h0", [P, NW, 2, 2 * GW], ar + 26 * K)
        fs = at("fs", [P, 2, S5G], ar + 28 * K)
        t12 = at("t12", [P, 2, 2, 2 * GW], ar + 29 * K)
        t12b = at("t12b", [P, 2, 2, 2 * GW], ar + 30 * K)
        fso = at("fso", [P, 2, P], ar + 26 * K)
        Y = at("Y", [P, NS, D], 64 * K)
        bglu = at("bglu", [P, D], ar)
        gfin = at("gfin", [P, D], ar + 8 * K)
        tg = at("tg", [P, 4, BN], ar + 16 * K)

        ps = ctx.enter_context(nc.psum_tensor("ps", [P, 8, BN], F32))

        band_d = nc.dram_tensor("band_scratch", (NW, 4, 4, 2, S5C, NDL * S5C), F32).ap()
        bt_d = nc.dram_tensor("btab_scratch", (NW, P, NR * 2 * P), F32).ap()
        ct_d = nc.dram_tensor("ctab_scratch", (NW, P, 2, GW, CH * S5C), F32).ap()
        u_d = nc.dram_tensor("u_scratch", (NS * P, D), F32).ap()
        x_keep = nc.dram_tensor("x_keep", (P, NS * D), F32).ap()
        gate_keep = nc.dram_tensor("gate_keep", (P, NS * D), F32).ap()
        y_d = nc.dram_tensor("y_scratch", (NS * P, D), F32).ap()

        s_const, s_pole, s_par, s_x = sem("const_in"), sem("poles_in"), sem("params_in"), sem("x_in")
        s_raw = [sem(f"raw_in{i}") for i in range(4)]
        s_araw = [sem(f"araw_in{i}") for i in range(2)]
        s_hi, s_lo, s_wused = sem("w_hi"), sem("w_lo"), sem("w_used")
        s_ada0, s_ada1 = sem("ada_early_used"), sem("ada_used")
        s_cz, s_cond, s_adasb = sem("cond_zero"), sem("cond_ready"), sem("ada_sb")
        s_adaE, s_adaEout = sem("ada_early_fin"), sem("ada_early_out")
        s_adafin, s_adaout, s_bg = sem("ada_fin"), sem("ada_out"), sem("bgate_in")
        s_evA, s_evV = sem("acc_evacuated_act"), sem("acc_evacuated_dve")
        s_tp, s_taff, s_xhi, s_xlo = sem("t_pe"), sem("t_affine"), sem("x_hi"), sem("x_lo")
        s_dve, s_act, s_pool = sem("dve_order"), sem("act_order"), sem("pool_order")
        s_ang, s_exp, s_pow, s_pbpy = sem("s5_angles"), sem("s5_exp"), sem("s5_powers"), sem("pb_py")
        s_btm, s_btT, s_bs, s_bsout = sem("b_table"), sem("b_tr"), sem("b_staged"), sem("b_stored")
        s_ctm, s_ends, s_bbm, s_ctout = sem("c_table"), sem("c_ends"), sem("bb_ready"), sem("c_stored")
        s_band, s_bandsb, s_bandd, s_bandout = sem("band_pe"), sem("band_sb"), sem("band_d"), sem("band_stored")
        s_attin, s_kvout = sem("att_in"), sem("kv_out")
        s_qT, s_qTsb, s_kT, s_kTsb = sem("qT_pe"), sem("qT_sb"), sem("kT_pe"), sem("kT_sb")
        s_sc, s_sub, s_prob, s_rs = sem("scores"), sem("scores_shifted"), sem("probs"), sem("row_sums")
        s_pT, s_pTsb, s_pv, s_og = sem("pT_pe"), sem("pT_sb"), sem("pv"), sem("gated_o")
        s_x2in, s_stat, s_rstd, s_xn = sem("x_again"), sem("square_sums"), sem("rstd"), sem("x_normed")
        s_ubout = [sem(f"u_stored{i}") for i in range(2)]
        s_u2, s_u2p, s_zero = sem("u2_in"), sem("u2_ordered"), sem("zeros")
        s_uT, s_uTsb = sem("uT_pe"), sem("uT_sb")
        s_bt = [sem(f"btab_in{i}") for i in range(2)]
        s_bth = [sem(f"b_half_in{i}") for i in range(2)]
        s_kept, s_back, s_kdz = sem("x_gate_kept"), sem("x_gate_back"), sem("kd_zero")
        s_hyf, s_factors = sem("hy_forward"), sem("scan_factors")
        s_ct, s_kd, s_h0 = sem("ctab_in"), sem("kd_in"), sem("h0_in")
        s_S, s_Ssb, s_ST, s_STsb = sem("S_pe"), sem("S_sb"), sem("ST_pe"), sem("ST_sb")
        s_scan, s_hy, s_y, s_ysb = sem("scan"), sem("hy"), sem("y_pe"), sem("y_sb")
        s_yout = [sem(f"y_stored{i}") for i in range(2)]
        s_fs, s_fsT, s_fso, s_yin = sem("fin_state"), sem("fin_T"), sem("fin_sb"), sem("y_in")
        s_mag = sem("s5_mag")
        s_vec, s_gsig, s_g = sem("vectors_in"), sem("glu_sig"), sem("gated_y")
        s_x2, s_fin, s_out = sem("x2"), sem("final"), sem("outputs")
        block = ctx.enter_context(nc.Block())

        def utf(w):
            return (utf01, utf23)[w // 2][:, w % 2]

        def wait_evacuated(eng, b):
            if b < B_OUT0:
                eng.wait_ge(s_evA, NS * (b + 1))
            elif b < B_IN1:
                eng.wait_ge(s_evV, NS * (b - B_OUT0 + 1))
            elif b < B_GLU:
                eng.wait_ge(s_evA, NS * (B_OUT0 + b - B_IN1 + 1))
            else:
                eng.wait_ge(s_evV, NS * (B_IN1 - B_OUT0 + b - B_GLU + 1))

        def chain(eng, s):
            n = [0]

            def mark(ins):
                n[0] += 1
                ins.then_inc(s, 1)
                eng.wait_ge(s, n[0])
            return mark

        @block.sync
        def _(sp):
            for name, dst in (("condT", condT), ("ident", ident), ("perm", perm), ("selbc", selbc),
                              ("sel2", sel2), ("bT", bT), ("gT", gT)):
                sp.dma_start(dst[:], d[name]).then_inc(s_const, 16)
            for e in range(A_EARLY * NCK):
                if e >= 4:
                    sp.wait_ge(s_ada0, e - 3)
                sp.dma_start(raw[:, e % 4], d["wada"][e // NCK, :, e % NCK]).then_inc(s_raw[e % 4], 16)
            def half_b_table(n):
                if n == 0:
                    sp.wait_ge(s_bsout, 16 * NW)
                    sp.wait_ge(s_ctout, 32 * NW)
                    sp.wait_ge(s_bandout, 128 * NW)
                    sp.wait_ge(s_ada1, NCK * ada_order(B_END))
                if n >= 2:
                    sp.wait_ge(s_S, NR // 2 * (n - 1))
                half = NR // 2 * 2 * P
                sp.dma_start(bth[:, n % 2].rearrange("p r i c -> p (r i c)"),
                             bt_d[n // 2, :, n % 2 * half:(n % 2 + 1) * half]).then_inc(s_bth[n % 2], 16)

            def load_tables():
                def b_table(w):
                    sp.dma_start(btab[:, w % 2].rearrange("p r i c -> p (r i c)"), bt_d[w]).then_inc(s_bt[w % 2], 16)

                def y_tables(w):
                    sp.dma_start(ctab[:], ct_d[w]).then_inc(s_ct, 16)
                    for e in range(2):
                        for s in range(CH):
                            p0 = e * CH * S5C + s * S5C
                            k0 = (CH - 1 - s) * S5C
                            sp.dma_start(kd[p0:p0 + S5C, :, e * 64:e * 64 + 64],
                                         band_d[w, :, :, e].rearrange("q j c k -> c (q j) k")[:, :, k0:k0 + 64]).then_inc(s_kd, 16)

                for w in (2, 3):
                    sp.wait_ge(s_lo, UB * B_GLU - 12 + 4 * w)
                    b_table(w)
                sp.wait_ge(s_kdz, 1)
                for w in range(NW):
                    if w >= 1:
                        sp.wait_ge(s_y, 4 * w)
                    y_tables(w)

            for g in range(B_END * NCK):
                b, c = g // NCK, g % NCK
                if g in (84, 85, 98, 100):
                    half_b_table((84, 85, 98, 100).index(g))
                if g == B_GLU * NCK:
                    load_tables()
                    sp.wait_ge(s_S, NR * NW)
                if g < 4:
                    sp.wait_ge(s_ada0, A_EARLY * NCK - 3 + g)
                else:
                    sp.wait_ge(s_hi, 2 * (g - 3))
                    sp.wait_ge(s_lo, 2 * (g - 3))
                sp.dma_start(raw[:, g % 4], d["w"][b, :, c]).then_inc(s_raw[g % 4], 16)
                b, c = (g - 3) // NCK, (g - 3) % NCK
                if ada_beside(b) is not None:
                    n = NCK * ada_order(b) + c
                    if n == 0:
                        sp.wait_ge(s_ends, NW)
                        sp.wait_ge(s_btm, NW)
                    if n >= 2:
                        sp.wait_ge(s_ada1, n - 1)
                    sp.dma_start(araw[:, n % 2], d["wada"][ada_beside(b), :, c]).then_inc(s_araw[n % 2], 16)

        @block.gpsimd
        def _(pool):
            seq = chain(pool, s_pool)
            for name, dst in (("ldt", tmp[:, 0]), ("are", tmp[:, 1]), ("aim", tmp[:, 2])):
                pool.dma_start(dst, d[name]).then_inc(s_pole, 16)
            for st in range(NS):
                pool.dma_start(WA[:, st], d["x"][st]).then_inc(s_x, 16)
            for name, dst in (("bre", bre), ("bim", bim), ("cre", cre), ("cim", cim), ("dm", dm)):
                pool.dma_start(dst[:], d[name]).then_inc(s_par, 16)
            seq(nc.gpsimd.memset(bbf[:], 0.0))
            seq(nc.gpsimd.memset(bbb[:], 0.0))
            pool.wait_ge(s_pow, 1)
            for w in range(NW):
                for e in range(2):
                    g0 = w * GW + e * NR
                    for src, dst, ri, sign in ((0, 0, 0, 1.0), (0, 1, 1, 1.0), (1, 0, 1, -1.0), (1, 1, 0, 1.0)):
                        o = coef[:, w, src, dst].rearrange("p (r e s) -> p r e s", e=2, s=NS)[:, :, e]
                        power = apw[:, ri, CH, g0:g0 + NR].unsqueeze(2).to_broadcast([P, NR, NS])
                        last = nc.gpsimd.tensor_scalar(o, power, sign, None, ALU.mult)
                        if (w, e, src, dst) != (NW - 1, 1, 1, 1):
                            seq(last)
            last.then_inc(s_factors, 1)
            pool.wait_ge(s_factors, 1)
            pool.wait_ge(s_par, 16 * 5)
            pool.wait_ge(s_bbm, 1)
            for w in range(NW):
                if w >= 1:
                    pool.wait_ge(s_band, 4 * w)
                    pool.wait_ge(s_ctout, 32 * w)
                for ri in range(2):
                    for e in range(2):
                        g0 = w * GW + e * NR
                        seq(nc.gpsimd.tensor_copy(bbf[0:64, ri, :, e], bb[0:64, ri, g0:g0 + NR]))
                        seq(nc.gpsimd.tensor_copy(bbb[64:128, ri, :, e], bb[64:128, ri, g0:g0 + NR]))
                gs = slice(w * GW, (w + 1) * GW)
                for j in (0, CH + 1):
                    seq(nc.gpsimd.tensor_copy(ce[:, 0, :, j], cre[:, gs]))
                    last = nc.gpsimd.tensor_scalar(ce[:, 1, :, j], cim[:, gs], -1.0, None, ALU.mult)
                    if j == 0:
                        seq(last)
                last.then_inc(s_ends, 1)
                pool.wait_ge(s_ends, w + 1)
            pool.wait_ge(s_bandout, 16 * 8 * NW)
            pool.wait_ge(s_bsout, 16 * NW)
            for hb in range(NH // HB):
                if hb >= 1:
                    pool.wait_ge(s_pv, hb)
                for name, dst in (("bias", bias_b), ("kcT", kc_b), ("vc", vc_b)):
                    pool.dma_start(dst[:], d[name][hb]).then_inc(s_attin, 16)
                if hb == 0:
                    pool.dma_start(bgate[:], d["bgate"][0].partition_broadcast(P)).then_inc(s_bg, 16)
                for i, name in ((1, "new_k"), (2, "new_v")):
                    pool.wait_ge(s_evA, NS * (4 * hb + i + 1))
                    pool.dma_start(d[name][:, hb * BN:(hb + 1) * BN], qkvz[:, i, 0]).then_inc(s_kvout, 16)
                    if hb == 0:
                        pool.wait_ge(s_adaout, 2 * i)
                        pool.dma_start(bgate[:], d["bgate"][i].partition_broadcast(P)).then_inc(s_bg, 16)
                if hb == 0:
                    pool.wait_ge(s_adaout, 6)
                    pool.dma_start(bgate[:], d["bgate"][3].partition_broadcast(P)).then_inc(s_bg, 16)
            pool.wait_ge(s_adaout, 8)
            pool.dma_start(bgate[:], d["bgate"][4].partition_broadcast(P)).then_inc(s_bg, 16)
            pool.wait_ge(s_og, 8)
            pool.wait_ge(s_kvout, 16 * 8)
            for st in range(NS):
                pool.dma_start(X[:, st], d["x"][st]).then_inc(s_x2in, 16)
            pool.dma_start(h0[:], d["h0"]).then_inc(s_h0, 16)
            for i in range(1, 4):
                pool.wait_ge(s_adaout, 16 + 2 * i)
                pool.dma_start(bgate[:], d["bgate"][4 + i].partition_broadcast(P)).then_inc(s_bg, 16)
            pool.wait_ge(s_x2, 1)
            pool.dma_start(x_keep, X[:].rearrange("p s c -> p (s c)")).then_inc(s_kept, 16)
            pool.wait_ge(s_adaout, fins(B_END))
            pool.dma_start(gate_keep, gate[:].rearrange("p s c -> p (s c)")).then_inc(s_kept, 16)
            seq(nc.gpsimd.memset(utf01[:], 0.0))
            nc.gpsimd.memset(utr[:], 0.0).then_inc(s_zero, 1)

            def store_u(w):
                wait_evacuated(pool, B_IN1 + w)
                for st in range(NS):
                    pool.dma_start(u_d[st * P:(st + 1) * P, w * BN:(w + 1) * BN], ub[:, w % 2, st]).then_inc(s_ubout[w % 2], 16)
                pool.wait_ge(s_ubout[w % 2], 32 * (w // 2 + 1))

            def load_u(w):
                for gh in range(2):
                    for e in range(2):
                        c0 = w * BN + e * 256 + gh * P
                        pool.dma_start(u2[gh * M2:(gh + 1) * M2, :, e],
                                       u_d[:, c0:c0 + P].rearrange("(m t) c -> m t c", t=CH)).then_inc(s_u2, 16)
                pool.wait_ge(s_u2, 64 * (w + 1))
                if w >= 1:
                    pool.wait_ge(s_uT, 4 * w)
                for e in range(2):
                    for t in range(CH):
                        o = u2p[:].rearrange("p v (e t c) -> p v e t c", e=2, t=CH)[:, :, e, t]
                        last = nc.gpsimd.tensor_copy(o, u2[:, t, e].rearrange("p (v c) -> p v c", c=S5C))
                        if (e, t) != (1, CH - 1):
                            seq(last)
                last.then_inc(s_u2p, 1)
                pool.wait_ge(s_u2p, w + 1)

            for w in range(NW):
                store_u(w)
                if w == 3:
                    pool.wait_ge(s_S, 2 * NR)
                    nc.gpsimd.memset(utf23[:], 0.0).then_inc(s_zero, 1)
                    pool.wait_ge(s_zero, 2)
                load_u(w)
            pool.wait_ge(s_wused, UB * B_GLU)
            nc.gpsimd.memset(kd[:], 0.0).then_inc(s_kdz, 1)
            for w in range(NW):
                pool.wait_ge(s_ysb, 4 * (w + 1))
                for e in range(2):
                    c0 = w * BN + e * 256
                    pool.dma_start(y_d[:, c0:c0 + 256].rearrange("(m t) c -> m t c", t=CH),
                                   ys[e * M2:(e + 1) * M2, w % 2]).then_inc(s_yout[w % 2], 16)
            for i in range(2):
                pool.wait_ge(s_yout[i], 32 * NW // 2)
            pool.wait_ge(s_y, 4 * NW)
            for st in range(NS):
                pool.dma_start(Y[:, st], y_d[st * P:(st + 1) * P]).then_inc(s_yin, 16)
            pool.dma_start(X[:].rearrange("p s c -> p (s c)"), x_keep).then_inc(s_back, 16)
            pool.dma_start(gate[:].rearrange("p s c -> p (s c)"), gate_keep).then_inc(s_back, 16)
            pool.dma_start(bglu[:], d["b_glu"].partition_broadcast(P)).then_inc(s_vec, 16)
            pool.dma_start(gfin[:], d["g_fin"].partition_broadcast(P)).then_inc(s_vec, 16)
            pool.wait_ge(s_fso, 1)
            for ri in range(2):
                pool.dma_start(d["new_state"][:, ri].rearrange("d g p -> g d p"),
                               fso[:, ri].rearrange("g (d p) -> g d p", d=2)).then_inc(s_out, 16)
            for st in range(NS):
                pool.wait_ge(s_fin, st + 1)
                pool.dma_start(d["y"][st], X[:, st]).then_inc(s_out, 16)
            pool.wait_ge(s_out, 64)
            pool.wait_ge(s_kvout, 128)

        @block.tensor
        def _(pe):
            mm = nc.tensor.matmul
            tr = nc.tensor.transpose

            def ada_chunk(bank, rhs, c):
                for j in range(CK):
                    last = mm(ps[32 * j:32 * j + 32, bank], cT32[:, c * CK + j], rhs[:, j * BN:(j + 1) * BN],
                              start=c == 0, stop=c == NCK - 1)
                return last

            def ada_columns(a, out):
                for i in range(4):
                    last = mm(out[:, 2 * i:2 * i + 2], adasb[:, a % 2, i * P:(i + 1) * P], sel2[:],
                              start=True, stop=True)
                return last

            pe.wait_ge(s_const, 16 * 7)
            pe.wait_ge(s_cond, 1)

            def ada_early(a):
                if a >= 2:
                    pe.wait_ge(s_adasb, a - 1)
                for c in range(NCK):
                    pe.wait_ge(s_raw[c], 16 * (a + 1))
                    last = ada_chunk(4 if a % 2 == 0 else 1, raw[:, c], c)
                    last.then_inc(s_ada0, 1)

            def b_tables(w):
                pe.wait_ge(s_btm, w + 1)
                for i in range(NR // 2):
                    n = w * 8 + i
                    if n >= 2:
                        pe.wait_ge(s_bs, n - 1)
                    for r in range(2):
                        for ri in range(2):
                            c0 = (2 * r + ri) * P
                            last = tr(ps[:, 5 + n % 2, c0:c0 + P],
                                      bt[:, ri, 2 * i + r].rearrange("p e c -> p (e c)"), ident[:])
                    last.then_inc(s_btT, 1)

            def band_products(w):
                pe.wait_ge(s_ctm, w + 1)
                pe.wait_ge(s_ends, w + 1)
                for q in range(4):
                    n = w * 4 + q
                    if n >= 2:
                        pe.wait_ge(s_bandd, n - 1)
                    for half in range(2):
                        for ri in range(2):
                            for j in range(4):
                                r = 4 * q + j
                                lhs = (bbf, bbb)[half][:, ri, r].rearrange("p e c -> p (e c)")
                                j0 = (0, 2)[half]
                                rhs = ce[:, ri].rearrange("p (e r) j c -> p e r (j c)", e=2)[
                                    :, :, r, j0 * S5C:(j0 + CH) * S5C]
                                last = mm(ps[32 * j:32 * j + 32, (7, 3)[n % 2], half * P:(half + 1) * P], lhs, rhs,
                                          start=ri == 0, stop=ri == 1)
                    last.then_inc(s_band, 1)

            for step, n in EARLY:
                if step == "ada":
                    ada_early(n)
                    pe.wait_ge(s_adasb, n + 1)
                    last = ada_columns(n, ps[:, 0, 8 * n:8 * n + 8])
                    if n == A_EARLY - 1:
                        last.then_inc(s_adaE, 1)
                elif step == "b":
                    b_tables(n)
                else:
                    band_products(n)
            pe.wait_ge(s_bandd, 16)
            pe.wait_ge(s_bs, 32)
            pe.wait_ge(s_adaEout, 1)

            def transposes(i, src):
                for g in range(TG):
                    n = TG * i + g
                    if g >= 3:
                        pe.wait_ge(s_xlo, n - 2)
                    for k in range(2):
                        for st in range(NS):
                            last = tr(ps[:, 5 + n % 3, (2 * k + st) * P:(2 * k + st + 1) * P],
                                      src[:, st, (2 * g + k) * P:(2 * g + k + 1) * P], ident[:])
                    last.then_inc(s_tp, 1)

            def unit(b, u):
                k0 = UB * b + u
                if b in STAGES:
                    pe.wait_ge(s_xlo, TG * STAGES.index(b) + u + 1)
                if u == 0 and b >= 2:
                    wait_evacuated(pe, b - 2)
                pe.wait_ge(s_lo, k0 + 1)
                s = k0 % 4
                for k in range(2):
                    kt = 2 * u + k
                    for st in range(NS):
                        acc = ps[:, 2 * (b % 2) + st]
                        mm(acc, xhi[:, kt, st], whi[:, s, k], start=kt == 0, stop=False)
                        mm(acc, xhi[:, kt, st], wlo[:, s, k], start=False, stop=False)
                        last = mm(acc, xlo[:, kt, st], whi[:, s, k], start=False, stop=kt == KT - 1)
                last.then_inc(s_wused, 1)

            def q_or_k(src, dst_bank, s):
                for st in range(NS):
                    for h in range(HB):
                        last = tr(ps[:, dst_bank + st, h * P:(h + 1) * P], src[:, st, h * P:(h + 1) * P], ident[:])
                last.then_inc(s, 1)

            def attention(hb, b, u):
                j = b % 4
                if (j, u) == (1, 3):
                    wait_evacuated(pe, 4 * hb)
                    if hb >= 1:
                        pe.wait_ge(s_og, 2 * hb)
                    q_or_k(qkvz[:, 0], 5, s_qT)
                if (j, u) == (2, 3):
                    wait_evacuated(pe, 4 * hb + 1)
                    pe.wait_ge(s_qTsb, 2 * (hb + 1))
                    q_or_k(qkvz[:, 1], 5, s_kT)
                if (j, u) == (2, 7):
                    pe.wait_ge(s_kTsb, 2 * (hb + 1))
                    pe.wait_ge(s_attin, 48 * (hb + 1))
                    pe.wait_ge(s_adaout, fins(b))
                    for h in range(HB):
                        c = slice(h * P, (h + 1) * P)
                        mm(ps[:, 5, c], qT[:, 0, c], kT[:, 0, c], start=True, stop=True)
                        mm(ps[:, 6, c], qT[:, 1, c], kT[:, 1, c], start=True, stop=True)
                        last = mm(ps[:, 7, c], qT[:, 1, c], kc_b[:, c], start=True, stop=True)
                    last.then_inc(s_sc, 1)
                if (j, u) == (3, 6):
                    pe.wait_ge(s_prob, 3 * (hb + 1))
                    pe.wait_ge(s_adaout, fins(b))
                    for i in range(3):
                        for h in range(HB):
                            c = slice(h * P, (h + 1) * P)
                            last = tr(ps[:, 5 + i, c], pr[:, i, c], ident[:])
                    last.then_inc(s_pT, 1)
                if (j, u) == (3, 7):
                    wait_evacuated(pe, 4 * hb + 2)
                    pe.wait_ge(s_pTsb, 3 * (hb + 1))
                    for h in range(HB):
                        c = slice(h * P, (h + 1) * P)
                        mm(ps[:, 5, c], pT[:, 0, c], qkvz[:, 2, 0, c], start=True, stop=True)
                        mm(ps[:, 6, c], pT[:, 1, c], qkvz[:, 2, 1, c], start=True, stop=False)
                        last = mm(ps[:, 6, c], pT[:, 2, c], vc_b[:, c], start=False, stop=True)
                    last.then_inc(s_pv, 1)

            def modulation(b, u):
                a0 = ada_beside(b - 1)
                a1 = ada_beside(b)
                if a0 is not None and u == 2:
                    pe.wait_ge(s_adasb, A_EARLY + ada_order(b))
                    if fins(b - 1) > 0:
                        pe.wait_ge(s_adaout, fins(b - 1))
                    if b % 4 == 3 and b < B_OUT0:
                        pe.wait_ge(s_sub, 3 * (b // 4 + 1))
                    elif 4 <= b < B_OUT0:
                        pe.wait_ge(s_pTsb, 3 * (b // 4))
                    elif b in STAGES:
                        pe.wait_ge(s_xlo, TG * (STAGES.index(b) + 1))
                    if is_gate(a0):
                        last = mm(ps[:, 7], selbc[:, 0], adasb[:, a0 % 2], start=True, stop=True)
                    else:
                        last = ada_columns(a0, ps[:, 7])
                    last.then_inc(s_adafin, 1)
                if a0 is not None and u == 4 and is_gate(a0):
                    pe.wait_ge(s_adaout, fins(b - 1) + 1)
                    mm(ps[:, 7], selbc[:, 1], adasb[:, a0 % 2], start=True, stop=True).then_inc(s_adafin, 1)
                if a1 is not None and u % 2 == 1:
                    c = u // 2
                    if c == 0:
                        pe.wait_ge(s_adasb, A_EARLY + ada_order(b))
                    n = NCK * ada_order(b) + c
                    pe.wait_ge(s_araw[n % 2], 16 * (n // 2 + 1))
                    ada_chunk(4, araw[:, n % 2], c).then_inc(s_ada1, 1)

            def s5_transposed(w, i):
                n = 4 * w + i
                if i == 0:
                    pe.wait_ge(s_u2p, w + 1)
                    if w >= 1:
                        pe.wait_ge(s_STsb, 8 * w)
                if n >= 2:
                    pe.wait_ge(s_uTsb, 2 * (n - 1))
                for v in range(4):
                    src = u2p[:, 4 * (i // 2) + v]
                    out = ps[:, 5 + n % 2, v * P:(v + 1) * P]
                    if i % 2 == 0:
                        last = tr(out, src, ident[:])
                    else:
                        last = mm(out, src, perm[:], start=True, stop=True)
                last.then_inc(s_uT, 1)

            def s5_sums(w, j):
                if j == 0:
                    pe.wait_ge(s_uTsb, 8 * (w + 1))
                    if w == 0:
                        pe.wait_ge(s_adaout, fins(B_END))
                    if w >= 2:
                        pe.wait_ge(s_bt[w % 2], 16)
                for r in (2 * j, 2 * j + 1) if j < NR // 2 else ():
                    n = NR * w + r
                    if n >= 2:
                        pe.wait_ge(s_Ssb, n - 1)
                    if w < 2:
                        h = 2 * w + r // 8
                        if r % 8 == 0:
                            pe.wait_ge(s_bth[h % 2], 16 * (w + 1))
                        table = bth[:, h % 2, r % 8]
                    else:
                        table = btab[:, w % 2, r]
                    for dr, src in ((0, utf(w)[:, r]), (1, utr[:, r])):
                        out = ps[:, (4, 7)[n % 2], 0:2 * P].rearrange("p (i c) -> p i c", i=2)[
                            :, :, dr * S5P:(dr + 1) * S5P]
                        last = mm(out, src, table[:, :, dr * S5P:(dr + 1) * S5P], start=True, stop=True)
                    last.then_inc(s_S, 1)
                if j >= 1:
                    n = NR // 2 * w + j - 1
                    pe.wait_ge(s_Ssb, 2 * n + 2)
                    if n >= 2:
                        pe.wait_ge(s_STsb, n - 1)
                    for k in range(2):
                        for ri in range(2):
                            c0 = (2 * ri + k) * P
                            last = tr(ps[:, 5 + n % 2, c0:c0 + P], ss[:, k, ri * P:(ri + 1) * P], ident[:])
                    last.then_inc(s_ST, 1)

            def s5_outputs(w):
                pe.wait_ge(s_hy, 2 * (w + 1))
                pe.wait_ge(s_hyf, 2 * (w + 1))
                pe.wait_ge(s_ct, 16 * (w + 1))
                pe.wait_ge(s_kd, 16 * 8 * (w + 1))
                for q in range(4):
                    n = 4 * w + q
                    if n >= 2:
                        pe.wait_ge(s_ysb, n - 1)
                    for k in range(4):
                        r = 4 * q + k
                        out = ps[:, 2 + n % 2, k * P:(k + 1) * P]
                        mm(out, utf(w)[:, r], kd[:, r], start=True, stop=False)
                        for ri in range(2):
                            last = mm(out.rearrange("p (e k) -> p e k", e=2),
                                      hy[:, w % 2, ri, 4 * r:4 * r + 4].rearrange("p x j -> p (x j)"),
                                      ctab[:, ri].rearrange("p (e r) k -> p e r k", e=2)[:, :, r],
                                      start=False, stop=ri == 1)
                    last.then_inc(s_y, 1)

            for b in range(B_END):
                if b == B_IN0:
                    pe.wait_ge(s_xn, 2)
                    transposes(0, WA)
                if b == B_OUT0:
                    pe.wait_ge(s_og, 8)
                    transposes(1, WA)
                if b == B_IN1:
                    pe.wait_ge(s_xn, 4)
                    transposes(2, WA)
                if b == B_GLU:
                    wait_evacuated(pe, B_GLU - 1)
                    for j in range(NR // 2 + 1):
                        s5_sums(2, j)
                    for i in range(4):
                        s5_transposed(3, i)
                    for j in range(NR // 2 + 1):
                        s5_sums(3, j)
                    for w in range(NW):
                        s5_outputs(w)
                    pe.wait_ge(s_scan, NW)
                    pe.wait_ge(s_Ssb, NR * NW)
                    for ri in range(2):
                        last = tr(ps[:, 4, ri * P:(ri + 1) * P], fs[:, ri], ident[:])
                    last.then_inc(s_fsT, 1)
                    pe.wait_ge(s_STsb, 8 * NW)
                    pe.wait_ge(s_ysb, 4 * NW)
                    pe.wait_ge(s_yin, 32)
                    transposes(3, Y)
                if b == B_OUT1:
                    pe.wait_ge(s_g, 8)
                    transposes(4, WA)
                for u in range(UB):
                    unit(b, u)
                    if b < B_OUT0:
                        attention(b // 4, b, u)
                    modulation(b, u)
                    step, w, i = s5_beside(UB * b + u)
                    if step == "u":
                        s5_transposed(w, 2 * i)
                        s5_transposed(w, 2 * i + 1)
                    elif step == "S":
                        s5_sums(w, i)

        @block.scalar
        def _(act):
            seq = chain(act, s_act)
            af = nc.scalar.activation
            act.wait_ge(s_const, 16 * 7)
            act.wait_ge(s_cz, 1)
            af(cT32[:, :, 0:NS], condT[:], ACT.Silu).then_inc(s_cond, 1)

            def square_sums(i, src, junk):
                for st in range(NS):
                    af(junk[:, st], src[:, st], ACT.Square, accum_out=stat[:, 8 * i + st:8 * i + st + 1]).then_inc(s_stat, 1)

            def scale_rows(i, src, dst):
                act.wait_ge(s_rstd, 2 * i + 1)
                af(stat[:, 8 * i + 4:8 * i + 6], stat[:, 8 * i + 2:8 * i + 4], ACT.Sqrt).then_inc(s_stat, 1)
                act.wait_ge(s_rstd, 2 * i + 2)
                for st in range(NS):
                    af(dst[:, st], src[:, st], ACT.Copy, scale=stat[:, 8 * i + 6 + st:8 * i + 7 + st]).then_inc(s_xn, 1)

            act.wait_ge(s_pole, 16 * 3)
            af(tmp[:, 3], tmp[:, 0], ACT.Exp).then_inc(s_exp, 1)
            act.wait_ge(s_ang, 1)
            af(tmp[:, 5], tmp[:, 4], ACT.Exp)
            af(tmp[:, 9], tmp[:, 8], ACT.Sin)
            af(tmp[:, 10], tmp[:, 8], ACT.Sin, scale=0.5).then_inc(s_mag, 1)
            act.wait_ge(s_pow, 1)
            fwd, bwd = slice(0, S5P), slice(S5P, P)
            af(pb[fwd], apw[fwd][:, :, ::-1][:, :, 1:CH + 1], ACT.Copy)
            af(pb[bwd], apw[bwd][:, :, 0:CH], ACT.Copy)
            af(py[fwd], apw[fwd][:, :, 1:CH + 1], ACT.Copy)
            af(py[bwd], apw[bwd][:, :, ::-1][:, :, 0:CH], ACT.Copy).then_inc(s_pbpy, 1)

            def adasb_early(a):
                act.wait_ge(s_ada0, NCK * (a + 1))
                af(adasb[:, a % 2], ps[:, 4 if a % 2 == 0 else 1], ACT.Copy).then_inc(s_adasb, 1)

            def b_staged(w):
                if w == 0:
                    act.wait_ge(s_factors, 1)
                    act.wait_ge(s_bbm, 1)
                else:
                    act.wait_ge(s_bsout, 16 * w)
                for i in range(NR // 2):
                    act.wait_ge(s_btT, NR // 2 * w + i + 1)
                    af(bs[:, 2 * i:2 * i + 2].rearrange("p r i c -> p (r i c)"), ps[:, 5 + i % 2], ACT.Copy).then_inc(s_bs, 1)
                act.wait_ge(s_bs, NR // 2 * (w + 1))
                act.dma_start(bt_d[w], bs[:].rearrange("p r i c -> p (r i c)")).then_inc(s_bsout, 16)
                if w >= 1:
                    store_bands(w - 1)

            def store_bands(w):
                act.wait_ge(s_bandd, 4 * (w + 1))
                for j in range(4):
                    for e in range(2):
                        p0 = 32 * j + 16 * e
                        act.dma_start(band_d[w, :, j, e].rearrange("q c k -> c q k"),
                                      bands[p0:p0 + 16, :, e].rearrange("p q k c -> p q (k c)")).then_inc(s_bandout, 16)

            def bands_staged(w):
                act.wait_ge(s_ctm, w + 1)
                for ri in range(2):
                    act.dma_start(ct_d[w, :, ri], ce[:, ri, :, 1:CH + 1].rearrange("p g j c -> p g (j c)")).then_inc(s_ctout, 16)
                if w >= 1:
                    act.wait_ge(s_bandout, 16 * 8 * w)
                for q in range(4):
                    n = 4 * w + q
                    act.wait_ge(s_band, n + 1)
                    bank = ps[:, (7, 3)[n % 2]]
                    af(bands[:, q, :, CH - 1:NDL], bank[:, 0:P].rearrange("p (e k c) -> p e k c", e=2, c=S5C), ACT.Copy)
                    af(bands[:, q, :, 0:CH - 1], bank[:, P:2 * P].rearrange("p (e k c) -> p e k c", e=2, c=S5C)[
                        :, :, 0:CH - 1], ACT.Copy).then_inc(s_bandsb, 1)

            for step, n in EARLY:
                if step == "ada":
                    adasb_early(n)
                    if n == 2:
                        act.wait_ge(s_x, 32)
                        square_sums(0, WA, gate)
                elif step == "b":
                    b_staged(n)
                else:
                    bands_staged(n)
                    if n == 0:
                        act.wait_ge(s_stat, 2)
                        scale_rows(0, WA, WA)
            store_bands(NW - 1)

            def split(k):
                g = k // 2
                if k == 0:
                    act.wait_ge(s_btT, NW * NR // 2)
                    act.wait_ge(s_ends, NW)
                    act.wait_ge(s_ctm, NW)
                act.wait_ge(s_raw[g % 4], 16 * (A_EARLY * NCK // 4 + g // 4 + 1))
                if k >= 4:
                    act.wait_ge(s_wused, k - 3)
                src = raw[:, g % 4, (k % 2) * 2 * BN:(k % 2 + 1) * 2 * BN]
                af(whi[:, k % 4].rearrange("p k c -> p (k c)"), src, ACT.Copy).then_inc(s_hi, 1)

            def stage(i):
                if i == 0:
                    act.wait_ge(s_ctm, NW)
                for g in range(TG):
                    n = TG * i + g
                    act.wait_ge(s_tp, n + 1)
                    if i in (0, 2):
                        act.wait_ge(s_taff, TG * (i // 2) + g + 1)
                    af(xhi[:, 2 * g:2 * g + 2].rearrange("p k s c -> p (k s c)"), ps[:, 5 + n % 3], ACT.Copy).then_inc(s_xhi, 1)

            def evacuate_in0(b):
                hb, j = b // 4, b % 4
                if b == 0:
                    act.wait_ge(s_ctout, 32 * NW)
                    act.wait_ge(s_ends, NW)
                if hb >= 1:
                    if j == 0:
                        act.wait_ge(s_qT, hb)
                    elif j == 1:
                        act.wait_ge(s_kT, hb)
                        act.wait_ge(s_kvout, 32 * hb)
                    elif j == 2:
                        act.wait_ge(s_pv, hb)
                        act.wait_ge(s_kvout, 32 * hb)
                    else:
                        act.wait_ge(s_og, 2 * hb)
                for st in range(NS):
                    af(qkvz[:, j, st], ps[:, 2 * (b % 2) + st], ACT.Silu if j == 3 else ACT.Copy).then_inc(s_evA, 1)

            def attention(hb, j, u):
                if (j, u) == (1, 3):
                    if hb == 0:
                        act.wait_ge(s_bsout, 16 * NW)
                        act.wait_ge(s_bandout, 128 * NW)
                    act.wait_ge(s_qT, hb + 1)
                    if hb >= 1:
                        act.wait_ge(s_sc, hb)
                    for st in range(NS):
                        af(qT[:, st], ps[:, 5 + st], ACT.Copy, scale=QSCALE).then_inc(s_qTsb, 1)
                if (j, u) == (2, 3):
                    act.wait_ge(s_kT, hb + 1)
                    for st in range(NS):
                        af(kT[:, st], ps[:, 5 + st], ACT.Copy).then_inc(s_kTsb, 1)
                if (j, u) == (3, 1):
                    for i in range(3):
                        act.wait_ge(s_sub, 3 * hb + i + 1)
                        af(pr[:, i], pr[:, i], ACT.Exp).then_inc(s_prob, 1)
                if (j, u) == (3, 6):
                    act.wait_ge(s_pT, hb + 1)
                    if hb >= 1:
                        act.wait_ge(s_pv, hb)
                    for i in range(3):
                        af(pT[:, i], ps[:, 5 + i], ACT.Copy).then_inc(s_pTsb, 1)

            def s5_transposed(w, i):
                act.wait_ge(s_uT, 4 * w + i + 1)
                if i == 0:
                    act.wait_ge(s_zero, 1 + w // 2)
                if i == 1 and w >= 1:
                    act.wait_ge(s_S, NR * w)
                for e in range(2):
                    h = slice(e * M2, (e + 1) * M2)
                    dst = (utf(w) if i % 2 == 0 else utr)[h]
                    dst = dst.rearrange("p (g v) m -> p v g m", g=2)[:, 4 * (i // 2):4 * (i // 2) + 4, :, h]
                    af(dst, ps[h, 5 + i % 2].rearrange("p (v g m) -> p v g m", v=4, g=2), ACT.Copy).then_inc(s_uTsb, 1)

            def s5_sums(w, j):
                for r in (2 * j, 2 * j + 1) if j < NR // 2 else ():
                    n = NR * w + r
                    act.wait_ge(s_S, n + 1)
                    if n >= 2:
                        act.wait_ge(s_ST, n // 2)
                    af(ss[:, r % 2], ps[:, (4, 7)[n % 2], 0:2 * P], ACT.Copy).then_inc(s_Ssb, 1)
                if j == 1 and w == 0:
                    act.wait_ge(s_kept, 32)
                    act.wait_ge(s_xn, 4)
                if j == 1 and w >= 2:
                    act.wait_ge(s_hy, 2 * (w - 1))
                    act.wait_ge(s_hyf, 2 * (w - 1))
                if j >= 1:
                    n = NR // 2 * w + j - 1
                    act.wait_ge(s_ST, n + 1)
                    dst = sb[:, w % 2, :, :, 8 * (j - 1):8 * j].rearrange("p k i x -> p i x k")
                    af(dst, ps[:, 5 + n % 2].rearrange("p (i x k) -> p i x k", i=2, k=NCH), ACT.Copy).then_inc(s_STsb, 1)

            def s5_backward(w):
                act.wait_ge(s_scan, w + 1)
                act.wait_ge(s_wused, UB * B_GLU)
                if w >= 2:
                    act.wait_ge(s_y, 4 * (w - 1))
                src = sb[:, w % 2].rearrange("p k i x -> p i x k")
                for ri in range(2):
                    dst = hy[S5P:P, w % 2, ri]
                    af(dst[:, :, NCH - 1], h0[S5P:P, w, ri], ACT.Copy)
                    af(dst[:, :, 0:NCH - 1], src[S5P:P, ri, :, 0:NCH - 1][:, :, ::-1], ACT.Copy).then_inc(s_hy, 1)

            def s5_outputs(w):
                if w >= 2:
                    act.wait_ge(s_yout[w % 2], 32)
                for q in range(4):
                    n = 4 * w + q
                    act.wait_ge(s_y, n + 1)
                    for e in range(2):
                        h = slice(e * M2, (e + 1) * M2)
                        src_y = ps[h, 2 + n % 2].rearrange("p (r e t c) -> p e t r c", r=4, e=2, t=CH)[:, e]
                        dst = ys[h, w % 2, :, 64 * q:64 * q + 64].rearrange("p t (r c) -> p t r c", r=4)
                        last = af(dst, src_y, ACT.Gelu_apprx_tanh)
                    last.then_inc(s_ysb, 1)

            for k in range(-4, NU):
                if k + 4 < NU and not 0 <= k + 4 - UB * B_GLU < 4:
                    split(k + 4)
                b, u = k // UB, k % UB
                if k >= 0 and u == 0 and ada_beside(b - 1) is not None:
                    a = ada_beside(b - 1)
                    act.wait_ge(s_ada1, NCK * ada_order(b))
                    if ada_order(b) > 2:
                        act.wait_ge(s_adafin, fins(b - 1))
                    af(adasb[:, a % 2], ps[:, 4], ACT.Copy).then_inc(s_adasb, 1)
                if 0 <= b < B_OUT0:
                    attention(b // 4, b % 4, u)
                step, w, i = s5_beside(k)
                if step == "u":
                    s5_transposed(w, 2 * i)
                    s5_transposed(w, 2 * i + 1)
                elif step == "S":
                    s5_sums(w, i)
                if u == UB - 1:
                    if 0 <= b < B_GLU and not B_OUT0 <= b < B_IN1:
                        act.wait_ge(s_wused, UB * (b + 1))
                    if 0 <= b < B_OUT0:
                        evacuate_in0(b)
                    if B_IN1 <= b < B_IN1 + NW:
                        w = b - B_IN1
                        if w >= 2:
                            act.wait_ge(s_ubout[w % 2], 32 * (w // 2))
                        for st in range(NS):
                            af(ub[:, w % 2, st], ps[:, 2 * (b % 2) + st], ACT.Copy).then_inc(s_evA, 1)
                    if b == B_IN1 + NW:
                        for i in range(2):
                            act.wait_ge(s_ubout[i], 32 * NW // 2)
                    if B_IN1 + NW <= b < B_GLU:
                        c0 = (b - B_IN1 - NW) * BN
                        for st in range(NS):
                            af(WA[:, st, c0:c0 + BN], ps[:, 2 * (b % 2) + st], ACT.Silu).then_inc(s_evA, 1)
                    if b == B_IN1 - 1:
                        act.wait_ge(s_x2, 1)
                        square_sums(1, X, WA)
                        act.wait_ge(s_stat, 5)
                        scale_rows(1, X, WA)
                    if b == B_GLU - 1:
                        s5_backward(0)
                        for j in range(NR // 2 + 1):
                            s5_sums(2, j)
                        for i in range(4):
                            s5_transposed(3, i)
                        s5_backward(1)
                        for j in range(NR // 2 + 1):
                            s5_sums(3, j)
                        s5_outputs(0)
                        s5_outputs(1)
                        for w in (2, 3):
                            s5_backward(w)
                            s5_outputs(w)
                        act.wait_ge(s_fsT, 1)
                        af(fso[:].rearrange("p i c -> p (i c)"), ps[:, 4, 0:2 * P], ACT.Copy).then_inc(s_fso, 1)
                        for j in range(4):
                            split(UB * B_GLU + j)
                    if B_GLU <= b < B_OUT1:
                        for st in range(NS):
                            n = NS * (b - B_GLU) + st
                            act.wait_ge(s_evV, NS * (B_IN1 - B_OUT0) + n + 1)
                            if n >= 2:
                                act.wait_ge(s_g, n - 1)
                            af(tg[:, 2 + st], tg[:, st], ACT.Sigmoid).then_inc(s_gsig, 1)
                    if b + 1 in STAGES:
                        stage(STAGES.index(b + 1))
            act.wait_ge(s_x2, 2)
            square_sums(2, X, WA)
            act.wait_ge(s_stat, 8)
            scale_rows(2, X, WA)

        @block.vector
        def _(dve):
            seq = chain(dve, s_dve)
            tt = nc.vector.tensor_tensor
            ts = nc.vector.tensor_scalar
            nc.vector.memset(cT32[:], 0.0).then_inc(s_cz, 1)
            nc.vector.memset(apw[:, 0, 0], 1.0)
            seq(nc.vector.memset(apw[:, 1, 0], 0.0))
            ldt, are, aim, dt, xr, mag, th, kk, rr, sn, sh_, t0, t1, t2, f_re, f_im, den = [tmp[:, i] for i in range(17)]

            dve.wait_ge(s_exp, 1)
            tt(xr, are, dt, ALU.mult)
            seq(tt(th, aim, dt, ALU.mult))
            seq(ts(kk, th, 1.0 / (2 * math.pi), ROUND, ALU.mult, ALU.add))
            seq(ts(kk, kk, -ROUND, None, ALU.add))
            seq(nc.vector.scalar_tensor_tensor(rr, kk, -TWO_PI_HI, th, ALU.mult, ALU.add))
            seq(nc.vector.scalar_tensor_tensor(rr, kk, -TWO_PI_LO, rr, ALU.mult, ALU.add))
            ts(rr, rr, 3.1415925, -3.1415925, ALU.min, ALU.max).then_inc(s_ang, 1)

            def mean_squares(i, first):
                dve.wait_ge(s_stat, first)
                ts(stat[:, 8 * i + 2:8 * i + 4], stat[:, 8 * i:8 * i + 2], 1.0 / D, EPS, ALU.mult, ALU.add).then_inc(s_rstd, 1)
                dve.wait_ge(s_stat, first + 1)
                nc.vector.reciprocal(stat[:, 8 * i + 6:8 * i + 8], stat[:, 8 * i + 4:8 * i + 6]).then_inc(s_rstd, 1)

            dve.wait_ge(s_mag, 1)
            seq(tt(t0, sh_, sh_, ALU.mult))
            seq(ts(t0, t0, -2.0, 1.0, ALU.mult, ALU.add))
            tt(apw[:, 0, 1], mag, t0, ALU.mult)
            seq(tt(apw[:, 1, 1], mag, sn, ALU.mult))
            for i, j in ((1, 1), (2, 1), (2, 2)):
                tt(t0, apw[:, 0, i], apw[:, 0, j], ALU.mult)
                tt(t1, apw[:, 1, i], apw[:, 1, j], ALU.mult)
                tt(t2, apw[:, 0, i], apw[:, 1, j], ALU.mult)
                seq(tt(den, apw[:, 1, i], apw[:, 0, j], ALU.mult))
                tt(apw[:, 0, i + j], t0, t1, ALU.subtract)
                last = tt(apw[:, 1, i + j], t2, den, ALU.add)
                if i + j < CH:
                    seq(last)
            last.then_inc(s_pow, 1)
            dve.wait_ge(s_pow, 1)
            tt(t0, are, are, ALU.mult)
            seq(tt(t1, aim, aim, ALU.mult))
            seq(tt(den, t0, t1, ALU.add))
            seq(nc.vector.reciprocal(den, den))
            seq(ts(t2, apw[:, 0, 1], -1.0, None, ALU.add))
            tt(f_re, t2, are, ALU.mult)
            seq(tt(t0, apw[:, 1, 1], aim, ALU.mult))
            seq(tt(f_re, f_re, t0, ALU.add))
            seq(tt(f_re, f_re, den, ALU.mult))
            tt(f_im, apw[:, 1, 1], are, ALU.mult)
            seq(tt(t0, t2, aim, ALU.mult))
            seq(tt(f_im, f_im, t0, ALU.subtract))
            seq(tt(f_im, f_im, den, ALU.mult))
            dve.wait_ge(s_par, 16 * 5)
            m1g = m1[:].rearrange("p (g c) -> p g c", c=S5C)
            m2g = m2[:].rearrange("p (g c) -> p g c", c=S5C)

            def times(out, f, v):
                return tt(out, f.unsqueeze(2).to_broadcast([P, S5G, S5C]), v, ALU.mult)

            times(m1g, f_re, bre[:])
            seq(times(m2g, f_im, bim[:]))
            seq(tt(bb[:, 0], m1g, m2g, ALU.subtract))
            times(m1g, f_re, bim[:])
            seq(times(m2g, f_im, bre[:]))
            tt(bb[:, 1], m1g, m2g, ALU.add).then_inc(s_bbm, 1)
            dve.wait_ge(s_bbm, 1)
            dve.wait_ge(s_pbpy, 1)

            def table(out, pw, v_re, v_im, w, im_sign, done):
                gs = slice(w * GW, (w + 1) * GW)

                def prod(dst, a, v):
                    return tt(dst[:].rearrange("p (g t c) -> p g t c", t=CH, c=S5C),
                              a[:, :, gs].rearrange("p t g -> p g t").unsqueeze(3).to_broadcast([P, GW, CH, S5C]),
                              v[:, gs].unsqueeze(2).to_broadcast([P, GW, CH, S5C]), ALU.mult)

                def shaped(x):
                    return x[:].rearrange("p (e r t c) -> p e r (t c)", e=2, t=CH, c=S5C)
                prod(m1, pw[:, 0], v_re)
                seq(prod(m2, pw[:, 1], v_im))
                seq(tt(out[0], shaped(m1), shaped(m2), ALU.subtract))
                prod(m1, pw[:, 0], v_im)
                seq(prod(m2, pw[:, 1], v_re))
                if im_sign > 0:
                    last = tt(out[1], shaped(m1), shaped(m2), ALU.add)
                else:
                    last = nc.vector.scalar_tensor_tensor(out[1], shaped(m1), -1.0, shaped(m2), ALU.mult, ALU.subtract)
                last.then_inc(done, 1)
                dve.wait_ge(done, w + 1)

            def add_diagonals(w):
                for q in range(4):
                    n = 4 * w + q
                    dve.wait_ge(s_bandsb, n + 1)
                    diag = bands[:, q, :, CH - 1]
                    back = ps[:, (7, 3)[n % 2], P:2 * P].rearrange("p (e k c) -> p e k c", e=2, c=S5C)[:, :, CH - 1]
                    seq(tt(diag, diag, back, ALU.add))
                    tt(diag, diag, dm[:, n], ALU.add).then_inc(s_bandd, 1)

            for w in range(NW):
                if w >= 1:
                    dve.wait_ge(s_btT, NR // 2 * w)
                table([bt[:, ri].rearrange("p r e k -> p e r k") for ri in range(2)], pb, bb[:, 0], bb[:, 1], w, 1, s_btm)
                if w >= 1:
                    add_diagonals(w - 1)
                    if w == 1:
                        mean_squares(0, 2)
                    dve.wait_ge(s_ctout, 32 * w)
                    dve.wait_ge(s_band, 4 * w)
                table([ce[:, ri, :, 1:CH + 1].rearrange("p (e r) j c -> p e r (j c)", e=2) for ri in range(2)],
                      py, cre, cim, w, -1, s_ctm)
            add_diagonals(NW - 1)

            def shift_or_scale(src, lay, a0, kt0, nk, done):
                nb = (nk + 3) // 4
                for isc in range(2):
                    a = a0 + 4 * isc
                    if src[isc] is None:
                        continue
                    val = src[isc]
                    bias = bT[:, a:a + nb].rearrange("p a i -> p (a i)").unsqueeze(2).to_broadcast([P, nk, NS])
                    if isc == 0:
                        last = tt(shT[:, lay, kt0:kt0 + nk], val, bias, ALU.add)
                    else:
                        t = modt[:, 0:nk * NS].rearrange("p (k s) -> p k s", s=NS)
                        seq(tt(t, val, bias, ALU.add))
                        gain = gT[:, lay, kt0:kt0 + nk].unsqueeze(2).to_broadcast([P, nk, NS])
                        last = nc.vector.scalar_tensor_tensor(gsT[:, lay, kt0:kt0 + nk], t, 1.0, gain, ALU.add, ALU.mult)
                last.then_inc(done, 1)

            dve.wait_ge(s_adaE, 1)
            cols = [ps[:, 0, 32 * i:32 * i + 32].rearrange("p (k s) -> p k s", s=NS) for i in range(2)]
            shift_or_scale(cols, 0, 0, 0, KT, s_adaEout)
            dve.wait_ge(s_adaEout, 1)

            def split(k):
                g = k // 2
                if k == 0:
                    dve.wait_ge(s_btT, NW * NR // 2)
                dve.wait_ge(s_hi, k + 1)
                if k >= 4:
                    dve.wait_ge(s_wused, k - 3)
                src = raw[:, g % 4, (k % 2) * 2 * BN:(k % 2 + 1) * 2 * BN]
                tt(wlo[:, k % 4].rearrange("p k c -> p (k c)"), src,
                   whi[:, k % 4].rearrange("p k c -> p (k c)").bitcast(F32), ALU.subtract).then_inc(s_lo, 1)

            def stage(i):
                if i == 0:
                    dve.wait_ge(s_band, 4 * NW)
                    dve.wait_ge(s_ctout, 32 * NW)
                lay = i // 2

                def affine(g):
                    n = TG * i + g
                    dve.wait_ge(s_tp, n + 1)
                    for k in range(2):
                        for st in range(NS):
                            kt = 2 * g + k
                            x = ps[:, 5 + n % 3, (2 * k + st) * P:(2 * k + st + 1) * P]
                            last = ts(x, x, gsT[:, lay, kt, st:st + 1], shT[:, lay, kt, st:st + 1], ALU.mult, ALU.add)
                    last.then_inc(s_taff, 1)

                def low(g):
                    n = TG * i + g
                    dve.wait_ge(s_xhi, n + 1)
                    tt(xlo[:, 2 * g:2 * g + 2].rearrange("p k s c -> p (k s c)"), ps[:, 5 + n % 3],
                       xhi[:, 2 * g:2 * g + 2].rearrange("p k s c -> p (k s c)").bitcast(F32), ALU.subtract).then_inc(s_xlo, 1)

                if i in (0, 2):
                    affine(0)
                    for g in range(TG):
                        if g + 1 < TG:
                            affine(g + 1)
                        low(g)
                else:
                    for g in range(TG):
                        low(g)

            def by_head(x):
                return x.rearrange("p (h c) -> p h c", h=HB)

            def over_keys(x):
                return x.unsqueeze(2).to_broadcast([P, HB, P])

            def attention(hb, j, u):
                if (j, u) == (3, 0):
                    dve.wait_ge(s_sc, hb + 1)
                    if hb >= 1:
                        dve.wait_ge(s_pT, hb)
                    tr_ = nc.vector.tensor_reduce
                    tr_(asm[:, 0], by_head(ps[:, 5]), AX, ALU.max)
                    seq(tr_(asm[:, 2], by_head(ps[:, 7]), AX, ALU.max))
                    tt(by_head(pr[:, 0]), by_head(ps[:, 5]), over_keys(asm[:, 0]), ALU.subtract).then_inc(s_sub, 1)
                    seq(tt(pr[:, 1], ps[:, 6], bias_b[:], ALU.add))
                    seq(tr_(asm[:, 1], by_head(pr[:, 1]), AX, ALU.max))
                    seq(tt(asm[:, 3], asm[:, 1], asm[:, 2], ALU.max))
                    tt(by_head(pr[:, 1]), by_head(pr[:, 1]), over_keys(asm[:, 3]), ALU.subtract).then_inc(s_sub, 1)
                    tt(by_head(pr[:, 2]), by_head(ps[:, 7]), over_keys(asm[:, 3]), ALU.subtract).then_inc(s_sub, 1)
                if (j, u) == (3, 2):
                    dve.wait_ge(s_prob, 3 * (hb + 1))
                    for i in range(3):
                        last = nc.vector.tensor_reduce(asm[:, 4 + i], by_head(pr[:, i]), AX, ALU.add)
                    seq(last)
                    seq(tt(asm[:, 5], asm[:, 5], asm[:, 6], ALU.add))
                    seq(nc.vector.reciprocal(asm[:, 8:10], asm[:, 4:6]))
                if (j, u) == (3, 7):
                    dve.wait_ge(s_pv, hb + 1)
                    wait_evacuated(dve, 4 * hb + 3)
                    if hb >= 1:
                        dve.wait_ge(s_og, 2 * hb)
                    for st in range(NS):
                        seq(tt(by_head(tmo[:, st]), by_head(ps[:, 5 + st]), over_keys(asm[:, 8 + st]), ALU.mult))
                        tt(WA[:, st, hb * BN:(hb + 1) * BN], tmo[:, st], qkvz[:, 3, st], ALU.mult).then_inc(s_og, 1)

            def modulation(b, u):
                a0 = ada_beside(b - 1)
                if a0 is None or not (u == 3 or u == 5 and is_gate(a0)):
                    return
                part = (u - 3) // 2
                dve.wait_ge(s_adafin, fins(b - 1) + part + 1)
                i = a0 % 4
                if is_gate(a0):
                    dve.wait_ge(s_bg, 16 * (4 * (a0 // 12) + i + 1))
                    if a0 >= 12:
                        wait_evacuated(dve, b - 1)
                    tt(gate[:, part, i * BN:(i + 1) * BN], ps[:, 7], bgate[:], ALU.add).then_inc(s_adaout, 1)
                else:
                    val = ps[:, 7, 0:4 * NS].rearrange("p (k s) -> p k s", s=NS)
                    scale = a0 % 12 >= 4
                    shift_or_scale((None, val) if scale else (val, None), a0 // 12, a0 - 4 * scale, 4 * i, 4, s_adaout)

            def residual(b, lay, buf):
                c0 = b % 4 * BN
                dve.wait_ge(s_wused, UB * (b + 1))
                for st in range(NS):
                    tt(buf[:, st], ps[:, 2 * (b % 2) + st], gate[:, st, c0:c0 + BN], ALU.mult).then_inc(s_evV, 1)
                wait_evacuated(dve, b)
                for st in range(NS):
                    last = tt(X[:, st, c0:c0 + BN], X[:, st, c0:c0 + BN], buf[:, st], ALU.add)
                if b % 4 == 3:
                    last.then_inc(s_x2, 1)
                else:
                    seq(last)

            def scan(*steps):
                chains = []
                for i, (w, k) in enumerate(steps):
                    if k == 0:
                        dve.wait_ge(s_STsb, 8 * (w + 1))
                        if w == 0:
                            dve.wait_ge(s_h0, 16)
                    now = h0[:, w].rearrange("p i x -> p i x") if k == 0 else sb[:, w % 2, k - 1]
                    last = tt((t12, t12b)[w % 2][:], coef[:, w], now.unsqueeze(2).to_broadcast([P, 2, 2, 2 * GW]), ALU.mult)
                    chains.append((sb[:, w % 2, k], (t12, t12b)[w % 2]))
                seq(last)
                for half in range(2):
                    for nxt, t in chains:
                        last = tt(nxt, nxt, t[:, half], ALU.add)
                    seq(last)

            def scanned(w):
                fin = sb[:, w % 2, NCH - 1].rearrange("p i (r e s) -> p i e r s", e=2, s=NS)
                for e in range(2):
                    g0 = w * GW + e * NR
                    last = nc.vector.tensor_copy(fs[:, :, g0:g0 + NR], fin[:, :, e, :, 0])
                last.then_inc(s_scan, 1)

            def s5_forward(w):
                dve.wait_ge(s_scan, w + 1)
                dve.wait_ge(s_wused, UB * B_GLU)
                if w >= 2:
                    dve.wait_ge(s_y, 4 * (w - 1))
                src = sb[:, w % 2].rearrange("p k i x -> p i x k")
                for ri in range(2):
                    dst = hy[0:S5P, w % 2, ri]
                    nc.vector.tensor_copy(dst[:, :, 0], h0[0:S5P, w, ri])
                    nc.vector.tensor_copy(dst[:, :, 1:NCH], src[0:S5P, ri, :, 0:NCH - 1]).then_inc(s_hyf, 1)

            for k in range(-4, NU):
                if k + 4 < NU and not 0 <= k + 4 - UB * B_GLU < 4:
                    split(k + 4)
                b, u = k // UB, k % UB
                if k >= 0:
                    modulation(b, u)
                due = [(w, k - SCAN_FROM[w]) for w in range(2) if 0 <= k - SCAN_FROM[w] < NCH and k < UB * B_GLU]
                if due:
                    scan(*due)
                    if due[0] == (0, NCH - 1):
                        scanned(0)
                if k == UB * B_GLU:
                    wait_evacuated(dve, B_GLU - 1)
                    dve.wait_ge(s_yin, 32)
                    for st in range(NS):
                        last = tt(WA[:, st], WA[:, st], Y[:, st], ALU.mult)
                    seq(last)
                if 0 <= b < B_OUT0:
                    attention(b // 4, b % 4, u)
                if u == UB - 1:
                    if B_OUT0 <= b < B_IN1:
                        if b == B_OUT0:
                            dve.wait_ge(s_x2in, 32)
                        residual(b, 0, pr)
                    if b == B_IN1 - 1:
                        mean_squares(1, 5)
                    if b == B_GLU - 1:
                        s5_forward(0)
                        for c in range(k + 1 - SCAN_FROM[1], NCH):
                            scan((1, c))
                        scanned(1)
                        s5_forward(1)
                        for c in range(NCH + SCAN_LAG):
                            scan(*(([(2, c)] if c < NCH else []) + ([(3, c - SCAN_LAG)] if c >= SCAN_LAG else [])))
                            if c == NCH - 1:
                                scanned(2)
                                s5_forward(2)
                        scanned(3)
                        s5_forward(3)
                        for j in range(4):
                            split(UB * B_GLU + j)
                    if B_GLU <= b < B_OUT1:
                        c0 = (b - B_GLU) * BN
                        dve.wait_ge(s_wused, UB * (b + 1))
                        dve.wait_ge(s_vec, 32)
                        for st in range(NS):
                            n = NS * (b - B_GLU) + st
                            if n >= 2:
                                dve.wait_ge(s_gsig, n - 1)
                            tt(tg[:, st], ps[:, 2 * (b % 2) + st], bglu[:, c0:c0 + BN], ALU.add).then_inc(s_evV, 1)
                        for st in range(NS):
                            n = NS * (b - B_GLU) + st
                            dve.wait_ge(s_gsig, n + 1)
                            g_ = WA[:, st, c0:c0 + BN]
                            tt(g_, g_, tg[:, 2 + st], ALU.mult).then_inc(s_g, 1)
                    if b == B_OUT1:
                        dve.wait_ge(s_back, 32)
                    if b >= B_OUT1:
                        residual(b, 1, tg)
                    if b + 1 in STAGES:
                        stage(STAGES.index(b + 1))
            mean_squares(2, 8)
            for st in range(NS):
                dve.wait_ge(s_xn, 5 + st)
                tt(X[:, st], WA[:, st], gfin[:], ALU.mult).then_inc(s_fin, 1)


_OUTS = {"y": (NS, P, D), "new_k": (P, D), "new_v": (P, D), "new_state": (2, 2, S5G, S5P)}


def _blocks(w):
    n = w.shape[1] // BN
    v = w.reshape(NCK, CK, P, n, BN).transpose(3, 2, 0, 1, 4)
    return v.reshape(n, P, NCK, CK * BN)


def _lay_out(i):
    f = np.float32
    w_in0 = _blocks(i["l0_w_in"]).reshape(4, 4, P, NCK, CK * BN).transpose(1, 0, 2, 3, 4).reshape(16, P, NCK, CK * BN)
    out = {
        "x": np.stack([i["x_prompt"][0], i["x_sample"][0]]),
        "w": np.concatenate([w_in0, _blocks(i["l0_w_out"]), _blocks(i["l1_w_in"]), _blocks(i["l1_w_glu"]),
                             _blocks(i["l1_w_out"])]),
        "wada": np.concatenate([_blocks(i["l0_w_ada"]), _blocks(i["l1_w_ada"])]),
        "condT": np.stack([i["c_ctx"], i["c"][0]]).reshape(NS, KT, P).transpose(2, 1, 0),
        "gT": np.stack([i["l0_norm_g"], i["l1_norm_g"]]).reshape(2, KT, P).transpose(2, 0, 1),
        "bT": np.stack([i["l0_b_ada"], i["l1_b_ada"]]).reshape(24, 4, P).transpose(2, 0, 1),
        "bgate": np.concatenate([i["l0_b_ada"][2 * D:], i["l1_b_ada"][2 * D:]]).reshape(8, BN),
        "b_glu": i["l1_b_glu"],
        "g_fin": i["final_norm_g"],
        "ident": np.eye(P, dtype=f),
        "kcT": i["cache_l0_k"][0].reshape(P, 4, HB, P).transpose(1, 3, 2, 0).reshape(4, P, BN),
        "vc": i["cache_l0_v"][0].reshape(P, 4, BN).transpose(1, 0, 2),
        "are": i["l1_a_re"].transpose(0, 2, 1).reshape(P, S5G),
        "aim": i["l1_a_im"].transpose(0, 2, 1).reshape(P, S5G),
        "ldt": np.repeat(i["l1_log_dt"][:, None], S5P, axis=1).reshape(P, S5G),
        "bre": i["l1_b_re"].transpose(0, 2, 1, 3).reshape(P, S5G, S5C),
        "bim": i["l1_b_im"].transpose(0, 2, 1, 3).reshape(P, S5G, S5C),
        "cre": i["l1_c_re"].transpose(0, 3, 1, 2).reshape(P, S5G, S5C),
        "cim": i["l1_c_im"].transpose(0, 3, 1, 2).reshape(P, S5G, S5C),
    }
    rows = np.arange(P)
    perm = np.zeros((P, P), f)
    perm[rows, rows // NCH * NCH + NCH - 1 - rows % NCH] = 1.0
    out["perm"] = perm
    sel2 = np.zeros((P, NS), f)
    sel2[rows[rows % 32 < NS], rows[rows % 32 < NS] % 32] = 1.0
    out["sel2"] = sel2
    out["selbc"] = np.repeat(sel2[:, :, None], P, axis=2)
    q, k = rows[:, None], rows[None, :]
    dr = k // GRID_W - q // GRID_W + NA_ROWS - 1
    dc = np.clip(k % GRID_W - q % GRID_W + NA_COLS - 1, 0, 2 * NA_COLS - 2)
    c0 = np.clip(q % GRID_W - NA_COLS // 2, 0, GRID_W - NA_COLS)
    ok = (k % GRID_W >= c0) & (k % GRID_W < c0 + NA_COLS)
    bias = np.where(ok[None], i["l0_rpb"][:, dr, dc], f(NEG))
    out["bias"] = bias.reshape(4, HB, P, P).transpose(0, 2, 1, 3).reshape(4, P, BN)
    skip = i["l1_d"].reshape(NW, 2, 4, 4, S5C)
    dm = np.zeros((4, 2, S5C, NW, 4, 2, S5C), f)
    for e in range(2):
        for c in range(S5C):
            dm[:, e, c, :, :, e, c] = skip[:, e, :, :, c].transpose(2, 0, 1)
    out["dm"] = dm.reshape(P, NR, 2, S5C)
    st = i["state_l1_s5"][0].reshape(2, 2, NW, 2, NR, S5P)
    h0 = np.zeros((2, S5P, NW, 2, NR, 2, NS), f)
    h0[..., 1] = st.transpose(0, 5, 2, 1, 4, 3)
    out["h0"] = h0.reshape(P, NW, 2, 2 * GW)
    return {name: np.ascontiguousarray(a) for name, a in out.items()}


def kernel(**inputs):
    import concourse.bacc as bacc
    from concourse.bass_utils import run_bass_kernel_spmd

    arrays = _lay_out({name: np.asarray(a) for name, a in inputs.items()})
    nc = bacc.Bacc("TRN2", target_bir_lowering=False, num_devices=1)
    d = {name: nc.dram_tensor("in_" + name, a.shape, mybir.dt.from_np(a.dtype), kind="ExternalInput").ap()
         for name, a in arrays.items()}
    for name, shape in _OUTS.items():
        d[name] = nc.dram_tensor("out_" + name, shape, F32, kind="ExternalOutput").ap()
    build(nc, d)
    r = run_bass_kernel_spmd(nc, [{"in_" + name: a for name, a in arrays.items()}], core_ids=[0]).results[0]
    y = r["out_y"]
    return (y[0:1], y[1:2], r["out_new_k"].reshape(1, P, NH, P), r["out_new_v"].reshape(1, P, NH, P),
            r["out_new_state"].reshape(1, 2, 2, S5G, S5P))
```

```python
import math
from contextlib import ExitStack

import concourse.bass as bass
from concourse import mybir
import numpy as np

F32 = mybir.dt.float32
F32R = mybir.dt.float32r
ALU = mybir.AluOpType
ACT = mybir.ActivationFunctionType
AX = mybir.AxisListType.X

P = 128
D = 2048
KT = D // P
NS = 2
BN = 512
CK = 4
NCK = KT // CK
NH = 16
HB = BN // P
EPS = 1e-6
QSCALE = float(P) ** -0.5
GRID_W, NA_COLS, NA_ROWS = 64, 16, 8
NEG = -1e30
S5G, S5P, S5C = 128, 64, 16
CH = 4
NCH = P // CH
M2 = NS * NCH
NW = 4
NR = 16
GW = 2 * NR
NDL = 2 * CH - 1

B_IN0, B_OUT0, B_IN1, B_GLU, B_OUT1, B_END = 0, 16, 20, 28, 32, 36
A_EARLY = 8

UB = 2 * NCK
NU = B_END * UB
AHEAD = 3
TG = KT // 2
STAGES = (B_IN0, B_OUT0, B_IN1, B_GLU, B_OUT1)

EARLY = (("ada", 0), ("ada", 1), ("ada", 2), ("ada", 3), ("b", 0), ("ada", 4), ("band", 0), ("ada", 5),
         ("b", 1), ("band", 1), ("ada", 6), ("b", 2), ("band", 2), ("ada", 7), ("b", 3), ("band", 3))
ROUND = 1.5 * 2.0 ** 23
TWO_PI_HI = 6.28125
TWO_PI_LO = 2 * math.pi - TWO_PI_HI


def ada_beside(b):
    if 0 <= b < 12:
        return 8 + b
    if B_OUT0 <= b < B_OUT0 + 4:
        return 20 + b - B_OUT0
    return None


S5_BESIDE = (("u", 0, UB * 22 + 1, 2), ("S", 0, UB * 22 + 3, 9), ("u", 1, UB * 23 + 4, 2), ("S", 1, UB * 23 + 6, 9),
             ("u", 2, UB * 25 + 2, 2))
SCAN_FROM = (UB * 23 + 4, UB * 24 + 7)
SCAN_LAG = 20


def s5_beside(k):
    return next(((step, w, k - first) for step, w, first, n in S5_BESIDE if first <= k < first + n), (None, 0, 0))


def is_gate(a):
    return a % 12 >= 8


def fins(b):
    return sum(1 + is_gate(ada_beside(x)) for x in range(b) if ada_beside(x) is not None)


def fin_bank(b):
    return 4 if b == B_IN1 else 7


def ada_order(b):
    return sum(ada_beside(x) is not None for x in range(b))



def build(nc, d):
    with ExitStack() as ctx:
        K = 1024

        def at(name, shape, off, dt=F32):
            return nc.alloc_sbuf_tensor_at(name, shape, dt, offset=16512 + off)

        def sem(name):
            return ctx.enter_context(nc.semaphore(name))

        raw = at("raw", [P, 4, CK * BN], 0)
        whi = at("whi", [P, 4, 2, BN], 32 * K, F32R)
        wlo = at("wlo", [P, 4, 2, BN], 48 * K, F32R)
        araw = at("araw", [P, 2, CK * BN], 64 * K)
        xhi = at("xhi", [P, KT, NS, P], 80 * K, F32R)
        xlo = at("xlo", [P, KT, NS, P], 96 * K, F32R)
        X = at("X", [P, NS, D], 112 * K)
        gate = at("gate", [P, NS, D], 128 * K)
        WA = at("WA", [P, NS, D], 144 * K)
        m = 160 * K
        ident = at("ident", [P, P], m)
        perm = at("perm", [P, P], m + 512)
        selbc = at("selbc", [P, NS, P], m + K)
        coef = at("coef", [P, NW, 2, 2, 2 * GW], m + 2 * K)
        sel2 = at("sel2", [P, NS], m + 6 * K)
        bT = at("bT", [P, 24, 4], m + 6 * K + 64)
        gT = at("gT", [P, 2, KT], m + 6 * K + 512)
        shT = at("shT", [P, 2, KT, NS], m + 6 * K + 768)
        gsT = at("gsT", [P, 2, KT, NS], m + 7 * K + 256)
        condT = at("condT", [P, KT, NS], m + 7 * K + 512)
        stat = at("stat", [P, 32], m + 7 * K + 640)
        modt = at("modt", [P, 64], m + 7 * K + 768)
        cT32 = at("cT32", [P, KT, 32], m + 8 * K)
        adasb = at("adasb", [P, 2, BN], m + 10 * K)
        bgate = at("bgate", [P, BN], m + 14 * K)
        ar = 176 * K
        qkvz = at("qkvz", [P, 4, NS, BN], 112 * K)
        qT = at("qT", [P, NS, BN], ar)
        kT = at("kT", [P, NS, BN], ar + 4 * K)
        pr = at("pr", [P, 3, BN], ar + 8 * K)
        pT = at("pT", [P, 3, BN], ar + 14 * K)
        bias_b = at("bias_b", [P, BN], ar + 20 * K)
        kc_b = at("kc_b", [P, BN], ar + 22 * K)
        vc_b = at("vc_b", [P, BN], ar + 24 * K)
        asm = at("asm", [P, 16, HB], ar + 26 * K)
        tmo = at("tmo", [P, 2, BN], ar + 27 * K)
        cre = at("cre", [P, S5G, S5C], 32 * K)
        cim = at("cim", [P, S5G, S5C], 40 * K)
        bre = at("bre", [P, S5G, S5C], 48 * K)
        bim = at("bim", [P, S5G, S5C], 56 * K)
        bt = at("bt", [P, 2, NR, 2, CH * S5C], 48 * K)
        bb = at("bb", [P, 2, S5G, S5C], 64 * K)
        m1 = at("m1", [P, GW * CH * S5C], 80 * K)
        m2 = at("m2", [P, GW * CH * S5C], 88 * K)
        ce = at("ce", [P, 2, CH + 2, GW, S5C], 96 * K)
        bbf = at("bbf", [P, 2, NR, 2, S5C], 120 * K)
        bbb = at("bbb", [P, 2, NR, 2, S5C], 124 * K)
        bs = at("bs", [P, NR, 2, P], ar)
        bands = at("bands", [P, 4, 2, NDL, S5C], ar + 16 * K)
        pb = at("pb", [P, 2, CH, S5G], ar + 20 * K)
        py = at("py", [P, 2, CH, S5G], ar + 24 * K)
        dm = at("dm", [P, NR, 2, S5C], ar + 28 * K)
        tmp = at("tmp", [P, 18, S5G], ar)
        apw = at("apw", [P, 2, CH + 1, S5G], ar + 9 * K)
        btab = at("btab", [P, 2, NR, 2, P], 0)
        bth = at("bth", [P, 2, NR // 2, 2, P], 64 * K)
        ctab0 = at("ctab0", [P, 2, CH, GW, S5C], 32 * K)
        ctab1 = at("ctab1", [P, 2, CH, GW, S5C], 16 * K)
        kd = at("kd", [P, 2, NR, P], 48 * K)
        hy = at("hy", [P, 2, 2, 2 * GW, NCH], 80 * K)
        sb = at("sb", [P, 2, NCH, 2, 2 * GW], 112 * K)
        ub = at("ub", [P, 2, NS, BN], 152 * K)
        utf01 = at("utf01", [P, 2, NR, P], ar)
        utf23 = at("utf23", [P, 2, NR, P], 64 * K)
        utr = at("utr", [P, NR, P], m + 8 * K)
        ys = at("ys", [P, 2, CH, NR * S5C], m + 8 * K)
        u2p = at("u2p", [P, 8, 2 * CH * S5C], ar + 16 * K)
        u2 = at("u2", [P, CH, 2, P], ar + 20 * K)
        ss = at("ss", [P, 2, 2 * P], ar + 24 * K)
        h0 = at("h0", [P, NW, 2, 2 * GW], ar + 26 * K)
        fs = at("fs", [P, 2, S5G], ar + 28 * K)
        t12 = at("t12", [P, 2, 2, 2 * GW], ar + 29 * K)
        t12b = at("t12b", [P, 2, 2, 2 * GW], ar + 30 * K)
        fso = at("fso", [P, 2, P], ar + 26 * K)
        Y = at("Y", [P, NS, D], 112 * K)
        bglu = at("bglu", [P, D], ar)
        gfin = at("gfin", [P, D], ar + 8 * K)
        tg = at("tg", [P, 4, BN], ar + 16 * K)

        ps = ctx.enter_context(nc.psum_tensor("ps", [P, 8, BN], F32))

        band_d = nc.dram_tensor("band_scratch", (NW, 4, 4, 2, S5C, NDL * S5C), F32).ap()
        bt_d = nc.dram_tensor("btab_scratch", (NW, P, NR * 2 * P), F32).ap()
        ct_d = nc.dram_tensor("ctab_scratch", (NW, P, 2, CH, GW, S5C), F32).ap()
        u_d = nc.dram_tensor("u_scratch", (NS * P, D), F32).ap()
        x_keep = nc.dram_tensor("x_keep", (P, NS * D), F32).ap()
        gate_keep = nc.dram_tensor("gate_keep", (P, NS * D), F32).ap()
        y_d = nc.dram_tensor("y_scratch", (NS * P, D), F32).ap()

        s_const, s_pole, s_par, s_x = sem("const_in"), sem("poles_in"), sem("params_in"), sem("x_in")
        s_raw = [sem(f"raw_in{i}") for i in range(4)]
        s_araw = [sem(f"araw_in{i}") for i in range(2)]
        s_hi, s_lo, s_wused = sem("w_hi"), sem("w_lo"), sem("w_used")
        s_ada0, s_ada1 = sem("ada_early_used"), sem("ada_used")
        s_cz, s_cond, s_adasb = sem("cond_zero"), sem("cond_ready"), sem("ada_sb")
        s_adaE, s_adaEout = sem("ada_early_fin"), sem("ada_early_out")
        s_adafin, s_adaout, s_bg = sem("ada_fin"), sem("ada_out"), sem("bgate_in")
        s_evA, s_evV = sem("acc_evacuated_act"), sem("acc_evacuated_dve")
        s_tp, s_taff, s_xhi, s_xlo = sem("t_pe"), sem("t_affine"), sem("x_hi"), sem("x_lo")
        s_dve, s_pool = sem("dve_order"), sem("pool_order")
        s_ang, s_exp, s_pow, s_pbpy = sem("s5_angles"), sem("s5_exp"), sem("s5_powers"), sem("pb_py")
        s_btm, s_btT, s_bs, s_bsout = sem("b_table"), sem("b_tr"), sem("b_staged"), sem("b_stored")
        s_ctm, s_ends, s_bbm = sem("c_table"), sem("c_ends"), sem("bb_ready")
        s_ctout = [sem(f"c_stored{i}") for i in range(2)]
        s_band, s_bandsb, s_bandd, s_bandout = sem("band_pe"), sem("band_sb"), sem("band_d"), sem("band_stored")
        s_attin, s_kvout = sem("att_in"), sem("kv_out")
        s_qT, s_qTsb, s_kT, s_kTsb = sem("qT_pe"), sem("qT_sb"), sem("kT_pe"), sem("kT_sb")
        s_sc, s_sub, s_prob = sem("scores"), sem("scores_shifted"), sem("probs")
        s_pT, s_pTsb, s_pv, s_og = sem("pT_pe"), sem("pT_sb"), sem("pv"), sem("gated_o")
        s_x2in, s_stat, s_rstd, s_xn = sem("x_again"), sem("square_sums"), sem("rstd"), sem("x_normed")
        s_ubout = [sem(f"u_stored{i}") for i in range(2)]
        s_u2, s_u2p, s_zero = sem("u2_in"), sem("u2_ordered"), sem("zeros")
        s_uT, s_uTsb = sem("uT_pe"), sem("uT_sb")
        s_bt = [sem(f"btab_in{i}") for i in range(2)]
        s_bth = [sem(f"b_half_in{i}") for i in range(2)]
        s_kept, s_back, s_kdz = sem("x_gate_kept"), sem("x_gate_back"), sem("kd_zero")
        s_hyf, s_factors = sem("hy_forward"), sem("scan_factors")
        s_ct, s_kd = [[sem(f"{x}{i}") for i in range(2)] for x in ("ctab_in", "kd_in")]
        s_h0, s_tact = sem("h0_in"), sem("t_affine_act")
        s_S, s_Ssb, s_ST, s_STsb = sem("S_pe"), sem("S_sb"), sem("ST_pe"), sem("ST_sb")
        s_scan, s_hy, s_y, s_ysb = sem("scan"), sem("hy"), sem("y_pe"), sem("y_sb")
        s_yout, s_yin = [[sem(f"{x}{i}") for i in range(NW)] for x in ("y_stored", "y_in")]
        s_yz = sem("y_times_z")
        s_fsT, s_fso = sem("fin_T"), sem("fin_sb")
        s_mag = sem("s5_mag")
        s_vec, s_gsig, s_g = sem("vectors_in"), sem("glu_sig"), sem("gated_y")
        s_x2, s_fin, s_out, s_stout = sem("x2"), sem("final"), sem("y_out"), sem("state_out")
        block = ctx.enter_context(nc.Block())

        def utf(w):
            return (utf01, utf23)[w // 2][:, w % 2]

        def wait_evacuated(eng, b):
            if b < B_OUT0:
                eng.wait_ge(s_evA, NS * (b + 1))
            elif b < B_IN1:
                eng.wait_ge(s_evV, NS * (b - B_OUT0 + 1))
            elif b < B_GLU:
                eng.wait_ge(s_evA, NS * (B_OUT0 + b - B_IN1 + 1))
            else:
                eng.wait_ge(s_evV, NS * (B_IN1 - B_OUT0 + b - B_GLU + 1))

        def chain(eng, s):
            n = [0]

            def mark(ins):
                n[0] += 1
                ins.then_inc(s, 1)
                eng.wait_ge(s, n[0])
            return mark

        @block.sync
        def _(sp):
            for name, dst in (("condT", condT), ("ident", ident), ("perm", perm), ("selbc", selbc),
                              ("sel2", sel2), ("bT", bT), ("gT", gT)):
                sp.dma_start(dst[:], d[name]).then_inc(s_const, 16)
            for e in range(A_EARLY * NCK):
                if e >= 4:
                    sp.wait_ge(s_ada0, e - 3)
                sp.dma_start(raw[:, e % 4], d["wada"][e // NCK, :, e % NCK]).then_inc(s_raw[e % 4], 16)
            def half_b_table(n):
                if n == 0:
                    sp.wait_ge(s_bsout, 16 * NW)
                    for ri in range(2):
                        sp.wait_ge(s_ctout[ri], 16 * NW)
                    sp.wait_ge(s_bandout, 128 * NW)
                    sp.wait_ge(s_ada1, NCK * ada_order(B_END))
                if n >= 2:
                    sp.wait_ge(s_S, NR // 2 * (n - 1))
                half = NR // 2 * 2 * P
                sp.dma_start(bth[:, n % 2].rearrange("p r i c -> p (r i c)"),
                             bt_d[n // 2, :, n % 2 * half:(n % 2 + 1) * half]).then_inc(s_bth[n % 2], 16)

            def load_tables():
                def b_table(w):
                    sp.dma_start(btab[:, w % 2].rearrange("p r i c -> p (r i c)"), bt_d[w]).then_inc(s_bt[w % 2], 16)

                def y_tables(w):
                    sp.dma_start((ctab0, ctab1)[w % 2][:], ct_d[w]).then_inc(s_ct[w % 2], 16)
                    for e in range(2):
                        for s in range(CH):
                            p0 = e * CH * S5C + s * S5C
                            k0 = (CH - 1 - s) * S5C
                            sp.dma_start(kd[p0:p0 + S5C, w % 2, :, e * 64:e * 64 + 64],
                                         band_d[w, :, :, e].rearrange("q j c k -> c (q j) k")[:, :, k0:k0 + 64]).then_inc(s_kd[w % 2], 16)

                for w in (2, 3):
                    sp.wait_ge(s_lo, UB * B_GLU - 12 + 4 * w)
                    b_table(w)
                sp.wait_ge(s_kdz, 1)
                for w in range(NW):
                    if w == 1:
                        sp.wait_ge(s_S, NR * NW)
                    if w >= 2:
                        sp.wait_ge(s_y, 4 * (w - 1))
                    y_tables(w)

            for g in range(B_END * NCK):
                b, c = g // NCK, g % NCK
                if g in (84, 85, 98, 100):
                    half_b_table((84, 85, 98, 100).index(g))
                if g == B_GLU * NCK:
                    load_tables()
                    sp.wait_ge(s_S, NR * NW)
                if g == B_GLU * NCK + 2:
                    sp.wait_ge(s_y, 4 * NW)
                if g < 4:
                    sp.wait_ge(s_ada0, A_EARLY * NCK - 3 + g)
                else:
                    sp.wait_ge(s_hi, 2 * (g - 3))
                    sp.wait_ge(s_lo, 2 * (g - 3))
                sp.dma_start(raw[:, g % 4], d["w"][b, :, c]).then_inc(s_raw[g % 4], 16)
                b, c = (g - 3) // NCK, (g - 3) % NCK
                if ada_beside(b) is not None:
                    n = NCK * ada_order(b) + c
                    if n == 0:
                        sp.wait_ge(s_ends, NW)
                        sp.wait_ge(s_btm, 2 * NW)
                    if n >= 2:
                        sp.wait_ge(s_ada1, n - 1)
                    sp.dma_start(araw[:, n % 2], d["wada"][ada_beside(b), :, c]).then_inc(s_araw[n % 2], 16)

            for c in range(NCK):
                sp.wait_ge(s_fin, c + 1)
                cols = slice(c * BN, (c + 1) * BN)
                sp.dma_start(d["y"][:, :, cols].rearrange("s p c -> p s c"), X[:, :, cols]).then_inc(s_out, 16)
            sp.wait_ge(s_out, 64)

        @block.gpsimd
        def _(pool):
            seq = chain(pool, s_pool)
            for name, dst in (("ldt", tmp[:, 0]), ("are", tmp[:, 1]), ("aim", tmp[:, 2])):
                pool.dma_start(dst, d[name]).then_inc(s_pole, 16)
            for st in range(NS):
                pool.dma_start(WA[:, st], d["x"][st]).then_inc(s_x, 16)
            for name, dst in (("bre", bre), ("bim", bim), ("cre", cre), ("cim", cim), ("dm", dm)):
                pool.dma_start(dst[:], d[name]).then_inc(s_par, 16)
            seq(nc.gpsimd.memset(bbf[:], 0.0))
            seq(nc.gpsimd.memset(bbb[:], 0.0))
            pool.wait_ge(s_pow, 1)
            for w in range(NW):
                for e in range(2):
                    g0 = w * GW + e * NR
                    for src, dst, ri, sign in ((0, 0, 0, 1.0), (0, 1, 1, 1.0), (1, 0, 1, -1.0), (1, 1, 0, 1.0)):
                        o = coef[:, w, src, dst].rearrange("p (r e s) -> p r e s", e=2, s=NS)[:, :, e]
                        power = apw[:, ri, CH, g0:g0 + NR].unsqueeze(2).to_broadcast([P, NR, NS])
                        last = nc.gpsimd.tensor_scalar(o, power, sign, None, ALU.mult)
                        if (w, e, src, dst) != (NW - 1, 1, 1, 1):
                            seq(last)
            last.then_inc(s_factors, 1)
            pool.wait_ge(s_factors, 1)
            pool.wait_ge(s_par, 16 * 5)
            pool.wait_ge(s_bbm, 1)
            for w in range(NW):
                if w >= 1:
                    pool.wait_ge(s_band, 4 * w)
                    for ri in range(2):
                        pool.wait_ge(s_ctout[ri], 16 * w)
                for ri in range(2):
                    for e in range(2):
                        g0 = w * GW + e * NR
                        seq(nc.gpsimd.tensor_copy(bbf[0:64, ri, :, e], bb[0:64, ri, g0:g0 + NR]))
                        seq(nc.gpsimd.tensor_copy(bbb[64:128, ri, :, e], bb[64:128, ri, g0:g0 + NR]))
                gs = slice(w * GW, (w + 1) * GW)
                for j in (0, CH + 1):
                    seq(nc.gpsimd.tensor_copy(ce[:, 0, j], cre[:, gs]))
                    last = nc.gpsimd.tensor_scalar(ce[:, 1, j], cim[:, gs], -1.0, None, ALU.mult)
                    if j == 0:
                        seq(last)
                last.then_inc(s_ends, 1)
                pool.wait_ge(s_ends, w + 1)
            pool.wait_ge(s_bandout, 16 * 8 * NW)
            pool.wait_ge(s_bsout, 16 * NW)
            for hb in range(NH // HB):
                if hb >= 1:
                    pool.wait_ge(s_pv, hb)
                for name, dst in (("bias", bias_b), ("kcT", kc_b), ("vc", vc_b)):
                    pool.dma_start(dst[:], d[name][hb]).then_inc(s_attin, 16)
                if hb == 0:
                    pool.dma_start(bgate[:], d["bgate"][0].partition_broadcast(P)).then_inc(s_bg, 16)
                for i, name in ((1, "new_k"), (2, "new_v")):
                    pool.wait_ge(s_evA, NS * (4 * hb + i + 1))
                    pool.dma_start(d[name][:, hb * BN:(hb + 1) * BN], qkvz[:, i, 0]).then_inc(s_kvout, 16)
                    if hb == 0:
                        pool.wait_ge(s_adaout, 2 * i)
                        pool.dma_start(bgate[:], d["bgate"][i].partition_broadcast(P)).then_inc(s_bg, 16)
                if hb == 0:
                    pool.wait_ge(s_adaout, 6)
                    pool.dma_start(bgate[:], d["bgate"][3].partition_broadcast(P)).then_inc(s_bg, 16)
            pool.wait_ge(s_adaout, 8)
            pool.dma_start(bgate[:], d["bgate"][4].partition_broadcast(P)).then_inc(s_bg, 16)
            pool.wait_ge(s_og, 8)
            pool.wait_ge(s_kvout, 16 * 8)
            for st in range(NS):
                pool.dma_start(X[:, st], d["x"][st]).then_inc(s_x2in, 16)
            pool.dma_start(h0[:], d["h0"]).then_inc(s_h0, 16)
            for i in range(1, 4):
                pool.wait_ge(s_adaout, 16 + 2 * i)
                pool.dma_start(bgate[:], d["bgate"][4 + i].partition_broadcast(P)).then_inc(s_bg, 16)
            pool.wait_ge(s_x2, 4)
            pool.dma_start(x_keep, X[:].rearrange("p s c -> p (s c)")).then_inc(s_kept, 16)
            pool.wait_ge(s_adaout, fins(B_END))
            pool.dma_start(gate_keep, gate[:].rearrange("p s c -> p (s c)")).then_inc(s_kept, 16)
            seq(nc.gpsimd.memset(utf01[:], 0.0))
            nc.gpsimd.memset(utr[:], 0.0).then_inc(s_zero, 1)

            def store_u(w):
                wait_evacuated(pool, B_IN1 + w)
                for st in range(NS):
                    pool.dma_start(u_d[st * P:(st + 1) * P, w * BN:(w + 1) * BN], ub[:, w % 2, st]).then_inc(s_ubout[w % 2], 16)
                pool.wait_ge(s_ubout[w % 2], 32 * (w // 2 + 1))

            def load_u(w):
                for gh in range(2):
                    for e in range(2):
                        c0 = w * BN + e * 256 + gh * P
                        pool.dma_start(u2[gh * M2:(gh + 1) * M2, :, e],
                                       u_d[:, c0:c0 + P].rearrange("(m t) c -> m t c", t=CH)).then_inc(s_u2, 16)
                pool.wait_ge(s_u2, 64 * (w + 1))
                if w >= 1:
                    pool.wait_ge(s_uT, 4 * w)
                for e in range(2):
                    for t in range(CH):
                        o = u2p[:].rearrange("p v (e t c) -> p v e t c", e=2, t=CH)[:, :, e, t]
                        last = nc.gpsimd.tensor_copy(o, u2[:, t, e].rearrange("p (v c) -> p v c", c=S5C))
                        if (e, t) != (1, CH - 1):
                            seq(last)
                last.then_inc(s_u2p, 1)
                pool.wait_ge(s_u2p, w + 1)

            for w in range(NW):
                store_u(w)
                if w == 3:
                    pool.wait_ge(s_S, 2 * NR)
                    nc.gpsimd.memset(utf23[:], 0.0).then_inc(s_zero, 1)
                    pool.wait_ge(s_zero, 2)
                load_u(w)
            pool.wait_ge(s_wused, UB * B_GLU)
            nc.gpsimd.memset(kd[:], 0.0).then_inc(s_kdz, 1)
            for w in range(NW):
                pool.wait_ge(s_yout[w], 32)
                if w == 0:
                    pool.wait_ge(s_hy, 6)
                    pool.wait_ge(s_hyf, 6)
                cols = slice(w * BN, (w + 1) * BN)
                pool.dma_start(Y[:, :, cols], y_d[:, cols].rearrange("(s p) c -> p s c", s=NS)).then_inc(s_yin[w], 16)
            pool.wait_ge(s_y, 4 * NW)
            pool.dma_start(bglu[:], d["b_glu"].partition_broadcast(P)).then_inc(s_vec, 16)
            pool.wait_ge(s_hy, 8)
            pool.wait_ge(s_hyf, 8)
            pool.dma_start(gate[:].rearrange("p s c -> p (s c)"), gate_keep).then_inc(s_back, 16)
            pool.dma_start(gfin[:], d["g_fin"].partition_broadcast(P)).then_inc(s_vec, 16)
            pool.wait_ge(s_tp, 4 * TG)
            pool.wait_ge(s_yz, 1)
            pool.dma_start(X[:].rearrange("p s c -> p (s c)"), x_keep).then_inc(s_back, 16)
            pool.wait_ge(s_fso, 1)
            for ri in range(2):
                pool.dma_start(d["new_state"][:, ri].rearrange("d g p -> g d p"),
                               fso[:, ri].rearrange("g (d p) -> g d p", d=2)).then_inc(s_stout, 16)
            pool.wait_ge(s_stout, 32)
            pool.wait_ge(s_kvout, 128)

        @block.tensor
        def _(pe):
            mm = nc.tensor.matmul
            tr = nc.tensor.transpose

            def ada_chunk(bank, rhs, c):
                for j in range(CK):
                    last = mm(ps[32 * j:32 * j + 32, bank], cT32[:, c * CK + j], rhs[:, j * BN:(j + 1) * BN],
                              start=c == 0, stop=c == NCK - 1)
                return last

            def ada_columns(a, out):
                for i in range(4):
                    last = mm(out[:, 2 * i:2 * i + 2], adasb[:, a % 2, i * P:(i + 1) * P], sel2[:],
                              start=True, stop=True)
                return last

            pe.wait_ge(s_const, 16 * 7)
            pe.wait_ge(s_cond, 1)

            def ada_early(a):
                if a >= 2:
                    pe.wait_ge(s_adasb, a - 1)
                for c in range(NCK):
                    pe.wait_ge(s_raw[c], 16 * (a + 1))
                    last = ada_chunk(4 if a % 2 == 0 else 1, raw[:, c], c)
                    last.then_inc(s_ada0, 1)

            def b_tables(w):
                pe.wait_ge(s_btm, 2 * (w + 1))
                for i in range(NR // 2):
                    n = w * 8 + i
                    if n >= 2:
                        pe.wait_ge(s_bs, n - 1)
                    for r in range(2):
                        for ri in range(2):
                            c0 = (2 * r + ri) * P
                            last = tr(ps[:, 5 + n % 2, c0:c0 + P],
                                      bt[:, ri, 2 * i + r].rearrange("p e c -> p (e c)"), ident[:])
                    last.then_inc(s_btT, 1)

            def band_products(w):
                pe.wait_ge(s_ctm, 2 * (w + 1))
                pe.wait_ge(s_ends, w + 1)
                for q in range(4):
                    n = w * 4 + q
                    if n >= 2:
                        pe.wait_ge(s_bandd, n - 1)
                    for half in range(2):
                        for ri in range(2):
                            for j in range(4):
                                r = 4 * q + j
                                lhs = (bbf, bbb)[half][:, ri, r].rearrange("p e c -> p (e c)")
                                j0 = (0, 2)[half]
                                rhs = ce[:, ri, j0:j0 + CH].rearrange("p j (e r) c -> p e j r c", e=2)[:, :, :, r]
                                out = ps[32 * j:32 * j + 32, (7, 3)[n % 2], half * P:(half + 1) * P]
                                last = mm(out.rearrange("p (e j c) -> p e j c", e=2, c=S5C), lhs, rhs,
                                          start=ri == 0, stop=ri == 1)
                    last.then_inc(s_band, 1)

            for step, n in EARLY:
                if step == "ada":
                    ada_early(n)
                    pe.wait_ge(s_adasb, n + 1)
                    last = ada_columns(n, ps[:, 0, 8 * n:8 * n + 8])
                    if n == A_EARLY - 1:
                        last.then_inc(s_adaE, 1)
                elif step == "b":
                    b_tables(n)
                else:
                    band_products(n)
            pe.wait_ge(s_bandd, 16)
            pe.wait_ge(s_bs, 32)
            pe.wait_ge(s_adaEout, 1)

            def transposed(i, g):
                n = TG * i + g
                src = (WA, WA, WA, Y, WA)[i]
                if i in (0, 2):
                    pe.wait_ge(s_xn, 4 * (i // 2) + g // 2 + 1)
                if i == 3:
                    pe.wait_ge(s_yin[g // 2], 16)
                if g >= AHEAD:
                    pe.wait_ge(s_xlo, n - AHEAD + 1)
                for k in range(2):
                    for st in range(NS):
                        last = tr(ps[:, 5 + n % 3, (2 * k + st) * P:(2 * k + st + 1) * P],
                                  src[:, st, (2 * g + k) * P:(2 * g + k + 1) * P], ident[:])
                last.then_inc(s_tp, 1)

            def unit(b, u):
                k0 = UB * b + u
                if b in STAGES:
                    pe.wait_ge(s_xlo, TG * STAGES.index(b) + u + 1)
                if u == 0 and b >= 2:
                    wait_evacuated(pe, b - 2)
                pe.wait_ge(s_lo, k0 + 1)
                s = k0 % 4
                for k in range(2):
                    kt = 2 * u + k
                    for st in range(NS):
                        acc = ps[:, 2 * (b % 2) + st]
                        mm(acc, xhi[:, kt, st], whi[:, s, k], start=kt == 0, stop=False)
                        mm(acc, xhi[:, kt, st], wlo[:, s, k], start=False, stop=False)
                        last = mm(acc, xlo[:, kt, st], whi[:, s, k], start=False, stop=kt == KT - 1)
                last.then_inc(s_wused, 1)

            def q_or_k(src, dst_bank, s):
                for st in range(NS):
                    for h in range(HB):
                        last = tr(ps[:, dst_bank + st, h * P:(h + 1) * P], src[:, st, h * P:(h + 1) * P], ident[:])
                last.then_inc(s, 1)

            def attention(hb, b, u):
                j = b % 4
                if (j, u) == (1, 3):
                    wait_evacuated(pe, 4 * hb)
                    if hb >= 1:
                        pe.wait_ge(s_og, 2 * hb)
                    q_or_k(qkvz[:, 0], 5, s_qT)
                if (j, u) == (2, 3):
                    wait_evacuated(pe, 4 * hb + 1)
                    pe.wait_ge(s_qTsb, 2 * (hb + 1))
                    q_or_k(qkvz[:, 1], 5, s_kT)
                if (j, u) == (2, 7):
                    pe.wait_ge(s_kTsb, 2 * (hb + 1))
                    pe.wait_ge(s_attin, 48 * (hb + 1))
                    pe.wait_ge(s_adaout, fins(b))
                    for h in range(HB):
                        c = slice(h * P, (h + 1) * P)
                        mm(ps[:, 5, c], qT[:, 0, c], kT[:, 0, c], start=True, stop=True)
                        mm(ps[:, 6, c], qT[:, 1, c], kT[:, 1, c], start=True, stop=True)
                        last = mm(ps[:, 7, c], qT[:, 1, c], kc_b[:, c], start=True, stop=True)
                    last.then_inc(s_sc, 1)
                if (j, u) == (3, 6):
                    pe.wait_ge(s_prob, 3 * (hb + 1))
                    pe.wait_ge(s_adaout, fins(b))
                    for i in range(3):
                        for h in range(HB):
                            c = slice(h * P, (h + 1) * P)
                            last = tr(ps[:, 5 + i, c], pr[:, i, c], ident[:])
                    last.then_inc(s_pT, 1)
                if (j, u) == (3, 7):
                    wait_evacuated(pe, 4 * hb + 2)
                    pe.wait_ge(s_pTsb, 3 * (hb + 1))
                    for h in range(HB):
                        c = slice(h * P, (h + 1) * P)
                        mm(ps[:, 5, c], pT[:, 0, c], qkvz[:, 2, 0, c], start=True, stop=True)
                        mm(ps[:, 6, c], pT[:, 1, c], qkvz[:, 2, 1, c], start=True, stop=False)
                        last = mm(ps[:, 6, c], pT[:, 2, c], vc_b[:, c], start=False, stop=True)
                    last.then_inc(s_pv, 1)

            def modulation(b, u):
                a0 = ada_beside(b - 1)
                a1 = ada_beside(b)
                if a0 is not None and u == 2:
                    pe.wait_ge(s_adasb, A_EARLY + ada_order(b))
                    if fins(b - 1) > 0:
                        pe.wait_ge(s_adaout, fins(b - 1))
                    if b % 4 == 3 and b < B_OUT0:
                        pe.wait_ge(s_sub, 3 * (b // 4 + 1))
                    elif 4 <= b < B_OUT0:
                        pe.wait_ge(s_pTsb, 3 * (b // 4))
                    if is_gate(a0):
                        last = mm(ps[:, fin_bank(b)], selbc[:, 0], adasb[:, a0 % 2], start=True, stop=True)
                    else:
                        last = ada_columns(a0, ps[:, fin_bank(b)])
                    last.then_inc(s_adafin, 1)
                if a0 is not None and u == 4 and is_gate(a0):
                    pe.wait_ge(s_adaout, fins(b - 1) + 1)
                    mm(ps[:, fin_bank(b)], selbc[:, 1], adasb[:, a0 % 2], start=True, stop=True).then_inc(s_adafin, 1)
                if a1 is not None and u % 2 == 1:
                    c = u // 2
                    if c == 0:
                        pe.wait_ge(s_adasb, A_EARLY + ada_order(b))
                    n = NCK * ada_order(b) + c
                    pe.wait_ge(s_araw[n % 2], 16 * (n // 2 + 1))
                    ada_chunk(4, araw[:, n % 2], c).then_inc(s_ada1, 1)

            def s5_transposed(w, i):
                n = 4 * w + i
                if i == 0:
                    pe.wait_ge(s_u2p, w + 1)
                    if w >= 1:
                        pe.wait_ge(s_STsb, 8 * w)
                if n >= 2:
                    pe.wait_ge(s_uTsb, 2 * (n - 1))
                for v in range(4):
                    src = u2p[:, 4 * (i // 2) + v]
                    out = ps[:, 5 + n % 2, v * P:(v + 1) * P]
                    if i % 2 == 0:
                        last = tr(out, src, ident[:])
                    else:
                        last = mm(out, src, perm[:], start=True, stop=True)
                last.then_inc(s_uT, 1)

            def s5_sums(w, j):
                if j == 0:
                    pe.wait_ge(s_uTsb, 8 * (w + 1))
                    if w == 0:
                        pe.wait_ge(s_adaout, fins(B_END))
                    if w >= 2:
                        pe.wait_ge(s_bt[w % 2], 16)
                for r in (2 * j, 2 * j + 1) if j < NR // 2 else ():
                    n = NR // 2 * w + j
                    if n >= 2 and r % 2 == 0:
                        pe.wait_ge(s_Ssb, n - 1)
                    if w < 2:
                        h = 2 * w + r // 8
                        if r % 8 == 0:
                            pe.wait_ge(s_bth[h % 2], 16 * (w + 1))
                        table = bth[:, h % 2, r % 8]
                    else:
                        table = btab[:, w % 2, r]
                    for dr, src in ((0, utf(w)[:, r]), (1, utr[:, r])):
                        out = ps[:, (4, 7)[n % 2], r % 2 * 2 * P:(r % 2 + 1) * 2 * P].rearrange("p (i c) -> p i c", i=2)[
                            :, :, dr * S5P:(dr + 1) * S5P]
                        last = mm(out, src, table[:, :, dr * S5P:(dr + 1) * S5P], start=True, stop=True)
                    last.then_inc(s_S, 1)
                if j >= 1:
                    n = NR // 2 * w + j - 1
                    pe.wait_ge(s_Ssb, n + 1)
                    if n >= 2:
                        pe.wait_ge(s_STsb, n - 1)
                    for k in range(2):
                        for ri in range(2):
                            c0 = (2 * ri + k) * P
                            last = tr(ps[:, 5 + n % 2, c0:c0 + P], ss[:, k, ri * P:(ri + 1) * P], ident[:])
                    last.then_inc(s_ST, 1)

            def s5_outputs(w):
                pe.wait_ge(s_hy, 2 * (w + 1))
                pe.wait_ge(s_hyf, 2 * (w + 1))
                pe.wait_ge(s_ct[w % 2], 16 * (w // 2 + 1))
                pe.wait_ge(s_kd[w % 2], 16 * 8 * (w // 2 + 1))
                for q in range(4):
                    n = 4 * w + q
                    if n >= 2:
                        pe.wait_ge(s_ysb, n - 1)
                    for k in range(4):
                        r = 4 * q + k
                        out = ps[:, 2 + n % 2, k * P:(k + 1) * P]
                        mm(out, utf(w)[:, r], kd[:, w % 2, r], start=True, stop=False)
                        for ri in range(2):
                            last = mm(out.rearrange("p (e t c) -> p e t c", e=2, c=S5C),
                                      hy[:, w % 2, ri, 4 * r:4 * r + 4].rearrange("p x j -> p (x j)"),
                                      (ctab0, ctab1)[w % 2][:, ri].rearrange("p t (e r) c -> p e t r c", e=2)[:, :, :, r],
                                      start=False, stop=ri == 1)
                    last.then_inc(s_y, 1)

            for b in range(B_END):
                if b == B_OUT0:
                    pe.wait_ge(s_og, 8)
                if b == B_GLU:
                    wait_evacuated(pe, B_GLU - 1)
                    for j in range(NR // 2 + 1):
                        s5_sums(2, j)
                    for i in range(4):
                        s5_transposed(3, i)
                    for j in range(NR // 2 + 1):
                        s5_sums(3, j)
                    for w in range(NW):
                        s5_outputs(w)
                    pe.wait_ge(s_scan, NW)
                    pe.wait_ge(s_Ssb, NR // 2 * NW)
                    for ri in range(2):
                        last = tr(ps[:, 4, ri * P:(ri + 1) * P], fs[:, ri], ident[:])
                    last.then_inc(s_fsT, 1)
                    pe.wait_ge(s_STsb, 8 * NW)
                    pe.wait_ge(s_ysb, 4 * NW)
                if b == B_OUT1:
                    pe.wait_ge(s_g, 8)
                if b in STAGES:
                    for g in range(AHEAD):
                        transposed(STAGES.index(b), g)
                for u in range(UB):
                    if b in STAGES and u + AHEAD < TG:
                        transposed(STAGES.index(b), u + AHEAD)
                    unit(b, u)
                    if b < B_OUT0:
                        attention(b // 4, b, u)
                    modulation(b, u)
                    step, w, i = s5_beside(UB * b + u)
                    if step == "u":
                        s5_transposed(w, 2 * i)
                        s5_transposed(w, 2 * i + 1)
                    elif step == "S":
                        s5_sums(w, i)

        @block.scalar
        def _(act):
            af = nc.scalar.activation
            act.wait_ge(s_const, 16 * 7)
            act.wait_ge(s_cz, 1)
            af(cT32[:, :, 0:NS], condT[:], ACT.Silu).then_inc(s_cond, 1)

            def square_sums(src, c, junk, before):
                for st in range(NS):
                    if before + st > 0:
                        act.wait_ge(s_stat, before + st)
                    af(junk(st), src[:, st, c * BN:(c + 1) * BN], ACT.Square,
                       accum_out=stat[:, 24 + NS * c + st:25 + NS * c + st]).then_inc(s_stat, 1)

            def junk_bank(st):
                return ps[:, 2]

            def junk_wa(st):
                return WA[:, st, 0:BN]

            def scale_rows(i, src, dst):
                act.wait_ge(s_rstd, 2 * i + 1)
                af(stat[:, 8 * i + 4:8 * i + 6], stat[:, 8 * i + 2:8 * i + 4], ACT.Sqrt).then_inc(s_stat, 1)
                act.wait_ge(s_rstd, 2 * i + 2)
                for c in range(NCK):
                    cols = slice(c * BN, (c + 1) * BN)
                    for st in range(NS):
                        last = af(dst[:, st, cols], src[:, st, cols], ACT.Copy, scale=stat[:, 8 * i + 6 + st:8 * i + 7 + st])
                    last.then_inc(s_xn, 1)

            act.wait_ge(s_pole, 16 * 3)
            af(tmp[:, 3], tmp[:, 0], ACT.Exp).then_inc(s_exp, 1)
            act.wait_ge(s_ang, 1)
            af(tmp[:, 5], tmp[:, 4], ACT.Exp)
            af(tmp[:, 9], tmp[:, 8], ACT.Sin)
            af(tmp[:, 10], tmp[:, 8], ACT.Sin, scale=0.5).then_inc(s_mag, 1)
            act.wait_ge(s_pow, 1)
            fwd, bwd = slice(0, S5P), slice(S5P, P)
            af(pb[fwd], apw[fwd][:, :, ::-1][:, :, 1:CH + 1], ACT.Copy)
            af(pb[bwd], apw[bwd][:, :, 0:CH], ACT.Copy)
            af(py[fwd], apw[fwd][:, :, 1:CH + 1], ACT.Copy)
            af(py[bwd], apw[bwd][:, :, ::-1][:, :, 0:CH], ACT.Copy).then_inc(s_pbpy, 1)

            def adasb_early(a):
                act.wait_ge(s_ada0, NCK * (a + 1))
                af(adasb[:, a % 2], ps[:, 4 if a % 2 == 0 else 1], ACT.Copy).then_inc(s_adasb, 1)

            def b_staged(w):
                if w == 0:
                    act.wait_ge(s_factors, 1)
                    act.wait_ge(s_bbm, 1)
                else:
                    act.wait_ge(s_bsout, 16 * w)
                for i in range(NR // 2):
                    act.wait_ge(s_btT, NR // 2 * w + i + 1)
                    af(bs[:, 2 * i:2 * i + 2].rearrange("p r i c -> p (r i c)"), ps[:, 5 + i % 2], ACT.Copy).then_inc(s_bs, 1)
                act.wait_ge(s_bs, NR // 2 * (w + 1))
                act.dma_start(bt_d[w], bs[:].rearrange("p r i c -> p (r i c)")).then_inc(s_bsout, 16)
                if w >= 1:
                    store_bands(w - 1)

            def store_bands(w):
                act.wait_ge(s_bandd, 4 * (w + 1))
                for j in range(4):
                    for e in range(2):
                        p0 = 32 * j + 16 * e
                        act.dma_start(band_d[w, :, j, e].rearrange("q c k -> c q k"),
                                      bands[p0:p0 + 16, :, e].rearrange("p q k c -> p q (k c)")).then_inc(s_bandout, 16)

            def bands_staged(w):
                for ri in range(2):
                    act.wait_ge(s_ctm, 2 * w + ri + 1)
                    act.dma_start(ct_d[w, :, ri], ce[:, ri, 1:CH + 1]).then_inc(s_ctout[ri], 16)
                if w >= 1:
                    act.wait_ge(s_bandout, 16 * 8 * w)
                for q in range(4):
                    n = 4 * w + q
                    act.wait_ge(s_band, n + 1)
                    bank = ps[:, (7, 3)[n % 2]]
                    af(bands[:, q, :, CH - 1:NDL], bank[:, 0:P].rearrange("p (e k c) -> p e k c", e=2, c=S5C), ACT.Copy)
                    af(bands[:, q, :, 0:CH - 1], bank[:, P:2 * P].rearrange("p (e k c) -> p e k c", e=2, c=S5C)[
                        :, :, 0:CH - 1], ACT.Copy).then_inc(s_bandsb, 1)

            for step, n in EARLY:
                if step == "ada":
                    adasb_early(n)
                    if n == 2:
                        act.wait_ge(s_x, 32)
                        for c in range(NCK):
                            square_sums(WA, c, junk_bank, NS * c)
                elif step == "b":
                    b_staged(n)
                else:
                    bands_staged(n)
                    if n == 0:
                        act.wait_ge(s_stat, 8)
                        scale_rows(0, WA, WA)
            store_bands(NW - 1)

            def split(k):
                g = k // 2
                if k == 0:
                    act.wait_ge(s_btT, NW * NR // 2)
                    act.wait_ge(s_ends, NW)
                    act.wait_ge(s_ctm, 2 * NW)
                act.wait_ge(s_raw[g % 4], 16 * (A_EARLY * NCK // 4 + g // 4 + 1))
                if k >= 4:
                    act.wait_ge(s_wused, k - 3)
                src = raw[:, g % 4, (k % 2) * 2 * BN:(k % 2 + 1) * 2 * BN]
                af(whi[:, k % 4].rearrange("p k c -> p (k c)"), src, ACT.Copy).then_inc(s_hi, 1)

            def high(i, g):
                n = TG * i + g
                if (i, g) == (0, 0):
                    act.wait_ge(s_ctm, 2 * NW)
                act.wait_ge(s_tp, n + 1)
                done = TG // 2 * (i // 2) + g // 2 + 1
                if i in (0, 2) and g % 2 == 0:
                    act.wait_ge(s_taff, done)
                elif i in (0, 2):
                    if g == 1:
                        act.wait_ge(s_adaEout, 1)
                        if i == 2:
                            act.wait_ge(s_adaout, fins(B_OUT0))
                    for k in range(2):
                        for st in range(NS):
                            kt = 2 * g + k
                            x = ps[:, 5 + n % 3, (2 * k + st) * P:(2 * k + st + 1) * P]
                            last = af(x, x, ACT.Identity, bias=shT[:, i // 2, kt, st:st + 1],
                                      scale=gsT[:, i // 2, kt, st:st + 1])
                    last.then_inc(s_tact, 1)
                    act.wait_ge(s_tact, done)
                af(xhi[:, 2 * g:2 * g + 2].rearrange("p k s c -> p (k s c)"), ps[:, 5 + n % 3], ACT.Copy).then_inc(s_xhi, 1)

            def evacuate_in0(b):
                hb, j = b // 4, b % 4
                if b == 0:
                    for ri in range(2):
                        act.wait_ge(s_ctout[ri], 16 * NW)
                    act.wait_ge(s_ends, NW)
                if hb >= 1:
                    if j == 0:
                        act.wait_ge(s_qT, hb)
                    elif j == 1:
                        act.wait_ge(s_kT, hb)
                        act.wait_ge(s_kvout, 32 * hb)
                    elif j == 2:
                        act.wait_ge(s_pv, hb)
                        act.wait_ge(s_kvout, 32 * hb)
                    else:
                        act.wait_ge(s_og, 2 * hb)
                for st in range(NS):
                    af(qkvz[:, j, st], ps[:, 2 * (b % 2) + st], ACT.Silu if j == 3 else ACT.Copy).then_inc(s_evA, 1)

            def attention(hb, j, u):
                if (j, u) == (1, 3):
                    if hb == 0:
                        act.wait_ge(s_bsout, 16 * NW)
                        act.wait_ge(s_bandout, 128 * NW)
                    act.wait_ge(s_qT, hb + 1)
                    if hb >= 1:
                        act.wait_ge(s_sc, hb)
                    for st in range(NS):
                        af(qT[:, st], ps[:, 5 + st], ACT.Copy, scale=QSCALE).then_inc(s_qTsb, 1)
                if (j, u) == (2, 3):
                    act.wait_ge(s_kT, hb + 1)
                    for st in range(NS):
                        af(kT[:, st], ps[:, 5 + st], ACT.Copy).then_inc(s_kTsb, 1)
                if (j, u) == (3, 1):
                    for i in range(3):
                        act.wait_ge(s_sub, 3 * hb + i + 1)
                        af(pr[:, i], pr[:, i], ACT.Exp).then_inc(s_prob, 1)
                if (j, u) == (3, 6):
                    act.wait_ge(s_pT, hb + 1)
                    if hb >= 1:
                        act.wait_ge(s_pv, hb)
                    for i in range(3):
                        af(pT[:, i], ps[:, 5 + i], ACT.Copy).then_inc(s_pTsb, 1)

            def s5_transposed(w, i):
                act.wait_ge(s_uT, 4 * w + i + 1)
                if i == 0:
                    act.wait_ge(s_zero, 1 + w // 2)
                if i == 1 and w >= 1:
                    act.wait_ge(s_S, NR * w)
                for e in range(2):
                    h = slice(e * M2, (e + 1) * M2)
                    dst = (utf(w) if i % 2 == 0 else utr)[h]
                    dst = dst.rearrange("p (g v) m -> p v g m", g=2)[:, 4 * (i // 2):4 * (i // 2) + 4, :, h]
                    af(dst, ps[h, 5 + i % 2].rearrange("p (v g m) -> p v g m", v=4, g=2), ACT.Copy).then_inc(s_uTsb, 1)

            def s5_sums(w, j):
                if j < NR // 2:
                    n = NR // 2 * w + j
                    act.wait_ge(s_S, 2 * n + 2)
                    if n >= 1:
                        act.wait_ge(s_ST, n)
                    af(ss[:].rearrange("p r c -> p (r c)"), ps[:, (4, 7)[n % 2]], ACT.Copy).then_inc(s_Ssb, 1)
                if j == 1 and w == 0:
                    act.wait_ge(s_kept, 32)
                    act.wait_ge(s_xn, 8)
                if j == 1 and w >= 2:
                    act.wait_ge(s_hy, 2 * (w - 1))
                    act.wait_ge(s_hyf, 2 * (w - 1))
                if j >= 1:
                    n = NR // 2 * w + j - 1
                    act.wait_ge(s_ST, n + 1)
                    dst = sb[:, w % 2, :, :, 8 * (j - 1):8 * j].rearrange("p k i x -> p i x k")
                    af(dst, ps[:, 5 + n % 2].rearrange("p (i x k) -> p i x k", i=2, k=NCH), ACT.Copy).then_inc(s_STsb, 1)

            def s5_backward(w):
                act.wait_ge(s_scan, w + 1)
                act.wait_ge(s_wused, UB * B_GLU)
                if w >= 2:
                    act.wait_ge(s_y, 4 * (w - 1))
                src = sb[:, w % 2].rearrange("p k i x -> p i x k")
                for ri in range(2):
                    dst = hy[S5P:P, w % 2, ri]
                    af(dst[:, :, NCH - 1], h0[S5P:P, w, ri], ACT.Copy)
                    af(dst[:, :, 0:NCH - 1], src[S5P:P, ri, :, 0:NCH - 1][:, :, ::-1], ACT.Copy).then_inc(s_hy, 1)

            def s5_outputs(w):
                if w >= 2:
                    act.wait_ge(s_yout[w - 2], 32)
                for q in range(4):
                    n = 4 * w + q
                    act.wait_ge(s_y, n + 1)
                    for e in range(2):
                        h = slice(e * M2, (e + 1) * M2)
                        src_y = ps[h, 2 + n % 2].rearrange("p (r e t c) -> p e t r c", r=4, e=2, t=CH)[:, e]
                        dst = ys[h, w % 2, :, 64 * q:64 * q + 64].rearrange("p t (r c) -> p t r c", r=4)
                        last = af(dst, src_y, ACT.Gelu_apprx_tanh)
                    last.then_inc(s_ysb, 1)
                act.wait_ge(s_ysb, 4 * (w + 1))
                for e in range(2):
                    c0 = w * BN + e * 256
                    act.dma_start(y_d[:, c0:c0 + 256].rearrange("(m t) c -> m t c", t=CH),
                                  ys[e * M2:(e + 1) * M2, w % 2]).then_inc(s_yout[w], 16)

            for k in range(-4, NU):
                if k + 4 < NU and not 0 <= k + 4 - UB * B_GLU < 4:
                    split(k + 4)
                b, u = k // UB, k % UB
                if b in STAGES and u + AHEAD < TG:
                    high(STAGES.index(b), u + AHEAD)
                if k >= 0 and u == 0 and ada_beside(b - 1) is not None:
                    a = ada_beside(b - 1)
                    act.wait_ge(s_ada1, NCK * ada_order(b))
                    if ada_order(b) > 2:
                        act.wait_ge(s_adafin, fins(b - 1))
                    af(adasb[:, a % 2], ps[:, 4], ACT.Copy).then_inc(s_adasb, 1)
                if 0 <= b < B_OUT0:
                    attention(b // 4, b % 4, u)
                step, w, i = s5_beside(k)
                if step == "u":
                    s5_transposed(w, 2 * i)
                    s5_transposed(w, 2 * i + 1)
                elif step == "S":
                    s5_sums(w, i)
                if u == UB - 1:
                    if 0 <= b < B_GLU and not B_OUT0 <= b < B_IN1:
                        act.wait_ge(s_wused, UB * (b + 1))
                    if 0 <= b < B_OUT0:
                        evacuate_in0(b)
                    if B_IN1 <= b < B_IN1 + NW:
                        w = b - B_IN1
                        if w >= 2:
                            act.wait_ge(s_ubout[w % 2], 32 * (w // 2))
                        for st in range(NS):
                            af(ub[:, w % 2, st], ps[:, 2 * (b % 2) + st], ACT.Copy).then_inc(s_evA, 1)
                    if b == B_IN1 + NW:
                        for i in range(2):
                            act.wait_ge(s_ubout[i], 32 * NW // 2)
                    if B_IN1 + NW <= b < B_GLU:
                        c0 = (b - B_IN1 - NW) * BN
                        for st in range(NS):
                            af(WA[:, st, c0:c0 + BN], ps[:, 2 * (b % 2) + st], ACT.Silu).then_inc(s_evA, 1)
                    if B_OUT0 <= b < B_IN1 or b >= B_OUT1:
                        n = b - B_OUT0 if b < B_IN1 else 4 + b - B_OUT1
                        act.wait_ge(s_x2, n + 1)
                        square_sums(X, b % 4, junk_wa, 9 * (1 + n // 4) + NS * (n % 4))
                    if b == B_IN1 - 1:
                        act.wait_ge(s_stat, 17)
                        scale_rows(1, X, WA)
                    if b == B_GLU - 1:
                        s5_backward(0)
                        for j in range(NR // 2 + 1):
                            s5_sums(2, j)
                        for i in range(4):
                            s5_transposed(3, i)
                        s5_backward(1)
                        for j in range(NR // 2 + 1):
                            s5_sums(3, j)
                        s5_outputs(0)
                        s5_outputs(1)
                        for w in (2, 3):
                            s5_backward(w)
                            s5_outputs(w)
                        act.wait_ge(s_fsT, 1)
                        af(fso[:].rearrange("p i c -> p (i c)"), ps[:, 4, 0:2 * P], ACT.Copy).then_inc(s_fso, 1)
                        for j in range(4):
                            split(UB * B_GLU + j)
                    if B_GLU <= b < B_OUT1:
                        for st in range(NS):
                            n = NS * (b - B_GLU) + st
                            act.wait_ge(s_evV, NS * (B_IN1 - B_OUT0) + n + 1)
                            if n >= 2:
                                act.wait_ge(s_g, n - 1)
                            af(tg[:, 2 + st], tg[:, st], ACT.Sigmoid).then_inc(s_gsig, 1)
                    if b + 1 in STAGES:
                        for g in range(AHEAD):
                            high(STAGES.index(b + 1), g)
            act.wait_ge(s_stat, 26)
            scale_rows(2, X, WA)

        @block.vector
        def _(dve):
            seq = chain(dve, s_dve)
            tt = nc.vector.tensor_tensor
            ts = nc.vector.tensor_scalar
            nc.vector.memset(cT32[:], 0.0).then_inc(s_cz, 1)
            nc.vector.memset(apw[:, 0, 0], 1.0)
            seq(nc.vector.memset(apw[:, 1, 0], 0.0))
            ldt, are, aim, dt, xr, mag, th, kk, rr, sn, sh_, t0, t1, t2, f_re, f_im, den = [tmp[:, i] for i in range(17)]

            dve.wait_ge(s_exp, 1)
            tt(xr, are, dt, ALU.mult)
            seq(tt(th, aim, dt, ALU.mult))
            seq(ts(kk, th, 1.0 / (2 * math.pi), ROUND, ALU.mult, ALU.add))
            seq(ts(kk, kk, -ROUND, None, ALU.add))
            seq(nc.vector.scalar_tensor_tensor(rr, kk, -TWO_PI_HI, th, ALU.mult, ALU.add))
            seq(nc.vector.scalar_tensor_tensor(rr, kk, -TWO_PI_LO, rr, ALU.mult, ALU.add))
            ts(rr, rr, 3.1415925, -3.1415925, ALU.min, ALU.max).then_inc(s_ang, 1)

            def mean_squares(i):
                ss_, ms, root, inv = (stat[:, 8 * i + j:8 * i + j + 2] for j in (0, 2, 4, 6))
                dve.wait_ge(s_stat, 9 * i + 8)
                seq(nc.vector.tensor_reduce(ss_, stat[:, 24:32].rearrange("p (c s) -> p s c", s=NS), AX, ALU.add))
                ts(ms, ss_, 1.0 / D, EPS, ALU.mult, ALU.add).then_inc(s_rstd, 1)
                dve.wait_ge(s_stat, 9 * i + 9)
                nc.vector.reciprocal(inv, root).then_inc(s_rstd, 1)

            dve.wait_ge(s_mag, 1)
            seq(tt(t0, sh_, sh_, ALU.mult))
            seq(ts(t0, t0, -2.0, 1.0, ALU.mult, ALU.add))
            tt(apw[:, 0, 1], mag, t0, ALU.mult)
            seq(tt(apw[:, 1, 1], mag, sn, ALU.mult))
            for i, j in ((1, 1), (2, 1), (2, 2)):
                tt(t0, apw[:, 0, i], apw[:, 0, j], ALU.mult)
                tt(t1, apw[:, 1, i], apw[:, 1, j], ALU.mult)
                tt(t2, apw[:, 0, i], apw[:, 1, j], ALU.mult)
                seq(tt(den, apw[:, 1, i], apw[:, 0, j], ALU.mult))
                tt(apw[:, 0, i + j], t0, t1, ALU.subtract)
                last = tt(apw[:, 1, i + j], t2, den, ALU.add)
                if i + j < CH:
                    seq(last)
            last.then_inc(s_pow, 1)
            dve.wait_ge(s_pow, 1)
            tt(t0, are, are, ALU.mult)
            seq(tt(t1, aim, aim, ALU.mult))
            seq(tt(den, t0, t1, ALU.add))
            seq(nc.vector.reciprocal(den, den))
            seq(ts(t2, apw[:, 0, 1], -1.0, None, ALU.add))
            tt(f_re, t2, are, ALU.mult)
            seq(tt(t0, apw[:, 1, 1], aim, ALU.mult))
            seq(tt(f_re, f_re, t0, ALU.add))
            seq(tt(f_re, f_re, den, ALU.mult))
            tt(f_im, apw[:, 1, 1], are, ALU.mult)
            seq(tt(t0, t2, aim, ALU.mult))
            seq(tt(f_im, f_im, t0, ALU.subtract))
            seq(tt(f_im, f_im, den, ALU.mult))
            dve.wait_ge(s_par, 16 * 5)
            m1g = m1[:].rearrange("p (g c) -> p g c", c=S5C)
            m2g = m2[:].rearrange("p (g c) -> p g c", c=S5C)

            def times(out, f, v):
                return tt(out, f.unsqueeze(2).to_broadcast([P, S5G, S5C]), v, ALU.mult)

            times(m1g, f_re, bre[:])
            seq(times(m2g, f_im, bim[:]))
            seq(tt(bb[:, 0], m1g, m2g, ALU.subtract))
            times(m1g, f_re, bim[:])
            seq(times(m2g, f_im, bre[:]))
            tt(bb[:, 1], m1g, m2g, ALU.add).then_inc(s_bbm, 1)
            dve.wait_ge(s_bbm, 1)
            dve.wait_ge(s_pbpy, 1)

            def table(out, pw, v_re, v_im, w, done):
                gs = slice(w * GW, (w + 1) * GW)
                for_c = done is s_ctm

                def prod(dst, a, v):
                    a, v = a[:, :, gs], v[:, gs]
                    if for_c:
                        return tt(dst[:].rearrange("p (t g c) -> p t g c", t=CH, c=S5C),
                                  a.unsqueeze(3).to_broadcast([P, CH, GW, S5C]),
                                  v.unsqueeze(1).to_broadcast([P, CH, GW, S5C]), ALU.mult)
                    return tt(dst[:].rearrange("p (g t c) -> p g t c", t=CH, c=S5C),
                              a.rearrange("p t g -> p g t").unsqueeze(3).to_broadcast([P, GW, CH, S5C]),
                              v.unsqueeze(2).to_broadcast([P, GW, CH, S5C]), ALU.mult)

                def shaped(x):
                    return x[:] if for_c else x[:].rearrange("p (e r t c) -> p e r (t c)", e=2, t=CH, c=S5C)
                for ri in range(2):
                    prod(m1, pw[:, 0], (v_re, v_im)[ri])
                    seq(prod(m2, pw[:, 1], (v_im, v_re)[ri]))
                    if w >= 1 and for_c:
                        dve.wait_ge(s_ctout[ri], 16 * w)
                        dve.wait_ge(s_band, 4 * w)
                    if ri == 0:
                        last = tt(out[0], shaped(m1), shaped(m2), ALU.subtract)
                    elif for_c:
                        last = nc.vector.scalar_tensor_tensor(out[1], shaped(m1), -1.0, shaped(m2), ALU.mult, ALU.subtract)
                    else:
                        last = tt(out[1], shaped(m1), shaped(m2), ALU.add)
                    last.then_inc(done, 1)
                    dve.wait_ge(done, 2 * w + ri + 1)

            def add_diagonals(w):
                for q in range(4):
                    n = 4 * w + q
                    dve.wait_ge(s_bandsb, n + 1)
                    diag = bands[:, q, :, CH - 1]
                    back = ps[:, (7, 3)[n % 2], P:2 * P].rearrange("p (e k c) -> p e k c", e=2, c=S5C)[:, :, CH - 1]
                    seq(tt(diag, diag, back, ALU.add))
                    tt(diag, diag, dm[:, n], ALU.add).then_inc(s_bandd, 1)

            for w in range(NW):
                if w >= 1:
                    dve.wait_ge(s_btT, NR // 2 * w)
                table([bt[:, ri].rearrange("p r e k -> p e r k") for ri in range(2)], pb, bb[:, 0], bb[:, 1], w, s_btm)
                if w >= 1:
                    add_diagonals(w - 1)
                    if w == 1:
                        mean_squares(0)
                    dve.wait_ge(s_band, 4 * w)
                table([ce[:, ri, 1:CH + 1].rearrange("p j g c -> p (j g c)") for ri in range(2)], py, cre, cim, w, s_ctm)
            add_diagonals(NW - 1)

            def shift_or_scale(src, lay, a0, kt0, nk, done):
                nb = (nk + 3) // 4
                for isc in range(2):
                    a = a0 + 4 * isc
                    if src[isc] is None:
                        continue
                    val = src[isc]
                    bias = bT[:, a:a + nb].rearrange("p a i -> p (a i)").unsqueeze(2).to_broadcast([P, nk, NS])
                    if isc == 0:
                        last = tt(shT[:, lay, kt0:kt0 + nk], val, bias, ALU.add)
                    else:
                        t = modt[:, 0:nk * NS].rearrange("p (k s) -> p k s", s=NS)
                        seq(tt(t, val, bias, ALU.add))
                        gain = gT[:, lay, kt0:kt0 + nk].unsqueeze(2).to_broadcast([P, nk, NS])
                        last = nc.vector.scalar_tensor_tensor(gsT[:, lay, kt0:kt0 + nk], t, 1.0, gain, ALU.add, ALU.mult)
                last.then_inc(done, 1)

            dve.wait_ge(s_adaE, 1)
            cols = [ps[:, 0, 32 * i:32 * i + 32].rearrange("p (k s) -> p k s", s=NS) for i in range(2)]
            shift_or_scale(cols, 0, 0, 0, KT, s_adaEout)
            dve.wait_ge(s_adaEout, 1)

            def split(k):
                g = k // 2
                if k == 0:
                    dve.wait_ge(s_btT, NW * NR // 2)
                dve.wait_ge(s_hi, k + 1)
                if k >= 4:
                    dve.wait_ge(s_wused, k - 3)
                src = raw[:, g % 4, (k % 2) * 2 * BN:(k % 2 + 1) * 2 * BN]
                tt(wlo[:, k % 4].rearrange("p k c -> p (k c)"), src,
                   whi[:, k % 4].rearrange("p k c -> p (k c)").bitcast(F32), ALU.subtract).then_inc(s_lo, 1)

            def modulated(i, g):
                n = TG * i + g
                lay = i // 2
                dve.wait_ge(s_tp, n + 1)
                for k in range(2):
                    for st in range(NS):
                        kt = 2 * g + k
                        x = ps[:, 5 + n % 3, (2 * k + st) * P:(2 * k + st + 1) * P]
                        last = ts(x, x, gsT[:, lay, kt, st:st + 1], shT[:, lay, kt, st:st + 1], ALU.mult, ALU.add)
                last.then_inc(s_taff, 1)

            def low(i, g):
                n = TG * i + g
                dve.wait_ge(s_xhi, n + 1)
                tt(xlo[:, 2 * g:2 * g + 2].rearrange("p k s c -> p (k s c)"), ps[:, 5 + n % 3],
                   xhi[:, 2 * g:2 * g + 2].rearrange("p k s c -> p (k s c)").bitcast(F32), ALU.subtract).then_inc(s_xlo, 1)

            def by_head(x):
                return x.rearrange("p (h c) -> p h c", h=HB)

            def over_keys(x):
                return x.unsqueeze(2).to_broadcast([P, HB, P])

            def attention(hb, j, u):
                if (j, u) == (3, 0):
                    dve.wait_ge(s_sc, hb + 1)
                    if hb >= 1:
                        dve.wait_ge(s_pT, hb)
                    tr_ = nc.vector.tensor_reduce
                    tr_(asm[:, 0], by_head(ps[:, 5]), AX, ALU.max)
                    seq(tr_(asm[:, 2], by_head(ps[:, 7]), AX, ALU.max))
                    tt(by_head(pr[:, 0]), by_head(ps[:, 5]), over_keys(asm[:, 0]), ALU.subtract).then_inc(s_sub, 1)
                    seq(tt(pr[:, 1], ps[:, 6], bias_b[:], ALU.add))
                    seq(tr_(asm[:, 1], by_head(pr[:, 1]), AX, ALU.max))
                    seq(tt(asm[:, 3], asm[:, 1], asm[:, 2], ALU.max))
                    tt(by_head(pr[:, 1]), by_head(pr[:, 1]), over_keys(asm[:, 3]), ALU.subtract).then_inc(s_sub, 1)
                    tt(by_head(pr[:, 2]), by_head(ps[:, 7]), over_keys(asm[:, 3]), ALU.subtract).then_inc(s_sub, 1)
                if (j, u) == (3, 2):
                    dve.wait_ge(s_prob, 3 * (hb + 1))
                    for i in range(3):
                        last = nc.vector.tensor_reduce(asm[:, 4 + i], by_head(pr[:, i]), AX, ALU.add)
                    seq(last)
                    seq(tt(asm[:, 5], asm[:, 5], asm[:, 6], ALU.add))
                    seq(nc.vector.reciprocal(asm[:, 8:10], asm[:, 4:6]))
                if (j, u) == (3, 7):
                    dve.wait_ge(s_pv, hb + 1)
                    wait_evacuated(dve, 4 * hb + 3)
                    if hb >= 1:
                        dve.wait_ge(s_og, 2 * hb)
                    for st in range(NS):
                        seq(tt(by_head(tmo[:, st]), by_head(ps[:, 5 + st]), over_keys(asm[:, 8 + st]), ALU.mult))
                        tt(WA[:, st, hb * BN:(hb + 1) * BN], tmo[:, st], qkvz[:, 3, st], ALU.mult).then_inc(s_og, 1)

            def modulation(b, u):
                a0 = ada_beside(b - 1)
                if a0 is None or not (u == 3 or u == 5 and is_gate(a0)):
                    return
                part = (u - 3) // 2
                dve.wait_ge(s_adafin, fins(b - 1) + part + 1)
                i = a0 % 4
                if is_gate(a0):
                    dve.wait_ge(s_bg, 16 * (4 * (a0 // 12) + i + 1))
                    if a0 >= 12:
                        wait_evacuated(dve, b - 1)
                    tt(gate[:, part, i * BN:(i + 1) * BN], ps[:, fin_bank(b)], bgate[:], ALU.add).then_inc(s_adaout, 1)
                else:
                    val = ps[:, fin_bank(b), 0:4 * NS].rearrange("p (k s) -> p k s", s=NS)
                    scale = a0 % 12 >= 4
                    shift_or_scale((None, val) if scale else (val, None), a0 // 12, a0 - 4 * scale, 4 * i, 4, s_adaout)

            def residual(b, lay, buf):
                c0 = b % 4 * BN
                dve.wait_ge(s_wused, UB * (b + 1))
                for st in range(NS):
                    tt(buf[:, st], ps[:, 2 * (b % 2) + st], gate[:, st, c0:c0 + BN], ALU.mult).then_inc(s_evV, 1)
                wait_evacuated(dve, b)
                for st in range(NS):
                    last = tt(X[:, st, c0:c0 + BN], X[:, st, c0:c0 + BN], buf[:, st], ALU.add)
                last.then_inc(s_x2, 1)
                dve.wait_ge(s_x2, b % 4 + 1 + 4 * lay)

            def scan(*steps):
                chains = []
                for i, (w, k) in enumerate(steps):
                    if k == 0:
                        dve.wait_ge(s_STsb, 8 * (w + 1))
                        if w == 0:
                            dve.wait_ge(s_h0, 16)
                    now = h0[:, w].rearrange("p i x -> p i x") if k == 0 else sb[:, w % 2, k - 1]
                    last = tt((t12, t12b)[w % 2][:], coef[:, w], now.unsqueeze(2).to_broadcast([P, 2, 2, 2 * GW]), ALU.mult)
                    chains.append((sb[:, w % 2, k], (t12, t12b)[w % 2]))
                seq(last)
                for half in range(2):
                    for nxt, t in chains:
                        last = tt(nxt, nxt, t[:, half], ALU.add)
                    seq(last)

            def scanned(w):
                fin = sb[:, w % 2, NCH - 1].rearrange("p i (r e s) -> p i e r s", e=2, s=NS)
                for e in range(2):
                    g0 = w * GW + e * NR
                    last = nc.vector.tensor_copy(fs[:, :, g0:g0 + NR], fin[:, :, e, :, 0])
                last.then_inc(s_scan, 1)

            def s5_forward(w):
                dve.wait_ge(s_scan, w + 1)
                dve.wait_ge(s_wused, UB * B_GLU)
                if w >= 2:
                    dve.wait_ge(s_y, 4 * (w - 1))
                src = sb[:, w % 2].rearrange("p k i x -> p i x k")
                for ri in range(2):
                    dst = hy[0:S5P, w % 2, ri]
                    nc.vector.tensor_copy(dst[:, :, 0], h0[0:S5P, w, ri])
                    nc.vector.tensor_copy(dst[:, :, 1:NCH], src[0:S5P, ri, :, 0:NCH - 1]).then_inc(s_hyf, 1)

            for k in range(-4, NU):
                if k + 4 < NU and not 0 <= k + 4 - UB * B_GLU < 4:
                    split(k + 4)
                b, u = k // UB, k % UB
                if b in STAGES and u + AHEAD < TG:
                    i = STAGES.index(b)
                    if i in (0, 2) and (u + AHEAD) % 2 == 0:
                        modulated(i, u + AHEAD)
                    low(i, u + AHEAD)
                if k >= 0:
                    modulation(b, u)
                due = [(w, k - SCAN_FROM[w]) for w in range(2) if 0 <= k - SCAN_FROM[w] < NCH and k < UB * B_GLU]
                if due:
                    scan(*due)
                    if due[0] == (0, NCH - 1):
                        scanned(0)
                if k == UB * B_GLU:
                    wait_evacuated(dve, B_GLU - 1)
                    for w in range(NW):
                        dve.wait_ge(s_yin[w], 16)
                    for st in range(NS):
                        last = tt(WA[:, st], WA[:, st], Y[:, st], ALU.mult)
                    last.then_inc(s_yz, 1)
                    dve.wait_ge(s_yz, 1)
                if 0 <= b < B_OUT0:
                    attention(b // 4, b % 4, u)
                if u == UB - 1:
                    if B_OUT0 <= b < B_IN1:
                        if b == B_OUT0:
                            dve.wait_ge(s_x2in, 32)
                        residual(b, 0, pr)
                    if b == B_IN1 - 1:
                        mean_squares(1)
                    if b == B_GLU - 1:
                        s5_forward(0)
                        for c in range(k + 1 - SCAN_FROM[1], NCH):
                            scan((1, c))
                        scanned(1)
                        s5_forward(1)
                        for c in range(NCH + SCAN_LAG):
                            scan(*(([(2, c)] if c < NCH else []) + ([(3, c - SCAN_LAG)] if c >= SCAN_LAG else [])))
                            if c == NCH - 1:
                                scanned(2)
                                s5_forward(2)
                        scanned(3)
                        s5_forward(3)
                        for j in range(4):
                            split(UB * B_GLU + j)
                    if B_GLU <= b < B_OUT1:
                        c0 = (b - B_GLU) * BN
                        dve.wait_ge(s_wused, UB * (b + 1))
                        dve.wait_ge(s_vec, 32)
                        for st in range(NS):
                            n = NS * (b - B_GLU) + st
                            if n >= 2:
                                dve.wait_ge(s_gsig, n - 1)
                            tt(tg[:, st], ps[:, 2 * (b % 2) + st], bglu[:, c0:c0 + BN], ALU.add).then_inc(s_evV, 1)
                        for st in range(NS):
                            n = NS * (b - B_GLU) + st
                            dve.wait_ge(s_gsig, n + 1)
                            g_ = WA[:, st, c0:c0 + BN]
                            tt(g_, g_, tg[:, 2 + st], ALU.mult).then_inc(s_g, 1)
                    if b == B_OUT1:
                        dve.wait_ge(s_back, 32)
                    if b >= B_OUT1:
                        residual(b, 1, tg)
                    if b + 1 in STAGES:
                        i = STAGES.index(b + 1)
                        if i == 0:
                            dve.wait_ge(s_band, 4 * NW)
                            for ri in range(2):
                                dve.wait_ge(s_ctout[ri], 16 * NW)
                        if i in (0, 2):
                            for g in range(0, AHEAD, 2):
                                modulated(i, g)
                        for g in range(AHEAD):
                            low(i, g)
            mean_squares(2)
            for c in range(NCK):
                cols = slice(c * BN, (c + 1) * BN)
                dve.wait_ge(s_xn, 8 + c + 1)
                for st in range(NS):
                    last = tt(X[:, st, cols], WA[:, st, cols], gfin[:, cols], ALU.mult)
                last.then_inc(s_fin, 1)

_OUTS = {"y": (NS, P, D), "new_k": (P, D), "new_v": (P, D), "new_state": (2, 2, S5G, S5P)}


def _blocks(w):
    n = w.shape[1] // BN
    v = w.reshape(NCK, CK, P, n, BN).transpose(3, 2, 0, 1, 4)
    return v.reshape(n, P, NCK, CK * BN)


def _lay_out(i):
    f = np.float32
    w_in0 = _blocks(i["l0_w_in"]).reshape(4, 4, P, NCK, CK * BN).transpose(1, 0, 2, 3, 4).reshape(16, P, NCK, CK * BN)
    out = {
        "x": np.stack([i["x_prompt"][0], i["x_sample"][0]]),
        "w": np.concatenate([w_in0, _blocks(i["l0_w_out"]), _blocks(i["l1_w_in"]), _blocks(i["l1_w_glu"]),
                             _blocks(i["l1_w_out"])]),
        "wada": np.concatenate([_blocks(i["l0_w_ada"]), _blocks(i["l1_w_ada"])]),
        "condT": np.stack([i["c_ctx"], i["c"][0]]).reshape(NS, KT, P).transpose(2, 1, 0),
        "gT": np.stack([i["l0_norm_g"], i["l1_norm_g"]]).reshape(2, KT, P).transpose(2, 0, 1),
        "bT": np.stack([i["l0_b_ada"], i["l1_b_ada"]]).reshape(24, 4, P).transpose(2, 0, 1),
        "bgate": np.concatenate([i["l0_b_ada"][2 * D:], i["l1_b_ada"][2 * D:]]).reshape(8, BN),
        "b_glu": i["l1_b_glu"],
        "g_fin": i["final_norm_g"],
        "ident": np.eye(P, dtype=f),
        "kcT": i["cache_l0_k"][0].reshape(P, 4, HB, P).transpose(1, 3, 2, 0).reshape(4, P, BN),
        "vc": i["cache_l0_v"][0].reshape(P, 4, BN).transpose(1, 0, 2),
        "are": i["l1_a_re"].transpose(0, 2, 1).reshape(P, S5G),
        "aim": i["l1_a_im"].transpose(0, 2, 1).reshape(P, S5G),
        "ldt": np.repeat(i["l1_log_dt"][:, None], S5P, axis=1).reshape(P, S5G),
        "bre": i["l1_b_re"].transpose(0, 2, 1, 3).reshape(P, S5G, S5C),
        "bim": i["l1_b_im"].transpose(0, 2, 1, 3).reshape(P, S5G, S5C),
        "cre": i["l1_c_re"].transpose(0, 3, 1, 2).reshape(P, S5G, S5C),
        "cim": i["l1_c_im"].transpose(0, 3, 1, 2).reshape(P, S5G, S5C),
    }
    rows = np.arange(P)
    perm = np.zeros((P, P), f)
    perm[rows, rows // NCH * NCH + NCH - 1 - rows % NCH] = 1.0
    out["perm"] = perm
    sel2 = np.zeros((P, NS), f)
    sel2[rows[rows % 32 < NS], rows[rows % 32 < NS] % 32] = 1.0
    out["sel2"] = sel2
    out["selbc"] = np.repeat(sel2[:, :, None], P, axis=2)
    q, k = rows[:, None], rows[None, :]
    dr = k // GRID_W - q // GRID_W + NA_ROWS - 1
    dc = np.clip(k % GRID_W - q % GRID_W + NA_COLS - 1, 0, 2 * NA_COLS - 2)
    c0 = np.clip(q % GRID_W - NA_COLS // 2, 0, GRID_W - NA_COLS)
    ok = (k % GRID_W >= c0) & (k % GRID_W < c0 + NA_COLS)
    bias = np.where(ok[None], i["l0_rpb"][:, dr, dc], f(NEG))
    out["bias"] = bias.reshape(4, HB, P, P).transpose(0, 2, 1, 3).reshape(4, P, BN)
    skip = i["l1_d"].reshape(NW, 2, 4, 4, S5C)
    dm = np.zeros((4, 2, S5C, NW, 4, 2, S5C), f)
    for e in range(2):
        for c in range(S5C):
            dm[:, e, c, :, :, e, c] = skip[:, e, :, :, c].transpose(2, 0, 1)
    out["dm"] = dm.reshape(P, NR, 2, S5C)
    st = i["state_l1_s5"][0].reshape(2, 2, NW, 2, NR, S5P)
    h0 = np.zeros((2, S5P, NW, 2, NR, 2, NS), f)
    h0[..., 1] = st.transpose(0, 5, 2, 1, 4, 3)
    out["h0"] = h0.reshape(P, NW, 2, 2 * GW)
    return {name: np.ascontiguousarray(a) for name, a in out.items()}


def kernel(**inputs):
    import concourse.bacc as bacc
    from concourse.bass_utils import run_bass_kernel_spmd

    arrays = _lay_out({name: np.asarray(a) for name, a in inputs.items()})
    nc = bacc.Bacc("TRN2", target_bir_lowering=False, num_devices=1)
    d = {name: nc.dram_tensor("in_" + name, a.shape, mybir.dt.from_np(a.dtype), kind="ExternalInput").ap()
         for name, a in arrays.items()}
    for name, shape in _OUTS.items():
        d[name] = nc.dram_tensor("out_" + name, shape, F32, kind="ExternalOutput").ap()
    build(nc, d)
    r = run_bass_kernel_spmd(nc, [{"in_" + name: a for name, a in arrays.items()}], core_ids=[0]).results[0]
    y = r["out_y"]
    return (y[0:1], y[1:2], r["out_new_k"].reshape(1, P, NH, P), r["out_new_v"].reshape(1, P, NH, P),
            r["out_new_state"].reshape(1, 2, 2, S5G, S5P))
```
